# Optimizing a Trainium2 kernel written in Bass

```python
import math
import jax, jax.numpy as jnp
from jax import lax
import numpy as np
import jax
import jax.numpy as jnp

D_MODEL = 1024
BATCH = 1
SEQ = 256
DEPTH = 1

HEAD_DIM = 64
N_HEADS_MOBA = 8
N_HEADS_SB = 8
W_MOBA = N_HEADS_MOBA * HEAD_DIM
W_SB = N_HEADS_SB * HEAD_DIM
MOBA_BLOCK = 256
MOBA_TOPK = 3
Q_CHUNK = 128
PEER_HEADS = 8
PEER_NKEYS = 128
PEER_N_EXPERTS = PEER_NKEYS * PEER_NKEYS
PEER_QDIM = 256
PEER_HALF = PEER_QDIM // 2
PEER_TOPK = 16
PEER_TOK_CHUNK = 128
RMS_EPS = 1e-6
IN_SPLITS = [W_MOBA, W_MOBA, W_MOBA, W_SB, W_SB, W_SB, D_MODEL, D_MODEL]
IN_WIDTH = sum(IN_SPLITS)


def rmsnorm(x, g):
    xf = x.astype(jnp.float32)
    y = xf * lax.rsqrt(jnp.mean(xf * xf, axis=-1, keepdims=True) + RMS_EPS)
    return (y * g.astype(jnp.float32)).astype(x.dtype)

def alibi_slopes(n_heads):
    return jnp.exp2(-8.0 * jnp.arange(1, n_heads + 1, dtype=jnp.float32) / n_heads)

def _heads(t, n):
    b, s, _ = t.shape
    return t.reshape(b, s, n, HEAD_DIM).transpose(0, 2, 1, 3)

def _merge(t):
    b, h, s, dh = t.shape
    return t.transpose(0, 2, 1, 3).reshape(b, s, h * dh)

def moba_attention(q, k, v):
    B, H, S, dh = q.shape
    nb = -(-S // MOBA_BLOCK)
    pad = nb * MOBA_BLOCK - S
    kp = jnp.pad(k, ((0, 0), (0, 0), (0, pad), (0, 0)))
    vp = jnp.pad(v, ((0, 0), (0, 0), (0, pad), (0, 0)))
    kb = kp.reshape(B, H, nb, MOBA_BLOCK, dh)
    vb = vp.reshape(B, H, nb, MOBA_BLOCK, dh)
    kmean = jnp.mean(kb.astype(jnp.float32), axis=3)
    ksel = min(MOBA_TOPK, nb)
    scale = dh ** -0.5
    slope = alibi_slopes(H).reshape(1, H, 1, 1)
    slope5 = slope[..., None]
    bidx = jnp.arange(B)[:, None, None, None]
    hidx = jnp.arange(H)[None, :, None, None]
    n_chunks = S // Q_CHUNK
    qc = q.reshape(B, H, n_chunks, Q_CHUNK, dh).transpose(2, 0, 1, 3, 4)

    def chunk(args):
        q_blk, c = args
        qf = q_blk.astype(jnp.float32)
        t = c * Q_CHUNK + jnp.arange(Q_CHUNK)
        own = (c * Q_CHUNK) // MOBA_BLOCK
        bs = jnp.einsum('bhqd,bhnd->bhqn', qf, kmean)
        bs = jnp.where(jnp.arange(nb) < own, bs, -jnp.inf)
        _, top_i = lax.top_k(bs, ksel)
        valid = top_i < own
        k_sel = kb[bidx, hidx, top_i].astype(jnp.float32)
        v_sel = vb[bidx, hidx, top_i].astype(jnp.float32)
        s_pos = top_i[..., None] * MOBA_BLOCK + jnp.arange(MOBA_BLOCK)
        dist_sel = (t[:, None, None] - s_pos).astype(jnp.float32)
        sc_sel = jnp.einsum('bhqd,bhqnkd->bhqnk', qf, k_sel) * scale - slope5 * dist_sel
        sc_sel = jnp.where(valid[..., None], sc_sel, -jnp.inf).reshape(B, H, Q_CHUNK, ksel * MOBA_BLOCK)
        k_own = lax.dynamic_slice_in_dim(kp, own * MOBA_BLOCK, MOBA_BLOCK, axis=2).astype(jnp.float32)
        v_own = lax.dynamic_slice_in_dim(vp, own * MOBA_BLOCK, MOBA_BLOCK, axis=2).astype(jnp.float32)
        s_own = own * MOBA_BLOCK + jnp.arange(MOBA_BLOCK)
        dist_own = (t[:, None] - s_own[None, :]).astype(jnp.float32)
        sc_own = jnp.einsum('bhqd,bhkd->bhqk', qf, k_own) * scale - slope * dist_own
        sc_own = jnp.where(s_own[None, :] <= t[:, None], sc_own, -jnp.inf)
        p = jax.nn.softmax(jnp.concatenate([sc_sel, sc_own], axis=-1), axis=-1)
        p_sel = p[..., :ksel * MOBA_BLOCK].reshape(B, H, Q_CHUNK, ksel, MOBA_BLOCK)
        p_own = p[..., ksel * MOBA_BLOCK:]
        o = (jnp.einsum('bhqnk,bhqnkd->bhqd', p_sel, v_sel)
             + jnp.einsum('bhqk,bhkd->bhqd', p_own, v_own))
        return o.astype(q.dtype)

    out = lax.map(chunk, (qc, jnp.arange(n_chunks)))
    return out.transpose(1, 2, 0, 3, 4).reshape(B, H, S, dh)

def stick_breaking_attention(q, k, v):
    B, H, S, dh = q.shape
    scale = dh ** -0.5
    kf = k.astype(jnp.float32)
    vf = v.astype(jnp.float32)
    s_idx = jnp.arange(S)
    n_chunks = S // Q_CHUNK
    qc = q.reshape(B, H, n_chunks, Q_CHUNK, dh).transpose(2, 0, 1, 3, 4)

    def chunk(args):
        q_blk, c = args
        t = c * Q_CHUNK + jnp.arange(Q_CHUNK)
        z = jnp.einsum('bhqd,bhkd->bhqk', q_blk.astype(jnp.float32), kf) * scale
        strict = s_idx[None, :] < t[:, None]
        log_1m = jnp.where(strict, jax.nn.log_sigmoid(-z), 0.0)
        suffix = lax.cumsum(log_1m, axis=3, reverse=True) - log_1m
        w = jnp.where(strict, jnp.exp(jax.nn.log_sigmoid(z) + suffix), 0.0)
        return jnp.einsum('bhqk,bhkd->bhqd', w, vf).astype(q.dtype)

    out = lax.map(chunk, (qc, jnp.arange(n_chunks)))
    return out.transpose(1, 2, 0, 3, 4).reshape(B, H, S, dh)

def peer_ffn(x, w_q, sub_keys, expert_u, expert_v):
    B, S, D = x.shape
    T = B * S
    xt = x.reshape(T // PEER_TOK_CHUNK, PEER_TOK_CHUNK, D)
    skf = sub_keys.astype(jnp.float32)

    def chunk(x_blk):
        tc = x_blk.shape[0]
        qh = (x_blk @ w_q).astype(jnp.float32).reshape(tc, PEER_HEADS, 2, PEER_HALF)
        scores = jnp.einsum('thpc,hpnc->thpn', qh, skf)
        s_top, i_top = lax.top_k(scores, PEER_TOPK)
        cand = s_top[:, :, 0, :, None] + s_top[:, :, 1, None, :]
        cand_idx = i_top[:, :, 0, :, None] * PEER_NKEYS + i_top[:, :, 1, None, :]
        c_s, c_pos = lax.top_k(cand.reshape(tc, PEER_HEADS, PEER_TOPK * PEER_TOPK), PEER_TOPK)
        e_idx = jnp.take_along_axis(cand_idx.reshape(tc, PEER_HEADS, PEER_TOPK * PEER_TOPK), c_pos, axis=-1)
        g = jax.nn.softmax(c_s, axis=-1)
        u = expert_u[e_idx].astype(jnp.float32)
        v = expert_v[e_idx].astype(jnp.float32)
        a = jax.nn.gelu(jnp.einsum('td,thkd->thk', x_blk.astype(jnp.float32), u), approximate=False)
        return jnp.einsum('thk,thkd->td', g * a, v).astype(x.dtype)

    return lax.map(chunk, xt).reshape(B, S, D)

def first_inputs(seed: int = 0) -> dict:
    key = jax.random.key(seed)
    ks = jax.random.split(key, 12)
    f32 = jnp.float32
    x = jax.random.normal(ks[0], (BATCH, SEQ, D_MODEL), f32)
    norm1_g = 1.0 + 0.01 * jax.random.normal(ks[1], (DEPTH, D_MODEL), f32)
    w_in = jax.random.normal(ks[2], (DEPTH, D_MODEL, IN_WIDTH), f32) * D_MODEL ** -0.5
    w_out_moba = jax.random.normal(ks[3], (DEPTH, W_MOBA, D_MODEL), f32) * W_MOBA ** -0.5
    w_out_sb = jax.random.normal(ks[4], (DEPTH, W_SB, D_MODEL), f32) * W_SB ** -0.5
    w_mix_out = jax.random.normal(ks[5], (DEPTH, D_MODEL, D_MODEL), f32) * D_MODEL ** -0.5
    norm2_g = 1.0 + 0.01 * jax.random.normal(ks[6], (DEPTH, D_MODEL), f32)
    peer_w_q = jax.random.normal(ks[7], (DEPTH, D_MODEL, PEER_HEADS * PEER_QDIM), f32) * D_MODEL ** -0.5
    peer_sub_keys = jax.random.normal(ks[8], (DEPTH, PEER_HEADS, 2, PEER_NKEYS, PEER_HALF), f32) * PEER_HALF ** -0.5
    peer_u = jax.random.normal(ks[9], (DEPTH, PEER_N_EXPERTS, D_MODEL), f32) * D_MODEL ** -0.5
    peer_v = jax.random.normal(ks[10], (DEPTH, PEER_N_EXPERTS, D_MODEL), f32) * PEER_HEADS ** -0.5
    final_norm_g = 1.0 + 0.01 * jax.random.normal(ks[11], (D_MODEL,), f32)
    return {"x": x, "norm1_g": norm1_g, "w_in": w_in, "w_out_moba": w_out_moba,
            "w_out_sb": w_out_sb, "w_mix_out": w_mix_out, "norm2_g": norm2_g,
            "peer_w_q": peer_w_q, "peer_sub_keys": peer_sub_keys, "peer_u": peer_u,
            "peer_v": peer_v, "final_norm_g": final_norm_g}

def first_block(x, norm1_g, w_in, w_out_moba, w_out_sb, w_mix_out, norm2_g,
              peer_w_q, peer_sub_keys, peer_u, peer_v, final_norm_g):
    split_at = [int(i) for i in np.cumsum(IN_SPLITS)[:-1]]
    h = x
    for l in range(DEPTH):
        xn = rmsnorm(h, norm1_g[l])
        proj = xn @ w_in[l]
        q_a, k_a, v_a, q_b, k_b, v_b, gate_a, gate_b = jnp.split(proj, split_at, axis=-1)
        y_a = _merge(moba_attention(_heads(q_a, N_HEADS_MOBA), _heads(k_a, N_HEADS_MOBA),
                                    _heads(v_a, N_HEADS_MOBA))) @ w_out_moba[l]
        y_b = _merge(stick_breaking_attention(_heads(q_b, N_HEADS_SB), _heads(k_b, N_HEADS_SB),
                                              _heads(v_b, N_HEADS_SB))) @ w_out_sb[l]
        mixed = jax.nn.sigmoid(gate_a) * y_a + jax.nn.sigmoid(gate_b) * y_b
        h = h + mixed @ w_mix_out[l]
        h = h + peer_ffn(rmsnorm(h, norm2_g[l]), peer_w_q[l], peer_sub_keys[l], peer_u[l], peer_v[l])
    return rmsnorm(h, final_norm_g)


DEPTH_2 = 2

GRID_W = 64
CTX_LEN = 256
N_MIXERS = 3
FFN_HIDDEN = -(-8 * D_MODEL // (3 * 256)) * 256
CONV_WIDTH = 3
MLA_HEADS = D_MODEL // 64
MLA_Q_LORA = 3 * D_MODEL // 4
MLA_KV_LORA = D_MODEL // 4
MLA_NOPE = 64
MLA_ROPE = 32
MLA_V = 64
DIFF_HEADS = 8
DIFF_HEAD_DIM = D_MODEL // (2 * DIFF_HEADS)
ROPE_THETA = 10000.0
NORM_EPS = 1e-6
Q_BLOCK = 128


def rms_norm(x, g):
    xf = x.astype(jnp.float32)
    y = xf * lax.rsqrt(jnp.mean(xf * xf, axis=-1, keepdims=True) + NORM_EPS)
    return (y * g.astype(jnp.float32)).astype(x.dtype)

def modulate(h, shift, scale):
    return h * (1.0 + scale) + shift

def swiglu(h, w_gate, w_up, w_down):
    return (jax.nn.silu(h @ w_gate) * (h @ w_up)) @ w_down

def axial_rope_tables(rows, rot_dim):
    axis_dim = rot_dim // 2
    inv_freq = ROPE_THETA ** (-jnp.arange(0, axis_dim, 2, dtype=jnp.float32) / axis_dim)
    row = jnp.repeat(jnp.arange(rows, dtype=jnp.float32), GRID_W)
    col = jnp.tile(jnp.arange(GRID_W, dtype=jnp.float32), rows)
    ang_r = row[:, None] * inv_freq
    ang_c = col[:, None] * inv_freq
    ang = jnp.concatenate([ang_r, ang_r, ang_c, ang_c], axis=-1)
    return jnp.cos(ang), jnp.sin(ang)

def apply_axial_rope(x, cos, sin):
    a = x.shape[-1] // 2
    h = a // 2
    xr, xc = x[..., :a], x[..., a:]
    rot = jnp.concatenate([-xr[..., h:], xr[..., :h], -xc[..., h:], xc[..., :h]], axis=-1)
    return x * cos.astype(x.dtype) + rot * sin.astype(x.dtype)

def sweep_query_blocks(block_fn, *qs):
    b, n = qs[0].shape[:2]
    if n % Q_BLOCK or n == Q_BLOCK:
        return block_fn(*qs)
    nb = n // Q_BLOCK
    blocks = tuple(jnp.swapaxes(a.reshape(b, nb, Q_BLOCK, *a.shape[2:]), 0, 1) for a in qs)
    out = lax.map(lambda blk: block_fn(*blk), blocks)
    out = jnp.swapaxes(out, 0, 1)
    return out.reshape(b, n, *out.shape[3:])

def short_conv_mixer(h, w_in, conv_k, conv_b, w_out):
    b_gate, c_gate, u = jnp.split(h @ w_in, 3, axis=-1)
    z = c_gate * u
    pad = CONV_WIDTH // 2
    y = lax.conv_general_dilated(z, conv_k[:, None, :], window_strides=(1,), padding=((pad, pad),),
                                 dimension_numbers=('NWC', 'WIO', 'NWC'), feature_group_count=D_MODEL)
    y = y + conv_b
    return (b_gate * y) @ w_out

def _mla_project(h, cos, sin, with_q, w_in, q_norm_g, w_q_up, kv_norm_g, w_kv_up,
                 qn_nope_g, qn_rope_g, kn_nope_g, kn_rope_g):
    b, n, _ = h.shape
    proj = h @ (w_in if with_q else w_in[:, MLA_Q_LORA:])
    if with_q:
        q_lat, proj = proj[..., :MLA_Q_LORA], proj[..., MLA_Q_LORA:]
    kv_lat, k_pe = proj[..., :MLA_KV_LORA], proj[..., MLA_KV_LORA:]
    kv = (rms_norm(kv_lat, kv_norm_g) @ w_kv_up).reshape(b, n, MLA_HEADS, MLA_NOPE + MLA_V)
    k_nope = rms_norm(kv[..., :MLA_NOPE], kn_nope_g)
    v = kv[..., MLA_NOPE:]
    k_pe = rms_norm(k_pe, kn_rope_g)
    if cos is not None:
        k_pe = apply_axial_rope(k_pe, cos, sin)
    if not with_q:
        return None, None, k_nope, k_pe, v
    q = (rms_norm(q_lat, q_norm_g) @ w_q_up).reshape(b, n, MLA_HEADS, MLA_NOPE + MLA_ROPE)
    q_nope = rms_norm(q[..., :MLA_NOPE], qn_nope_g)
    q_pe = rms_norm(q[..., MLA_NOPE:], qn_rope_g)
    if cos is not None:
        q_pe = apply_axial_rope(q_pe, cos[:, None, :], sin[:, None, :])
    return q_nope, q_pe, k_nope, k_pe, v

def _mla_block(k_nope, k_pe, v):
    scale = (MLA_NOPE + MLA_ROPE) ** -0.5

    def attend(q_nope, q_pe):
        s = (jnp.einsum('bqhd,bkhd->bhqk', q_nope, k_nope)
             + jnp.einsum('bqhr,bkr->bhqk', q_pe, k_pe))
        p = jax.nn.softmax(s.astype(jnp.float32) * scale, axis=-1).astype(v.dtype)
        return jnp.einsum('bhqk,bkhd->bqhd', p, v)
    return attend

def mla_mixer(a_ctx, a_lat, ctx_out, cos, sin, w_in, q_norm_g, w_q_up, kv_norm_g, w_kv_up,
              qn_nope_g, qn_rope_g, kn_nope_g, kn_rope_g, w_out):
    prm = (w_in, q_norm_g, w_q_up, kv_norm_g, w_kv_up, qn_nope_g, qn_rope_g, kn_nope_g, kn_rope_g)
    cq_n, cq_p, ck_n, ck_p, cv = _mla_project(a_ctx, None, None, ctx_out, *prm)
    lq_n, lq_p, lk_n, lk_p, lv = _mla_project(a_lat, cos, sin, True, *prm)
    b, n = a_lat.shape[:2]
    attend_lat = _mla_block(jnp.concatenate([ck_n, lk_n], axis=1),
                            jnp.concatenate([ck_p, lk_p], axis=1),
                            jnp.concatenate([cv, lv], axis=1))
    o_lat = sweep_query_blocks(attend_lat, lq_n, lq_p).reshape(b, n, MLA_HEADS * MLA_V) @ w_out
    o_ctx = None
    if ctx_out:
        o_ctx = sweep_query_blocks(_mla_block(ck_n, ck_p, cv), cq_n, cq_p)
        o_ctx = o_ctx.reshape(b, a_ctx.shape[1], MLA_HEADS * MLA_V) @ w_out
    return o_ctx, o_lat

def _diff_project(h, cos, sin, with_q, w_in, qn_g, kn_g):
    b, n, _ = h.shape
    proj = h @ (w_in if with_q else w_in[:, D_MODEL:])
    parts = jnp.split(proj, 3 if with_q else 2, axis=-1)
    k = rms_norm(parts[-2].reshape(b, n, DIFF_HEADS, 2, DIFF_HEAD_DIM), kn_g)
    v = parts[-1].reshape(b, n, DIFF_HEADS, 2 * DIFF_HEAD_DIM)
    if cos is not None:
        k = apply_axial_rope(k, cos[:, None, None, :], sin[:, None, None, :])
    if not with_q:
        return None, k, v
    q = rms_norm(parts[0].reshape(b, n, DIFF_HEADS, 2, DIFF_HEAD_DIM), qn_g)
    if cos is not None:
        q = apply_axial_rope(q, cos[:, None, None, :], sin[:, None, None, :])
    return q, k, v

def _diff_block(k, v, lam):
    scale = DIFF_HEAD_DIM ** -0.5
    k1, k2 = k[..., 0, :], k[..., 1, :]

    def attend(q):
        s1 = jnp.einsum('bqhd,bkhd->bhqk', q[..., 0, :], k1).astype(jnp.float32) * scale
        s2 = jnp.einsum('bqhd,bkhd->bhqk', q[..., 1, :], k2).astype(jnp.float32) * scale
        p = jax.nn.softmax(s1, axis=-1) - lam * jax.nn.softmax(s2, axis=-1)
        return jnp.einsum('bhqk,bkhe->bqhe', p.astype(v.dtype), v)
    return attend

def diff_mixer(a_ctx, a_lat, ctx_out, cos, sin, lam_init, w_in, qn_g, kn_g,
               lq1, lk1, lq2, lk2, sub_g, w_out):
    lam = (jnp.exp(jnp.sum(lq1.astype(jnp.float32) * lk1.astype(jnp.float32)))
           - jnp.exp(jnp.sum(lq2.astype(jnp.float32) * lk2.astype(jnp.float32))) + lam_init)
    cq, ck, cv = _diff_project(a_ctx, None, None, ctx_out, w_in, qn_g, kn_g)
    lq, lk, lv = _diff_project(a_lat, cos, sin, True, w_in, qn_g, kn_g)

    def finish(o):
        o = rms_norm(o, sub_g) * (1.0 - lam_init)
        return o.reshape(o.shape[0], o.shape[1], D_MODEL) @ w_out

    attend_lat = _diff_block(jnp.concatenate([ck, lk], axis=1), jnp.concatenate([cv, lv], axis=1), lam)
    o_lat = finish(sweep_query_blocks(attend_lat, lq))
    o_ctx = finish(sweep_query_blocks(_diff_block(ck, cv, lam), cq)) if ctx_out else None
    return o_ctx, o_lat

def second_inputs(seed: int = 0) -> dict:
    key = jax.random.key(seed)
    ks = iter(jax.random.split(key, 40))

    def nrm(shape, scale):
        return jax.random.normal(next(ks), shape, jnp.float32) * scale

    def gain(shape):
        return 1.0 + 0.02 * jax.random.normal(next(ks), shape, jnp.float32)

    n_a, n_b, n_c = (len(range(k, DEPTH_2, N_MIXERS)) for k in range(N_MIXERS))
    d, f = D_MODEL, FFN_HIDDEN
    return {
        'x': nrm((BATCH, SEQ, d), 1.0),
        'c': nrm((BATCH, d), 1.0),
        'ctx': nrm((BATCH, CTX_LEN, d), 1.0),
        'c_ctx': nrm((d,), 1.0),
        'norm_mix_g': gain((DEPTH_2, d)),
        'norm_ffn_g': gain((DEPTH_2, d)),
        'mod_w': nrm((DEPTH_2, d, 6 * d), 0.5 * d ** -0.5),
        'mod_b': nrm((DEPTH_2, 6 * d), 0.02),
        'ffn_w_gate': nrm((DEPTH_2, d, f), d ** -0.5),
        'ffn_w_up': nrm((DEPTH_2, d, f), d ** -0.5),
        'ffn_w_down': nrm((DEPTH_2, f, d), f ** -0.5),
        'conv_w_in': nrm((n_a, d, 3 * d), d ** -0.5),
        'conv_k': nrm((n_a, CONV_WIDTH, d), CONV_WIDTH ** -0.5),
        'conv_b': nrm((n_a, d), 0.02),
        'conv_w_out': nrm((n_a, d, d), d ** -0.5),
        'mla_w_in': nrm((n_b, d, MLA_Q_LORA + MLA_KV_LORA + MLA_ROPE), d ** -0.5),
        'mla_q_norm_g': gain((n_b, MLA_Q_LORA)),
        'mla_w_q_up': nrm((n_b, MLA_Q_LORA, MLA_HEADS * (MLA_NOPE + MLA_ROPE)), MLA_Q_LORA ** -0.5),
        'mla_kv_norm_g': gain((n_b, MLA_KV_LORA)),
        'mla_w_kv_up': nrm((n_b, MLA_KV_LORA, MLA_HEADS * (MLA_NOPE + MLA_V)), MLA_KV_LORA ** -0.5),
        'mla_qn_nope_g': gain((n_b, MLA_NOPE)),
        'mla_qn_rope_g': gain((n_b, MLA_ROPE)),
        'mla_kn_nope_g': gain((n_b, MLA_NOPE)),
        'mla_kn_rope_g': gain((n_b, MLA_ROPE)),
        'mla_w_out': nrm((n_b, MLA_HEADS * MLA_V, d), (MLA_HEADS * MLA_V) ** -0.5),
        'diff_w_in': nrm((n_c, d, 3 * d), d ** -0.5),
        'diff_qn_g': gain((n_c, DIFF_HEAD_DIM)),
        'diff_kn_g': gain((n_c, DIFF_HEAD_DIM)),
        'diff_lq1': nrm((n_c, DIFF_HEAD_DIM), 0.1),
        'diff_lk1': nrm((n_c, DIFF_HEAD_DIM), 0.1),
        'diff_lq2': nrm((n_c, DIFF_HEAD_DIM), 0.1),
        'diff_lk2': nrm((n_c, DIFF_HEAD_DIM), 0.1),
        'diff_sub_g': gain((n_c, 2 * DIFF_HEAD_DIM)),
        'diff_w_out': nrm((n_c, d, d), d ** -0.5),
    }

def second_block(x, c, ctx, c_ctx, norm_mix_g, norm_ffn_g, mod_w, mod_b, ffn_w_gate, ffn_w_up, ffn_w_down,
              conv_w_in, conv_k, conv_b, conv_w_out,
              mla_w_in, mla_q_norm_g, mla_w_q_up, mla_kv_norm_g, mla_w_kv_up,
              mla_qn_nope_g, mla_qn_rope_g, mla_kn_nope_g, mla_kn_rope_g, mla_w_out,
              diff_w_in, diff_qn_g, diff_kn_g, diff_lq1, diff_lk1, diff_lq2, diff_lk2, diff_sub_g, diff_w_out):
    n_lat = x.shape[1]
    rows = n_lat // GRID_W
    cos_mla, sin_mla = axial_rope_tables(rows, MLA_ROPE)
    cos_diff, sin_diff = axial_rope_tables(rows, DIFF_HEAD_DIM)
    silu_c = jax.nn.silu(c)
    silu_cctx = jax.nn.silu(c_ctx)
    h_lat, h_ctx = x, ctx
    for i in range(DEPTH_2):
        kind, slot = i % N_MIXERS, i // N_MIXERS
        last = i == DEPTH_2 - 1
        sh1, sc1, g1, sh2, sc2, g2 = jnp.split((silu_c @ mod_w[i] + mod_b[i])[:, None, :], 6, axis=-1)
        a_lat = modulate(rms_norm(h_lat, norm_mix_g[i]), sh1, sc1)
        need_ctx_in = not (last and kind == 0)
        if need_ctx_in:
            csh1, csc1, cg1, csh2, csc2, cg2 = jnp.split(silu_cctx @ mod_w[i] + mod_b[i], 6, axis=-1)
            a_ctx = modulate(rms_norm(h_ctx, norm_mix_g[i]), csh1, csc1)
        if kind == 0:
            o_lat = short_conv_mixer(a_lat, conv_w_in[slot], conv_k[slot], conv_b[slot], conv_w_out[slot])
            o_ctx = None if last else short_conv_mixer(a_ctx, conv_w_in[slot], conv_k[slot], conv_b[slot],
                                                       conv_w_out[slot])
        elif kind == 1:
            o_ctx, o_lat = mla_mixer(a_ctx, a_lat, not last, cos_mla, sin_mla,
                                     mla_w_in[slot], mla_q_norm_g[slot], mla_w_q_up[slot],
                                     mla_kv_norm_g[slot], mla_w_kv_up[slot],
                                     mla_qn_nope_g[slot], mla_qn_rope_g[slot],
                                     mla_kn_nope_g[slot], mla_kn_rope_g[slot], mla_w_out[slot])
        else:
            lam_init = 0.8 - 0.6 * math.exp(-0.3 * i)
            o_ctx, o_lat = diff_mixer(a_ctx, a_lat, not last, cos_diff, sin_diff, lam_init,
                                      diff_w_in[slot], diff_qn_g[slot], diff_kn_g[slot],
                                      diff_lq1[slot], diff_lk1[slot], diff_lq2[slot], diff_lk2[slot],
                                      diff_sub_g[slot], diff_w_out[slot])
        h_lat = h_lat + g1 * o_lat
        h_lat = h_lat + g2 * swiglu(modulate(rms_norm(h_lat, norm_ffn_g[i]), sh2, sc2),
                                    ffn_w_gate[i], ffn_w_up[i], ffn_w_down[i])
        if not last:
            h_ctx = h_ctx + cg1 * o_ctx
            h_ctx = h_ctx + cg2 * swiglu(modulate(rms_norm(h_ctx, norm_ffn_g[i]), csh2, csc2),
                                         ffn_w_gate[i], ffn_w_up[i], ffn_w_down[i])
    return h_lat


def setup_inputs(seed=0):
    out = dict(first_inputs(seed))
    for name, value in second_inputs(seed + 1).items():
        if name != "x":
            out[name + "_2"] = value
    return out


def reference(
    x, norm1_g, w_in, w_out_moba, w_out_sb, w_mix_out, norm2_g, peer_w_q, peer_sub_keys, peer_u,
    peer_v, final_norm_g, c_2, ctx_2, c_ctx_2, norm_mix_g_2, norm_ffn_g_2, mod_w_2, mod_b_2,
    ffn_w_gate_2, ffn_w_up_2, ffn_w_down_2, conv_w_in_2, conv_k_2, conv_b_2, conv_w_out_2,
    mla_w_in_2, mla_q_norm_g_2, mla_w_q_up_2, mla_kv_norm_g_2, mla_w_kv_up_2, mla_qn_nope_g_2,
    mla_qn_rope_g_2, mla_kn_nope_g_2, mla_kn_rope_g_2, mla_w_out_2, diff_w_in_2, diff_qn_g_2,
    diff_kn_g_2, diff_lq1_2, diff_lk1_2, diff_lq2_2, diff_lk2_2, diff_sub_g_2, diff_w_out_2,
):
    x = first_block(
        x, norm1_g, w_in, w_out_moba, w_out_sb, w_mix_out, norm2_g, peer_w_q, peer_sub_keys,
        peer_u, peer_v, final_norm_g,
    )
    return second_block(
        x, c_2, ctx_2, c_ctx_2, norm_mix_g_2, norm_ffn_g_2, mod_w_2, mod_b_2, ffn_w_gate_2,
        ffn_w_up_2, ffn_w_down_2, conv_w_in_2, conv_k_2, conv_b_2, conv_w_out_2, mla_w_in_2,
        mla_q_norm_g_2, mla_w_q_up_2, mla_kv_norm_g_2, mla_w_kv_up_2, mla_qn_nope_g_2,
        mla_qn_rope_g_2, mla_kn_nope_g_2, mla_kn_rope_g_2, mla_w_out_2, diff_w_in_2,
        diff_qn_g_2, diff_kn_g_2, diff_lq1_2, diff_lk1_2, diff_lq2_2, diff_lk2_2, diff_sub_g_2,
        diff_w_out_2,
    )


_drawn_inputs = setup_inputs


def setup_inputs(seed=0):
    import zlib

    import numpy as np

    out = dict(_drawn_inputs(seed))
    spreads = {}
    factors = {'norm1_g': 3.566,
     'norm2_g': 2.682,
     'final_norm_g': 4.859,
     'ctx_2': 4.269,
     'norm_mix_g_2': 4.061,
     'norm_ffn_g_2': 19.633,
     'conv_b_2': 32.649,
     'mla_q_norm_g_2': 31.418,
     'mla_kv_norm_g_2': 42.054,
     'mla_qn_nope_g_2': 41.968,
     'mla_qn_rope_g_2': 64.0,
     'mla_kn_nope_g_2': 51.268,
     'mla_kn_rope_g_2': 52.587}
    for name, (base, spread) in spreads.items():
        noise = np.random.default_rng([zlib.crc32(name.encode()), seed]).standard_normal(out[name].shape)
        drawn = base * np.exp(spread * noise) if base else spread * noise
        out[name] = jnp.asarray(drawn.astype(out[name].dtype))
    for name, factor in factors.items():
        out[name] = (out[name] * factor).astype(out[name].dtype)
    return out
```

```python
from contextlib import ExitStack
from itertools import chain

import numpy as np

import concourse.bass as bass
from concourse import mybir

P = 128
T = 256
D = 1024
KD = D // P
HID = 2816
KH = HID // P
HEADS = 8
DH = 64
PH, KEYS, TOPK = 8, 128, 16
MH, NOPE, ROPE, MV = 16, 64, 32, 64
QH = NOPE + ROPE
QLAT, KVLAT = 768, 256
SLOTS = 4
SLOT = 2048
WIDE = SLOT // KD
BANKS = 4
EPS = 1e-6
BIG = 1e30

F32 = mybir.dt.float32
BF16 = mybir.dt.bfloat16
U32 = mybir.dt.uint32
ALU = mybir.AluOpType
ACT = mybir.ActivationFunctionType
AX = mybir.AxisListType


def firsts(table):
    out, at = {}, 0
    for name, n in table:
        out[name] = at
        at += n
    return out


HALVES = 2 * HEADS
ATT = []
for _s in range(2, HALVES + 3):
    if _s - 2 < HALVES:
        ATT.append(("turn", _s - 2))
    if _s >= 3 and (_s - 3) % 2 == 1:
        ATT.append(("value", (_s - 3) // 2))
MATT = []
for _s in range(1, MH + 2):
    if _s - 1 < MH:
        MATT += [("turn", 2 * (_s - 1)), ("turn", 2 * (_s - 1) + 1)]
    if _s >= 2 and (_s - 2) % 2 == 1:
        MATT.append(("value", (_s - 2) // 2))


def layer0(s):
    return ([(f"mixnorm_{s}", 0, 1), (f"conv_in_{s}", 12, 12), (f"conv_out_{s}", 4, 4)]
            + [(f"ffnnorm_{s}", 0, 1), (f"up_{s}", 22, 22), (f"down_{s}", 11, 4)])


STAGES = ([("vectors", 0, 2), ("turn_x", 0, 4), ("turn_ctx", 0, 4), ("norm1", 0, 1), ("qkv", 12, 12),
           ("gates", 8, 8), ("attention", 0, len(ATT)), ("out_moba", 2, 4), ("out_sb", 2, 4), ("mix", 4, 4),
           ("norm2", 0, 1), ("peer_q", 8, 8), ("turn_keys", 0, 4), ("peer_scores", 0, 8),
           ("turn_x2", 0, 4), ("mod0", 24, 1), ("mod1", 24, 1)]
          + layer0("ctx") + [("turn_chosen", 0, 1), ("norm_final", 0, 1)] + layer0("lat")
          + [("mixnorm1_ctx", 0, 1), ("mixnorm1_lat", 0, 1), ("mla_in", 5, 6), ("qlat_norm", 0, 1),
             ("kvlat_norm", 0, 1), ("kpe_norm", 0, 1), ("kpe_turn", 0, 1), ("kv_up", 2, 24),
             ("k_norm", 0, 16), ("q_up", 8, 8), ("q_norm", 0, 8), ("q_turn", 0, 8),
             ("mla_attention", 0, len(MATT)), ("mla_out", 4, 4), ("ffnnorm1", 0, 1), ("up_1", 22, 22),
             ("down_1", 11, 4), ("turn_out", 0, 4)])
CHUNK = firsts([(n, c) for n, c, _ in STAGES])
GROUP = firsts([(n, g) for n, _, g in STAGES])

VROWS = firsts([("norm1", 8), ("norm2", 8), ("final", 8), ("mix", 16), ("ffn", 16), ("conv_k", 24),
                ("conv_b", 8), ("q_lat", 6), ("kv_lat", 2), ("c", 8), ("c_ctx", 8), ("qn", 1), ("kn", 1),
                ("end", 0)])

CCOLS = firsts([("ident", 128), ("ones", 256), ("mean", 128), ("turn", 128), ("cos", T), ("sin", T),
                ("dist", 2 * T), ("strict", 2 * T), ("iota", 16), ("row", 32), ("eps", 1), ("end", 0)])


def constants():
    c = np.zeros((P, CCOLS["end"]), np.float32)

    def put(name, a):
        c[:a.shape[0], CCOLS[name]:CCOLS[name] + a.shape[1]] = a

    put("ident", np.eye(P))
    put("ones", np.ones((P, 256)))
    mean = np.zeros((QH, QH))
    mean[:NOPE, :NOPE] = 1.0 / NOPE
    mean[NOPE:, NOPE:] = 1.0 / ROPE
    put("mean", mean)
    axis, half = ROPE // 2, ROPE // 4
    turn = np.zeros((QH, QH))
    for a in range(2):
        for j in range(half):
            lo = NOPE + a * axis + j
            turn[lo, lo + half] = -1.0
            turn[lo + half, lo] = 1.0
    put("turn", turn.T)
    inv = np.float32(10000.0) ** (-np.arange(0, axis, 2, dtype=np.float32) / np.float32(axis))
    t = np.arange(T)
    ang = np.concatenate([(t // 64).astype(np.float32)[:, None] * inv] * 2
                         + [(t % 64).astype(np.float32)[:, None] * inv] * 2, axis=1)
    cos, sin = np.ones((QH, T)), np.zeros((QH, T))
    cos[NOPE:], sin[NOPE:] = np.cos(ang).T, np.sin(ang).T
    put("cos", cos)
    put("sin", sin)
    s = np.arange(T)[None, :]
    for tile in range(2):
        q = (tile * P + np.arange(P))[:, None]
        c[:, CCOLS["dist"] + tile * T:CCOLS["dist"] + (tile + 1) * T] = np.where(s <= q, q - s, BIG)
        c[:, CCOLS["strict"] + tile * T:CCOLS["strict"] + (tile + 1) * T] = np.where(s < q, 0.0, -BIG)
    c[:, CCOLS["iota"]:CCOLS["iota"] + 16] = np.arange(16)
    put("row", (np.arange(96)[:, None] % 32 == np.arange(32)[None, :]).astype(np.float32))
    c[:, CCOLS["eps"]] = EPS
    return c


def program(nc, w, consts_dram, out_dram):
    with ExitStack() as ctx:
        def sb(name, shape, dt=F32):
            return ctx.enter_context(nc.sbuf_tensor(name, shape, dt))

        def sem(name):
            return ctx.enter_context(nc.semaphore(name))

        bank = [ctx.enter_context(nc.psum_tensor(f"bank{b}", [P, 512], F32)) for b in range(BANKS)]
        wide = [ctx.enter_context(nc.psum_tensor(f"wide{b}", [P, 1024], F32)) for b in range(2)]
        sbank = [wide[b // 2][:, 512 * (b % 2):512 * (b % 2) + 512] for b in range(4)]

        ring = [sb(f"weights{s}", [P, SLOT]) for s in range(SLOTS)]
        consts = sb("consts", [P, CCOLS["end"]])
        vec = sb("vec", [P, VROWS["end"]])
        cvec = sb("cvec", [P, KD, 2])
        modb = sb("modb", [P, 96])
        mod = sb("mod", [P, 2, 48, 2])
        gmod = sb("gmod", [P, 2, 2, KD, 2])
        h_lat = sb("h_lat", [P, KD, T])
        h_ctx = sb("h_ctx", [P, KD, T])
        nrm = sb("nrm", [P, KD, 2 * T])
        sq = sb("sq", [P, KD, T])
        std = sb("std", [P, 2, 2 * T])
        rstd = sb("rstd", [P, 2, 2 * T])
        idx_t = sb("idx_t", [P, T], U32)
        gate_t = sb("gate_t", [P, T])
        idx8 = sb("idx8", [P, 2, 8], U32)
        dots = sb("dots", [P, 16])
        gelus = sb("gelus", [P, 16])
        wts = sb("wts", [P, 16])
        big = sb("big", [P, 10368])
        more = sb("more", [P, 18432])

        def view(a, at, *dims, dt=None):
            n = int(np.prod(dims))
            if dt is BF16:
                v = a[:, at:at + n // 2].bitcast(BF16)
            elif dt is U32:
                v = a[:, at:at + n].bitcast(U32)
            else:
                v = a[:, at:at + n]
            names = "abcd"[:len(dims)]
            return v.rearrange(f"p ({' '.join(names)}) -> p {' '.join(names)}",
                               **{x: d for x, d in zip(names, dims)})

        qk = view(big, 0, 16, T)
        gate = view(big, 4096, 16, T)
        vtok = view(big, 8192, 2, 1024)
        logit = view(more, 0, 3, 2, T)
        prob = view(more, 1536, 3, 2, T)
        expo = view(more, 3072, 3, 2, T)
        soft = view(more, 4608, 3, 2, T)
        prob_t = view(more, 6144, 2, 2, T)
        o_t = view(more, 7168, 8, T)
        small = view(more, 9216, 16, 8)
        x_tok = view(more, 9472, 2, D)
        ctx_tok = view(more, 11520, 2, D)
        vrows = view(more, 13568, P)
        brows = view(more, 13696, P)
        pq = view(big, 0, 16, T)
        keys_t = view(big, 4096, 16, P)
        keys = view(big, 6144, 16, P)
        x2_tok = view(big, 8320, 2, D)
        score = view(more, 0, 2, 16, P)
        top = view(more, 4096, 2, 16, TOPK)
        top_i = view(more, 4608, 2, 16, TOPK, dt=U32)
        top_f = view(more, 5120, 2, 16, TOPK)
        cand = view(more, 5632, 8, 256)
        eq = view(more, 7680, P, TOPK)
        best = view(more, 9728, 2, PH, TOPK)
        pos = view(more, 9984, P, dt=U32)
        part = view(more, 10112, 2, P, dt=U32)
        part_f = view(more, 10368, 2, P)
        pick = view(more, 10624, 2, P)
        chosen = view(more, 10880, 2, P)
        shifted = view(more, 11136, 2, PH, TOPK)
        sums = view(more, 11392, 2, 2, PH)
        split = [view(big, 1024 * j, 2, D, dt=BF16) for j in range(3)]
        rest = view(big, 3072, 2, D)
        ubuf = [view(more, 1024 * j, D) for j in range(4)]
        vbuf = [view(more, 4096 + 1024 * j, D) for j in range(8)]
        xs = view(more, 12288, 8, D, dt=BF16)[0:96]
        sel = view(more, 16384, 32, P, dt=BF16)[0:96]
        peer = view(big, 0, KD, T)
        cproj = view(big, 0, 24, T)
        z = view(big, 6144, KD, T + 2)
        hid = view(big, 0, KH, T)
        qlat = view(big, 0, 6, T)
        kvlat = view(big, 1536, 2, 2 * T)
        q = view(big, 2560, MH, T)
        msmall = view(big, 6656, 16, 8)
        kpe = view(big, 6784, 512)
        kcat = view(more, 0, MH, 2 * T)
        vmla = view(more, 8192, 4, MH * MV)
        o_mla = view(more, 12288, KD, T)
        mprob = view(more, 14336, 2, 2, 2 * T)
        mprob_t = view(more, 16384, 2, 4, T)
        out_tok = view(big, 0, 2, D)

        ident = consts[:, CCOLS["ident"]:CCOLS["ident"] + P]
        ones = consts[:, CCOLS["ones"]:CCOLS["ones"] + 256]
        mean = consts[:, CCOLS["mean"]:CCOLS["mean"] + P]
        turn = consts[:, CCOLS["turn"]:CCOLS["turn"] + P]
        cos = consts[:, CCOLS["cos"]:CCOLS["cos"] + T]
        sin = consts[:, CCOLS["sin"]:CCOLS["sin"] + T]
        dist = view(consts, CCOLS["dist"], 2, T)
        strict = view(consts, CCOLS["strict"], 2, T)
        iota = consts[:, CCOLS["iota"]:CCOLS["iota"] + 16]
        row32 = consts[0:96, CCOLS["row"]:CCOLS["row"] + 32]
        eps = consts[:, CCOLS["eps"]:CCOLS["eps"] + 1]

        def vcol(name, k):
            return vec[:, VROWS[name] + k:VROWS[name] + k + 1]

        s_start = sem("constants_and_tokens_landed")
        s_keys = sem("keys_landed")
        w_landed = [sem(f"weights_landed{s}") for s in range(SLOTS)]
        w_free = [sem(f"weights_free{s}") for s in range(SLOTS)]
        full = [sem(f"bank_full{b}") for b in range(BANKS)]
        free = [sem(f"bank_free{b}") for b in range(BANKS)]
        sc_full = [sem(f"scores_full{b}") for b in range(4)]
        sc_free = [sem(f"scores_free{b}") for b in range(4)]
        s_step = sem("vector_step")
        a_step = sem("scalar_step")
        s_sq = sem("squares_ready")
        s_norm = sem("norm_ready")
        s_soft_in = sem("softmax_in_ready")
        s_soft_exp = sem("softmax_exp_done")
        s_arg = sem("stick_argument_ready")
        s_prob_v = sem("probs_ready_by_vector")
        s_prob_s = sem("probs_ready_by_scalar")
        s_mixed = sem("mixed_ready")
        s_shift = sem("peer_shifted_ready")
        s_pexp = sem("peer_exp_done")
        s_chosen = sem("chosen_ready")
        s_index = sem("indices_ready")
        s_split = sem("split_ready")
        s_xs = sem("split_landed")
        s_idx8 = sem("indices_staged")
        s_turn = sem("gather_may_start")
        u_landed = [sem(f"u_landed{j}") for j in range(4)]
        u_free = [sem(f"u_free{j}") for j in range(4)]
        v_landed = [sem(f"v_landed{j}") for j in range(8)]
        v_free = [sem(f"v_free{j}") for j in range(8)]
        xb_full = [sem(f"x_broadcast_full{j}") for j in range(2)]
        xb_free = [sem(f"x_broadcast_free{j}") for j in range(2)]
        s_dots = sem("dots_ready")
        s_gelu = sem("gelus_ready")
        s_wts = sem("expert_weights_ready")
        vo_free = sem("peer_out_free")
        s_conv = sem("conv_ready")
        s_cvec = sem("conditioning_ready")
        s_kpe = sem("kpe_ready")
        s_ksq = sem("k_squares_ready")
        s_kn = sem("k_normed")
        s_qsq = sem("q_squares_ready")
        s_qn = sem("q_normed")
        s_qr = sem("q_rotated")
        s_kcat = sem("kpe_spread")
        s_out = sem("out_stored")

        def steps(eng, first, count, size=4):
            runs = count // size
            if runs >= 2:
                with eng.Fori(0, runs) as i:
                    for s in range(size):
                        yield i * size + (first + s), first + s, i
            else:
                runs = 0
            for s in range(runs * size, count):
                yield first + s, first + s, 0

        def slot_of(stage, s):
            return (CHUNK[stage] + s) % SLOTS

        def bank_of(stage, s):
            return (GROUP[stage] + s) % BANKS

        def wait_weights(eng, stage, s, i=0):
            c = CHUNK[stage] + s
            eng.wait_ge(w_landed[c % SLOTS], i * 16 + 16 * (c // SLOTS + 1))

        def wait_slot(eng, stage, s, i=0):
            c = CHUNK[stage] + s
            eng.wait_ge(w_free[c % SLOTS], i + (c // SLOTS + 1))

        def wait_full(eng, stage, s, i=0):
            g = GROUP[stage] + s
            eng.wait_ge(full[g % BANKS], i + (g // BANKS + 1))

        def wait_free(eng, stage, s, i=0):
            g = GROUP[stage] + s
            eng.wait_ge(free[g % BANKS], i + (g // BANKS + 1))

        def wait_emptied(eng, stage, s, i=0):
            g = GROUP[stage] + s
            eng.wait_ge(free[g % BANKS], i + (g // BANKS + 2))

        def wait_all_emptied(eng, stage, n):
            for s in range(max(0, n - BANKS), n):
                wait_emptied(eng, stage, s)

        block = ctx.enter_context(nc.Block())

        @block.sync
        def _(sp):
            def load(stage, s, i, src, shape):
                wait_slot(sp, stage, s, i)
                b = slot_of(stage, s)
                n = shape[0] * shape[1]
                sp.dma_start(ring[b][:, 0:n].rearrange("p (k n) -> p k n", k=shape[0]), src)\
                    .then_inc(w_landed[b], 16)

            def load_wide(stage, m, n, kt=KD, cols=WIDE, first=0):
                mv = m.rearrange("(k p) n -> p k n", p=P)
                for j, s, i in steps(sp, 0, n):
                    load(stage, s, i, mv[:, :, bass.ds(j * cols + first, cols)], (kt, cols))

            def load_deep(stage, m, n):
                mv = m.rearrange("(k p) n -> p k n", p=P)
                load(stage, 0, 0, mv[:, 0:2, :], (2, D))
                for j, s, i in steps(sp, 1, n - 2):
                    load(stage, s, i, mv[:, bass.ds(j * 2, 2), :], (2, D))
                load(stage, n - 1, 0, mv[:, 2 * n - 2:2 * n, :], (2, D))

            def load_ffn(up, down, layer):
                gv = w["ffn_w_gate_2"][layer].rearrange("(k p) n -> p k n", p=P)
                uv = w["ffn_w_up_2"][layer].rearrange("(k p) n -> p k n", p=P)
                for j, s, i in steps(sp, 0, 11, 2):
                    load(up, 2 * s, i, gv[:, :, bass.ds(j * WIDE, WIDE)], (KD, WIDE))
                    load(up, 2 * s + 1, i, uv[:, :, bass.ds(j * WIDE, WIDE)], (KD, WIDE))
                load_deep(down, w["ffn_w_down_2"][layer], 11)

            def load_layer0(s):
                load_wide(f"conv_in_{s}", w["conv_w_in_2"][0], 12)
                load_wide(f"conv_out_{s}", w["conv_w_out_2"][0], 4)
                load_ffn(f"up_{s}", f"down_{s}", 0)

            for b in range(SLOTS - 1):
                sp.sem_inc(w_free[b], 1)

            def start(dst, src):
                sp.dma_start(dst, src).then_inc(s_start, 16)

            start(consts[:, :], consts_dram)
            start(x_tok, w["x"][0].rearrange("(a p) d -> p a d", p=P))
            for name, key, rows in (("norm1", "norm1_g", 8), ("norm2", "norm2_g", 8), ("mix", "norm_mix_g_2", 16),
                                    ("ffn", "norm_ffn_g_2", 16), ("q_lat", "mla_q_norm_g_2", 6),
                                    ("kv_lat", "mla_kv_norm_g_2", 2), ("conv_b", "conv_b_2", 8),
                                    ("c", "c_2", 8)):
                a = VROWS[name]
                start(vrows[a:a + rows, :], w[key].rearrange("l (k p) -> (l k) p", p=P))
            for name, key in (("final", "final_norm_g"), ("c_ctx", "c_ctx_2")):
                start(vrows[VROWS[name]:VROWS[name] + 8, :], w[key].rearrange("(k p) -> k p", p=P))
            start(vrows[VROWS["conv_k"]:VROWS["conv_k"] + 24, :],
                  w["conv_k_2"][0].rearrange("j (k p) -> (j k) p", p=P))
            start(brows[0:96, :], w["mod_b_2"].rearrange("l (k p) -> (l k) p", p=P))
            for name, a, b in (("qn", "mla_qn_nope_g_2", "mla_qn_rope_g_2"), ("kn", "mla_kn_nope_g_2", "mla_kn_rope_g_2")):
                r = VROWS[name]
                start(vrows[r:r + 1, 0:NOPE], w[a])
                start(vrows[r:r + 1, NOPE:QH], w[b])
                start(vrows[r:r + 1, QH:P], w[b])
            start(ctx_tok, w["ctx_2"][0].rearrange("(a p) d -> p a d", p=P))

            wi = w["w_in"][0].rearrange("(k p) n -> p k n", p=P)
            for s in range(12):
                load("qkv", s, 0, wi[:, :, s * WIDE:(s + 1) * WIDE], (KD, WIDE))
            load_wide("gates", w["w_in"][0], 8, first=12 * WIDE)
            for stage, key in (("out_moba", "w_out_moba"), ("out_sb", "w_out_sb")):
                mv = w[key][0].rearrange("(k p) n -> p k n", p=P)
                for s in range(2):
                    load(stage, s, 0, mv[:, :, s * 512:(s + 1) * 512], (4, 512))
            load_wide("mix", w["w_mix_out"][0], 4)
            load_wide("peer_q", w["peer_w_q"][0], 8)
            sp.wait_ge(s_mixed, 1)
            sp.dma_start(keys, w["peer_sub_keys"][0].rearrange("h b n c -> n (h b) c")).then_inc(s_keys, 16)
            load_wide("mod0", w["mod_w_2"][0], 24)
            sp.wait_ge(s_split, 3)
            for a in range(2):
                for b in range(4):
                    for j in range(3):
                        sp.dma_start(xs[32 * j:32 * j + 32, 4 * a + b, :],
                                     split[j][32 * b:32 * b + 32, a, :]).then_inc(s_xs, 16)
            load_wide("mod1", w["mod_w_2"][1], 24)
            load_layer0("ctx")
            load_layer0("lat")
            load_wide("mla_in", w["mla_w_in_2"][0], 4)
            mv = w["mla_w_in_2"][0].rearrange("(k p) n -> p k n", p=P)
            load("mla_in", 4, 0, mv[:, :, QLAT + KVLAT:QLAT + KVLAT + ROPE], (KD, ROPE))
            mv = w["mla_w_kv_up_2"][0].rearrange("(k p) n -> p k n", p=P)
            for s in range(2):
                load("kv_up", s, 0, mv[:, :, 1024 * s:1024 * s + 1024], (2, 1024))
            load_wide("q_up", w["mla_w_q_up_2"][0], 8, kt=6, cols=2 * QH)
            load_wide("mla_out", w["mla_w_out_2"][0], 4)
            load_ffn("up_1", "down_1", 1)
            wait_all_emptied(sp, "turn_out", 4)
            sp.dma_start(out_dram[0].rearrange("(a p) d -> p a d", p=P), out_tok).then_inc(s_out, 16)
            sp.wait_ge(s_out, 16)

        N_START = 16 * 21

        @block.gpsimd
        def _(pool):
            pool.wait_ge(s_index, 3)
            pool.wait_ge(s_xs, 16 * 24)
            with pool.Fori(0, 16) as it:
                for s in range(16):
                    if s % 8 == 0:
                        for j in range(8):
                            pool.wait_ge(v_free[j], it * 2 + s // 8 + 1)
                        pool.sem_inc(s_turn, 1)
                        nc.gpsimd.tensor_copy(idx8[:, s // 8, :], idx_t[:, bass.ds(it * 16 + s, 8)])\
                            .then_inc(s_idx8, 1)
                        pool.wait_ge(s_idx8, it * 2 + s // 8 + 1)
                        pool.sem_inc(s_turn, 1)
                    at = bass.IndirectOffsetOnAxis(ap=idx8[:, s // 8, s % 8:s % 8 + 1], axis=0)
                    pool.wait_ge(u_free[s % 4], it * 4 + s // 4 + 1)
                    pool.sem_inc(s_turn, 1)
                    nc.gpsimd.indirect_dma_start(out=ubuf[s % 4], out_offset=None, in_=w["peer_u"][0],
                                                 in_offset=at).then_inc(u_landed[s % 4], 16)
                    pool.wait_ge(v_free[s % 8], it * 2 + s // 8 + 2)
                    pool.sem_inc(s_turn, 1)
                    nc.gpsimd.indirect_dma_start(out=vbuf[s % 8], out_offset=None, in_=w["peer_v"][0],
                                                 in_offset=at).then_inc(v_landed[s % 8], 16)

        @block.tensor
        def _(pe):
            for j in range(8):
                pe.sem_inc(v_free[j], 2)

            def product(stage, rhs, kt, i, s, cols=WIDE, width=T, group=None, first=0):
                wt = ring[slot_of(stage, s)][:, 0:kt * cols].rearrange("p (k n) -> p k n", k=kt)
                g = s if group is None else group
                wait_weights(pe, stage, s, i)
                wait_free(pe, stage, g, i)
                b = bank[bank_of(stage, g)]
                for m in range(cols // P):
                    for k in range(kt):
                        mm = nc.tensor.matmul(b[:, m * width:(m + 1) * width], wt[:, k, m * P:(m + 1) * P],
                                              rhs(k), start=(k == 0), stop=(k == kt - 1))
                        if m == k == 0:
                            opens(stage, s, mm)
                mm.then_inc(full[bank_of(stage, g)], 1)

            def opens(stage, s, mm):
                mm.then_inc(w_free[(CHUNK[stage] + s - 1) % SLOTS], 1)

            def products(stage, rhs, n, kt=KD):
                for j, s, i in steps(pe, 0, n):
                    product(stage, rhs, kt, i, s)

            def turns(stage, g, pieces):
                wait_free(pe, stage, g)
                b = bank[bank_of(stage, g)]
                for col, src in pieces:
                    n, m = src.shape[0], src.shape[1]
                    mm = nc.tensor.transpose(b[0:m, col:col + n], src, ident[0:n, 0:n])
                mm.then_inc(full[bank_of(stage, g)], 1)

            def norm(r, stage, kt=KD, width=T, src=None):
                pe.wait_ge(s_sq, r + 1)
                wait_free(pe, stage, 0)
                b = bank[bank_of(stage, 0)]
                for k in range(kt):
                    mm = nc.tensor.matmul(b[:, 0:width], ones[:, 0:P], sq[:, k, 0:T] if src is None else src(k),
                                          start=(k == 0), stop=(k == kt - 1))
                mm.then_inc(full[bank_of(stage, 0)], 1)

            def down(stage):
                for g in range(4):
                    wait_free(pe, stage, g)

                def part(j, s, i, first, last):
                    wait_weights(pe, stage, s, i)
                    wt = ring[slot_of(stage, s)].rearrange("p (k n) -> p k n", k=2)
                    for k in range(2):
                        for m in range(KD):
                            b = bank_of(stage, m // 2)
                            mm = nc.tensor.matmul(
                                bank[b][:, (m % 2) * T:(m % 2) * T + T], wt[:, k, m * P:(m + 1) * P],
                                hid[:, j * 2 + k, :] if isinstance(j, int) else hid[:, bass.ds(j * 2 + k, 1), :]
                                .rearrange("p a t -> p (a t)"),
                                start=(first and k == 0 and m % 2 == 0), stop=(last and k == 1),
                                skip_group_check=True)
                            if m == k == 0:
                                opens(stage, s, mm)
                            if last and k == 1 and m % 2 == 1:
                                mm.then_inc(full[b], 1)

                part(0, 0, 0, True, False)
                for j, s, i in steps(pe, 1, 9):
                    part(j, s, i, False, False)
                part(10, 10, 0, False, True)

            def ffn(up, dn, x, r):
                pe.wait_ge(s_norm, r + 1)
                for j, s, i in steps(pe, 0, 11, 2):
                    for half in range(2):
                        product(up, x, KD, i, 2 * s + half)
                wait_all_emptied(pe, up, 22)
                down(dn)

            def layer0(name, r, x, n):
                norm(r, f"mixnorm_{name}")
                pe.wait_ge(s_norm, r + 1)
                products(f"conv_in_{name}", x, 12)
                pe.wait_ge(s_conv, n + 1)
                products(f"conv_out_{name}", lambda k: cproj[:, k, :], 4)
                norm(r + 1, f"ffnnorm_{name}")
                ffn(f"up_{name}", f"down_{name}", x, r + 1)

            def lat(k):
                return nrm[:, k, T:2 * T]

            def con(k):
                return nrm[:, k, 0:T]

            pe.wait_ge(s_start, N_START)
            turns("vectors", 0, [(0, vrows[0:VROWS["end"], :])])
            turns("vectors", 1, [(0, brows[0:96, :])])
            for stage, src in (("turn_x", x_tok), ("turn_ctx", ctx_tok)):
                for g in range(4):
                    turns(stage, g, [(256 * a + 128 * t, src[:, t, (2 * g + a) * P:(2 * g + a + 1) * P])
                                     for a in range(2) for t in range(2)])

            norm(0, "norm1")
            pe.wait_ge(s_norm, 1)
            for s in range(12):
                if s % 6 < 4:
                    product("qkv", lat, KD, 0, s)
                else:
                    wait_weights(pe, "qkv", s)
                    wait_free(pe, "qkv", s)
                    wt = ring[slot_of("qkv", s)].rearrange("p (k n) -> p k n", k=KD)
                    for t in range(2):
                        for k in range(KD):
                            mm = nc.tensor.matmul(bank[bank_of("qkv", s)][:, t * WIDE:(t + 1) * WIDE],
                                                  nrm[:, k, T + t * P:T + (t + 1) * P], wt[:, k, :],
                                                  start=(k == 0), stop=(k == KD - 1))
                            if t == k == 0:
                                opens("qkv", s, mm)
                    mm.then_inc(full[bank_of("qkv", s)], 1)
            products("gates", lat, 8)

            wait_all_emptied(pe, "qkv", 12)
            for s in range(HALVES + 3):
                if s < HALVES:
                    b, kind, h = s % 4, s // HEADS, s % HEADS
                    pe.wait_ge(sc_free[b], s // 4 + 1)
                    lo = DH * (h % 2)
                    for t in range(2):
                        mm = nc.tensor.matmul(sbank[b][:, t * T:(t + 1) * T],
                                              qk[lo:lo + DH, 8 * kind + h // 2, t * P:(t + 1) * P],
                                              qk[lo:lo + DH, 8 * kind + 4 + h // 2, :], start=True, stop=True)
                    mm.then_inc(sc_full[b], 1)
                if 2 <= s < HALVES + 2:
                    n = s - 2
                    if n < HEADS:
                        pe.wait_ge(s_prob_v, n + 1)
                    else:
                        pe.wait_ge(s_prob_s, n - HEADS + 1)
                    turns("attention", ATT.index(("turn", n)),
                          [(256 * a + 128 * t, prob[:, n % 3, t, a * P:(a + 1) * P])
                           for a in range(2) for t in range(2)])
                if s >= 3:
                    n = s - 3
                    kind, h = n // HEADS, n % HEADS
                    g = ATT.index(("value", n // 2))
                    b = bank[bank_of("attention", g)]
                    wait_emptied(pe, "attention", ATT.index(("turn", n)))
                    if n % 2 == 0:
                        wait_free(pe, "attention", g)
                    lo = DH * (n % 2)
                    for a in range(2):
                        mm = nc.tensor.matmul(b[lo:lo + DH, 0:T], vtok[:, a, 512 * kind + DH * h:512 * kind + DH * h + DH],
                                              prob_t[:, n % 2, a, :], start=(a == 0), stop=(a == 1))
                    if n % 2 == 1:
                        mm.then_inc(full[bank_of("attention", g)], 1)

            wait_all_emptied(pe, "attention", len(ATT))
            for n, stage in enumerate(("out_moba", "out_sb")):
                for s in range(2):
                    wt = ring[slot_of(stage, s)].rearrange("p (k n) -> p k n", k=4)
                    wait_weights(pe, stage, s)
                    for g in range(2 * s, 2 * s + 2):
                        wait_free(pe, stage, g)
                        for m in range(2):
                            col = (g % 2) * 256 + m * P
                            for k in range(4):
                                mm = nc.tensor.matmul(bank[bank_of(stage, g)][:, m * T:(m + 1) * T],
                                                      wt[:, k, col:col + P], o_t[:, 4 * n + k, :],
                                                      start=(k == 0), stop=(k == 3))
                                if g == 2 * s and m == k == 0:
                                    opens(stage, s, mm)
                        mm.then_inc(full[bank_of(stage, g)], 1)
            pe.wait_ge(s_mixed, 1)
            products("mix", lambda k: gate[:, k, :], 4)

            norm(1, "norm2")
            pe.wait_ge(s_norm, 2)
            products("peer_q", lat, 8)
            pe.wait_ge(s_keys, 16)
            for g in range(4):
                turns("turn_keys", g, [(P * a, keys[:, 4 * g + a, :]) for a in range(4)])
            wait_all_emptied(pe, "peer_q", 8)
            wait_all_emptied(pe, "turn_keys", 4)
            for g in range(8):
                t, n = g // 4, g % 4
                wait_free(pe, "peer_scores", g)
                for a in range(4):
                    mm = nc.tensor.matmul(bank[bank_of("peer_scores", g)][:, a * P:(a + 1) * P],
                                          pq[:, 4 * n + a, t * P:(t + 1) * P], keys_t[:, 4 * n + a, :],
                                          start=True, stop=True)
                mm.then_inc(full[bank_of("peer_scores", g)], 1)
            for g in range(4):
                turns("turn_x2", g, [(P * a, lat(4 * (g % 2) + a)[:, (g // 2) * P:(g // 2) * P + P]) for a in range(4)])

            wait_emptied(pe, "vectors", 0)
            pe.wait_ge(s_cvec, 2)
            for stage in ("mod0", "mod1"):
                wait_free(pe, stage, 0)
                b = bank[bank_of(stage, 0)]
                for j, s, i in chain(steps(pe, 0, 20), steps(pe, 20, 4)):
                    wait_weights(pe, stage, s, i)
                    wt = ring[slot_of(stage, s)].rearrange("p (k n) -> p k n", k=KD)
                    for m in range(2):
                        for k in range(KD):
                            mm = nc.tensor.matmul(b[:, bass.ds(j * 4 + 2 * m, 2)], wt[:, k, m * P:(m + 1) * P],
                                                  cvec[:, k, :], start=(k == 0), stop=(k == KD - 1))
                            if m == k == 0:
                                opens(stage, s, mm)
                    if s == 23:
                        mm.then_inc(full[bank_of(stage, 0)], 1)

            pe.wait_ge(s_xs, 16 * 24)
            layer0("ctx", 2, con, 0)

            pe.wait_ge(s_chosen, 1)
            turns("turn_chosen", 0, [(P * t, chosen[:, t, :]) for t in range(2)]
                  + [(256 + P * t, shifted[:, t].rearrange("p h k -> p (h k)")) for t in range(2)])

            pe.wait_ge(s_index, 3)
            vo = [bank[bank_of("norm_final", half)] for half in range(2)]
            for half in range(2):
                wait_free(pe, "norm_final", half)
            with pe.Fori(0, 8) as g:
                with pe.Fori(0, 2) as h:
                    it = g * 2 + h

                    def spread(quad):
                        for s in range(4 * quad, 4 * quad + 4):
                            pe.wait_ge(xb_free[s % 2], it * 8 + s // 2 + 1)
                            for c in range(2):
                                mm = nc.tensor.matmul(
                                    wide[s % 2][:, 512 * c:512 * c + 512],
                                    sel[:, bass.ds(h * 16 + s, 1), :].rearrange("p a n -> p (a n)"),
                                    xs[:, bass.ds(g, 1), 512 * c:512 * c + 512].rearrange("p a n -> p (a n)"),
                                    start=True, stop=True)
                            mm.then_inc(xb_full[s % 2], 1)

                    def experts(quad):
                        pe.wait_ge(s_wts, it * 4 + quad + 1)
                        if quad % 2 == 0:
                            pe.wait_ge(vo_free, it * 2 + quad // 2 + 1)
                        for s in range(4 * quad, 4 * quad + 4):
                            pe.wait_ge(v_landed[s % 8], (it * 2 + s // 8 + 1) * 16)
                            for m in range(KD):
                                col = m * 8 + s % 8
                                mm = nc.tensor.matmul(vo[s // 8][:, col:col + 1], vbuf[s % 8][:, m * P:(m + 1) * P],
                                                      wts[:, s:s + 1], start=True, stop=True)
                            mm.then_inc(v_free[s % 8], 1)

                    spread(0)
                    spread(1)
                    experts(0)
                    spread(2)
                    experts(1)
                    spread(3)
                    experts(2)
                    experts(3)
            pe.wait_ge(vo_free, 34)

            norm(4, "norm_final")
            layer0("lat", 5, lat, 1)

            norm(7, "mixnorm1_ctx")
            norm(8, "mixnorm1_lat")
            pe.wait_ge(s_norm, 9)
            for s in range(3):
                product("mla_in", lat, KD, 0, s)
            wait_weights(pe, "mla_in", 3)
            wt = ring[slot_of("mla_in", 3)].rearrange("p (k n) -> p k n", k=KD)
            for m in range(2):
                wait_free(pe, "mla_in", 3 + m)
                for k in range(KD):
                    mm = nc.tensor.matmul(bank[bank_of("mla_in", 3 + m)][:, :], wt[:, k, m * P:(m + 1) * P],
                                          nrm[:, k, :], start=(k == 0), stop=(k == KD - 1))
                    if m == k == 0:
                        opens("mla_in", 3, mm)
                mm.then_inc(full[bank_of("mla_in", 3 + m)], 1)
            wait_weights(pe, "mla_in", 4)
            wait_free(pe, "mla_in", 5)
            wt = ring[slot_of("mla_in", 4)][:, 0:KD * ROPE].rearrange("p (k n) -> p k n", k=KD)
            for k in range(KD):
                mm = nc.tensor.matmul(bank[bank_of("mla_in", 5)][NOPE:QH, :], wt[:, k, :], nrm[:, k, :],
                                      start=(k == 0), stop=(k == KD - 1))
                if k == 0:
                    opens("mla_in", 4, mm)
            mm.then_inc(full[bank_of("mla_in", 5)], 1)

            def square_wide(k):
                return sq[:, 2 * k:2 * k + 2, :].rearrange("p a t -> p (a t)")

            norm(9, "qlat_norm", 6)
            norm(10, "kvlat_norm", 2, 2 * T, square_wide)
            pe.wait_ge(s_sq, 12)
            wait_free(pe, "kpe_norm", 0)
            nc.tensor.matmul(bank[bank_of("kpe_norm", 0)][NOPE:QH, :], mean[NOPE:QH, NOPE:QH],
                             square_wide(0)[NOPE:QH, :], start=True, stop=True)\
                .then_inc(full[bank_of("kpe_norm", 0)], 1)
            pe.wait_ge(s_norm, 12)
            wait_free(pe, "kpe_turn", 0)
            nc.tensor.matmul(bank[bank_of("kpe_turn", 0)][NOPE:QH, 0:T], turn[NOPE:QH, NOPE:QH],
                             kpe[NOPE:QH, T:2 * T], start=True, stop=True)\
                .then_inc(full[bank_of("kpe_turn", 0)], 1)
            for s in range(2):
                wait_weights(pe, "kv_up", s)
                wt = ring[slot_of("kv_up", s)].rearrange("p (k n) -> p k n", k=2)
                for n in range(8):
                    g = 12 * s + n
                    wait_free(pe, "kv_up", g)
                    for k in range(2):
                        mm = nc.tensor.matmul(bank[bank_of("kv_up", g)][0:NOPE, :], wt[:, k, P * n:P * n + NOPE],
                                              kvlat[:, k, :], start=(k == 0), stop=(k == 1))
                        if n == k == 0:
                            opens("kv_up", s, mm)
                    mm.then_inc(full[bank_of("kv_up", g)], 1)
                for t in range(4):
                    g = 12 * s + 8 + t
                    wait_free(pe, "kv_up", g)
                    for k in range(2):
                        mm = nc.tensor.matmul(
                            bank[bank_of("kv_up", g)][:, :], kvlat[:, k, t * P:(t + 1) * P],
                            wt[:, k, :].rearrange("p (h c) -> p h c", h=8)[:, :, NOPE:P],
                            start=(k == 0), stop=(k == 1))
                    mm.then_inc(full[bank_of("kv_up", g)], 1)
            for n in range(MH):
                pe.wait_ge(s_ksq, n + 1)
                wait_free(pe, "k_norm", n)
                nc.tensor.matmul(bank[bank_of("k_norm", n)][0:NOPE, :], mean[0:NOPE, 0:NOPE],
                                 square_wide(n % 4)[0:NOPE, :], start=True, stop=True)\
                    .then_inc(full[bank_of("k_norm", n)], 1)
            for s in range(8):
                wait_weights(pe, "q_up", s)
                wait_free(pe, "q_up", s)
                wt = ring[slot_of("q_up", s)][:, 0:12 * QH].rearrange("p (k n) -> p k n", k=6)
                for m in range(2):
                    for k in range(6):
                        mm = nc.tensor.matmul(bank[bank_of("q_up", s)][0:QH, m * T:(m + 1) * T],
                                              wt[:, k, m * QH:(m + 1) * QH], qlat[:, k, :],
                                              start=(k == 0), stop=(k == 5))
                        if m == k == 0:
                            opens("q_up", s, mm)
                mm.then_inc(full[bank_of("q_up", s)], 1)
            for n in range(8):
                pe.wait_ge(s_qsq, n + 1)
                wait_free(pe, "q_norm", n)
                nc.tensor.matmul(bank[bank_of("q_norm", n)][0:QH, :], mean[0:QH, 0:QH],
                                 square_wide(n % 4)[0:QH, :], start=True, stop=True)\
                    .then_inc(full[bank_of("q_norm", n)], 1)
            for n in range(8):
                pe.wait_ge(s_qn, n + 1)
                wait_free(pe, "q_turn", n)
                nc.tensor.matmul(bank[bank_of("q_turn", n)][0:QH, :], turn[0:QH, 0:QH],
                                 q[0:QH, 2 * n:2 * n + 2, :].rearrange("p a t -> p (a t)"), start=True, stop=True)\
                    .then_inc(full[bank_of("q_turn", n)], 1)
            pe.wait_ge(s_qr, 8)
            pe.wait_ge(s_kn, MH)
            pe.wait_ge(s_kcat, 1)
            for s in range(MH + 2):
                if s < MH:
                    for t in range(2):
                        n = 2 * s + t
                        pe.wait_ge(sc_free[n % 4], 4 + n // 4 + 1)
                        nc.tensor.matmul(sbank[n % 4], q[0:QH, s, t * P:(t + 1) * P], kcat[0:QH, s, :],
                                         start=True, stop=True).then_inc(sc_full[n % 4], 1)
                if 1 <= s <= MH:
                    n = s - 1
                    pe.wait_ge(s_prob_v, HEADS + n + 1)
                    for half in range(2):
                        turns("mla_attention", MATT.index(("turn", 2 * n + half)),
                              [(256 * a + 128 * t, mprob[:, n % 2, t, (2 * half + a) * P:(2 * half + a + 1) * P])
                               for a in range(2) for t in range(2)])
                if s >= 2:
                    n = s - 2
                    g = MATT.index(("value", n // 2))
                    b = bank[bank_of("mla_attention", g)]
                    for half in range(2):
                        wait_emptied(pe, "mla_attention", MATT.index(("turn", 2 * n + half)))
                    if n % 2 == 0:
                        wait_free(pe, "mla_attention", g)
                    lo = MV * (n % 2)
                    for a in range(4):
                        mm = nc.tensor.matmul(b[lo:lo + MV, 0:T], vmla[:, a, MV * n:MV * n + MV], mprob_t[:, n % 2, a, :],
                                              start=(a == 0), stop=(a == 3))
                    if n % 2 == 1:
                        mm.then_inc(full[bank_of("mla_attention", g)], 1)
            wait_all_emptied(pe, "mla_attention", len(MATT))
            products("mla_out", lambda k: o_mla[:, k, :], 4)
            norm(12, "ffnnorm1")
            ffn("up_1", "down_1", lat, 12)
            wait_all_emptied(pe, "down_1", 4)
            for g in range(4):
                turns("turn_out", g, [(P * a, h_lat[:, 4 * (g % 2) + a, (g // 2) * P:(g // 2) * P + P]) for a in range(4)])

        @block.scalar
        def _(act):
            for b in range(BANKS):
                act.sem_inc(free[b], 1)
            act.sem_inc(vo_free, 2)

            def leave(stage, g, dst, i=0, cols=slice(0, 512), rows=slice(0, P), func=ACT.Copy, scale=1.0, bias=None):
                wait_full(act, stage, g, i)
                b = bank_of(stage, g)
                src = bank[b][rows, cols]
                if len(dst.shape) == 3:
                    src = src.rearrange("p (a n) -> p a n", a=dst.shape[1])
                more_args = {} if bias is None else {"bias": bias}
                nc.scalar.activation(dst, src, func, scale=scale, **more_args).then_inc(free[b], 1)

            def leaves(stage, n, dst, per=2, **kw):
                for j, s, i in steps(act, 0, n):
                    where = bass.ds(j * per, per) if not isinstance(j, int) else slice(j * per, j * per + per)
                    leave(stage, s, dst[:, where, :], i, **kw)

            def root(stage, d, width=T, rows=slice(0, P), slot=0):
                leave(stage, 0, std[rows, slot, 0:width], cols=slice(0, width), rows=rows,
                      func=ACT.Sqrt, scale=1.0 / d, bias=eps[rows, :])

            def gated(up):
                for j, s, i in steps(act, 0, 11, 2):
                    dst = hid[:, 2 * j:2 * j + 2, :] if isinstance(j, int) else hid[:, bass.ds(j * 2, 2), :]
                    leave(up, 2 * s, dst, i, func=ACT.Silu)

            def layer0(name):
                root(f"mixnorm_{name}", D)
                leaves(f"conv_in_{name}", 12, cproj)
                root(f"ffnnorm_{name}", D)
                gated(f"up_{name}")

            leave("vectors", 0, vec[:, :], cols=slice(0, VROWS["end"]))
            leave("vectors", 1, modb[:, :], cols=slice(0, 96))
            leaves("turn_x", 4, h_lat)
            leaves("turn_ctx", 4, h_ctx)
            wait_emptied(act, "vectors", 0)
            for s, name in enumerate(("c", "c_ctx")):
                nc.scalar.activation(cvec[:, :, s], vec[:, VROWS[name]:VROWS[name] + 8], ACT.Silu).then_inc(s_cvec, 1)
            root("norm1", D)
            for s in range(12):
                kind, n = s // 6, s % 6
                if n < 4:
                    leave("qkv", s, qk[:, 8 * kind + 2 * n:8 * kind + 2 * n + 2, :], scale=DH ** -0.5 if n < 2 else 1.0)
                else:
                    at = 512 * kind + 256 * (n - 4)
                    leave("qkv", s, vtok[:, :, at:at + 256])
            leaves("gates", 8, gate, func=ACT.Sigmoid)

            for s in range(HALVES + 3):
                if s < HALVES:
                    act.wait_ge(s_soft_in, s + 1)
                    if s < HEADS:
                        for t in range(2):
                            last = nc.scalar.activation(prob[:, s % 3, t, :], logit[:, s % 3, t, :], ACT.Exp,
                                                        bias=small[:, s, t:t + 1], accum_out=small[:, s, 2 + t:3 + t])
                        last.then_inc(s_soft_exp, 1)
                    else:
                        nc.scalar.activation(expo[:, s % 3], expo[:, s % 3], ACT.Exp).then_inc(a_step, 1)
                        act.wait_ge(a_step, s - HEADS + 1)
                        nc.scalar.activation(soft[:, s % 3], expo[:, s % 3], ACT.Ln, bias=ones[:, 0:1])\
                            .then_inc(s_soft_exp, 1)
                if HEADS < s <= HALVES:
                    n = s - 1
                    act.wait_ge(s_arg, n - HEADS + 1)
                    nc.scalar.activation(prob[:, n % 3], logit[:, n % 3], ACT.Exp).then_inc(s_prob_s, 1)
                if 2 <= s < HALVES + 2:
                    leave("attention", ATT.index(("turn", s - 2)), prob_t[:, (s - 2) % 2])
                if s >= 3 and (s - 3) % 2 == 1:
                    leave("attention", ATT.index(("value", (s - 3) // 2)), o_t[:, (s - 3) // 2, :], cols=slice(0, T))

            root("norm2", D)
            leaves("peer_q", 8, pq)
            for g in range(4):
                leave("turn_keys", g, keys_t[:, 4 * g:4 * g + 4, :])
            for g in range(8):
                leave("peer_scores", g, score[:, g // 4, 4 * (g % 4):4 * (g % 4) + 4, :])
            for g in range(4):
                leave("turn_x2", g, x2_tok[:, g // 2, 512 * (g % 2):512 * (g % 2) + 512])
            act.wait_ge(s_shift, 1)
            nc.scalar.activation(shifted, shifted, ACT.Exp).then_inc(s_pexp, 1)

            layer0("ctx")

            vo = [bank[bank_of("norm_final", half)] for half in range(2)]

            with act.Fori(0, 16) as it:
                def sums_out(half):
                    act.wait_ge(v_free[7], it * 2 + half + 3)
                    nc.scalar.activation(peer[:, :, bass.ds(it * 16 + 8 * half, 8)],
                                         vo[half][:, 0:64].rearrange("p (m t) -> p m t", m=KD),
                                         ACT.Copy).then_inc(vo_free, 1)

                for quad in range(4):
                    act.wait_ge(s_dots, it * 4 + quad + 1)
                    nc.scalar.activation(gelus[:, 4 * quad:4 * quad + 4], dots[:, 4 * quad:4 * quad + 4], ACT.Gelu)\
                        .then_inc(s_gelu, 1)
                sums_out(0)
                sums_out(1)

            root("norm_final", D)
            layer0("lat")

            root("mixnorm1_ctx", D)
            root("mixnorm1_lat", D)
            for s in range(3):
                leave("mla_in", s, qlat[:, 2 * s:2 * s + 2, :])
            for m in range(2):
                leave("mla_in", 3 + m, kvlat[:, m, :])
            leave("mla_in", 5, kpe[NOPE:QH, :], rows=slice(NOPE, QH))
            root("qlat_norm", QLAT)
            root("kvlat_norm", KVLAT, 2 * T)
            root("kpe_norm", 1.0, 2 * T, slice(NOPE, QH))
            for s in range(2):
                for n in range(8):
                    leave("kv_up", 12 * s + n, kcat[0:NOPE, 8 * s + n, :], rows=slice(0, NOPE))
                for t in range(4):
                    leave("kv_up", 12 * s + 8 + t, vmla[:, t, 512 * s:512 * s + 512])
            act.wait_ge(s_kpe, 1)
            nc.scalar.activation(kcat[NOPE:QH], kpe[NOPE:QH, :].unsqueeze(1).to_broadcast([ROPE, MH, 2 * T]),
                                 ACT.Copy).then_inc(s_kcat, 1)
            for stage, done, rows, n_groups in (("k_norm", s_kn, NOPE, MH), ("q_norm", s_qn, QH, 8)):
                if stage == "q_norm":
                    for s in range(8):
                        leave("q_up", s, q[0:QH, 2 * s:2 * s + 2, :], rows=slice(0, QH))
                for n in range(n_groups):
                    if n >= 2:
                        act.wait_ge(done, n - 1)
                    leave(stage, n, std[0:rows, n % 2, :], rows=slice(0, rows), func=ACT.Sqrt, bias=eps[0:rows, :])
            for s in range(MH + 2):
                if s < MH:
                    act.wait_ge(s_soft_in, HALVES + s + 1)
                    for t in range(2):
                        n = 2 * s + t
                        nc.scalar.activation(mprob[:, s % 2, t, :], sbank[n % 4], ACT.Exp, scale=QH ** -0.5,
                                             bias=msmall[:, s, t:t + 1], accum_out=msmall[:, s, 2 + t:3 + t])\
                            .then_inc(sc_free[n % 4], 1)
                if 1 <= s <= MH:
                    for half in range(2):
                        leave("mla_attention", MATT.index(("turn", 2 * (s - 1) + half)),
                              mprob_t[:, (s - 1) % 2, 2 * half:2 * half + 2, :])
                if s >= 2 and s % 2 == 1:
                    leave("mla_attention", MATT.index(("value", (s - 2) // 2)), o_mla[:, (s - 2) // 2, :],
                          cols=slice(0, T))
            root("ffnnorm1", D)
            gated("up_1")
            for g in range(4):
                leave("turn_out", g, out_tok[:, g // 2, 512 * (g % 2):512 * (g % 2) + 512])

        @block.vector
        def _(v):
            for b in range(4):
                v.sem_inc(sc_free[b], 1)
                v.sem_inc(u_free[b], 1)
            for b in range(2):
                v.sem_inc(xb_free[b], 1)

            counted = [0]

            def settle(instruction):
                counted[0] += 1
                instruction.then_inc(s_step, 1)
                v.wait_ge(s_step, counted[0])

            def tt(out, a, b, op):
                return nc.vector.tensor_tensor(out, a, b, op)

            def spread_last(a, n):
                return a.unsqueeze(len(a.shape)).to_broadcast([*a.shape, n])

            def apply_norm(r, root_stage, kt, src, gain, dst, shift=None, width=T, rows=slice(0, P)):
                wait_emptied(v, root_stage, 0)
                settle(nc.vector.reciprocal(rstd[rows, 0, 0:width], std[rows, 0, 0:width]))
                for k in range(kt):
                    last = nc.vector.scalar_tensor_tensor(dst(k), src(k), gain(k), rstd[rows, 0, 0:width],
                                                          ALU.mult, ALU.mult)
                if shift is not None:
                    settle(last)
                    for k in range(kt):
                        last = nc.vector.tensor_scalar(dst(k), dst(k), shift(k), None, ALU.add)
                last.then_inc(s_norm, 1)
                v.wait_ge(s_norm, r + 1)

            def norm(r, stage, x, gain, dst, shift=None):
                tt(sq[:, :, :], x[:, :, :], x[:, :, :], ALU.mult).then_inc(s_sq, 1)
                apply_norm(r, stage, KD, lambda k: x[:, k, :], gain, dst, shift)

            def lat(k):
                return nrm[:, k, T:2 * T]

            def con(k):
                return nrm[:, k, 0:T]

            def mod_norm(r, stage, layer, i, x, dst, who):
                norm(r, stage, x, lambda k: gmod[:, layer, i, k, who:who + 1], dst,
                     lambda k: mod[:, layer, 24 * i + k, who:who + 1])

            def residual(stage, layer, i, h, who, n):
                for g in range(4):
                    wait_full(v, stage, g)
                    b = bank_of(stage, g)
                    for m in range(2):
                        k = 2 * g + m
                        last = nc.vector.scalar_tensor_tensor(
                            h[:, k, :], bank[b][:, m * T:(m + 1) * T], mod[:, layer, 24 * i + 16 + k, who:who + 1],
                            h[:, k, :], ALU.mult, ALU.add)
                    last.then_inc(free[b], 1)
                wait_all_emptied(v, stage, 4)

            def hidden(up):
                for j, s, i in steps(v, 0, 11, 2):
                    wait_full(v, up, 2 * s + 1, i)
                    wait_emptied(v, up, 2 * s, i)
                    b = bank_of(up, 2 * s + 1)
                    here = hid[:, 2 * j:2 * j + 2, :] if isinstance(j, int) else hid[:, bass.ds(j * 2, 2), :]
                    tt(here, here, bank[b][:, :].rearrange("p (a t) -> p a t", a=2), ALU.mult).then_inc(free[b], 1)

            def layer0(name, r, h, dst, who, n):
                mod_norm(r, f"mixnorm_{name}", 0, 0, h, dst, who)
                nc.vector.memset(z[:, :, 0:1], 0.0)
                settle(nc.vector.memset(z[:, :, T + 1:T + 2], 0.0))
                wait_all_emptied(v, f"conv_in_{name}", 12)
                settle(tt(z[:, :, 1:T + 1], cproj[:, 8:16, :], cproj[:, 16:24, :], ALU.mult))
                for k in range(KD):
                    last = nc.vector.tensor_scalar(cproj[:, 8 + k, :], z[:, k, 0:T], vcol("conv_k", k),
                                                   vcol("conv_b", k), ALU.mult, ALU.add)
                settle(last)
                for tap in (1, 2):
                    for k in range(KD):
                        last = nc.vector.scalar_tensor_tensor(
                            cproj[:, 8 + k, :], z[:, k, tap:tap + T], vcol("conv_k", 8 * tap + k), cproj[:, 8 + k, :],
                            ALU.mult, ALU.add)
                    settle(last)
                tt(cproj[:, 0:8, :], cproj[:, 0:8, :], cproj[:, 8:16, :], ALU.mult).then_inc(s_conv, 1)
                residual(f"conv_out_{name}", 0, 0, h, who, n)
                mod_norm(r + 1, f"ffnnorm_{name}", 0, 1, h, dst, who)
                hidden(f"up_{name}")
                residual(f"down_{name}", 0, 1, h, who, n + 1)

            wait_emptied(v, "vectors", 0)
            wait_all_emptied(v, "turn_x", 4)
            norm(0, "norm1", h_lat, lambda k: vcol("norm1", k), lat)
            nc.vector.tensor_copy(sel[:, :, :], spread_last(row32, P)).then_inc(s_index, 1)

            def front(n):
                b, c = n % 4, n % 3
                v.wait_ge(sc_full[b], n // 4 + 1)
                scores = sbank[b].rearrange("p (t k) -> p t k", t=2)
                if n < HEADS:
                    slope = 2.0 ** (-8.0 * (n + 1) / HEADS)
                    nc.vector.scalar_tensor_tensor(logit[:, c], dist, -slope, scores, ALU.mult, ALU.add)\
                        .then_inc(sc_free[b], 1)
                    v.wait_ge(sc_free[b], n // 4 + 2)
                    nc.vector.tensor_reduce(small[:, n, 0:2], logit[:, c], AX.X, ALU.max, negate=True)\
                        .then_inc(s_soft_in, 1)
                else:
                    if n - 3 >= HEADS:
                        v.wait_ge(s_prob_s, n - 3 - HEADS + 1)
                    tt(logit[:, c], scores, strict, ALU.add).then_inc(sc_free[b], 1)
                    v.wait_ge(sc_free[b], n // 4 + 2)
                    nc.vector.scalar_tensor_tensor(expo[:, c], logit[:, c], -1.0, logit[:, c], ALU.mult, ALU.min)\
                        .then_inc(s_soft_in, 1)

            def back(n):
                c = n % 3
                v.wait_ge(s_soft_exp, n + 1)
                if n < HEADS:
                    settle(nc.vector.reciprocal(small[:, n, 4:6], small[:, n, 2:4]))
                    tt(prob[:, c], prob[:, c], spread_last(small[:, n, 4:6], T), ALU.mult).then_inc(s_prob_v, 1)
                else:
                    settle(nc.vector.scalar_tensor_tensor(soft[:, c], logit[:, c], 0.0, soft[:, c], ALU.max, ALU.add))
                    for t in range(2):
                        last = nc.vector.tensor_tensor_scan(expo[:, c, t, ::-1], ones, soft[:, c, t, ::-1], 0.0,
                                                            ALU.mult, ALU.add)
                    settle(last)
                    tt(logit[:, c], logit[:, c], expo[:, c], ALU.subtract).then_inc(s_arg, 1)

            for s in range(HALVES + 1):
                if s < HALVES:
                    front(s)
                if s >= 1:
                    back(s - 1)

            wait_all_emptied(v, "gates", 8)
            for n, stage in enumerate(("out_moba", "out_sb")):
                for g in range(4):
                    wait_full(v, stage, g)
                    b = bank_of(stage, g)
                    here = gate[:, 8 * n + 2 * g:8 * n + 2 * g + 2, :]
                    tt(here, here, bank[b][:, :].rearrange("p (a t) -> p a t", a=2), ALU.mult).then_inc(free[b], 1)
                wait_all_emptied(v, stage, 4)
            tt(gate[:, 0:8, :], gate[:, 0:8, :], gate[:, 8:16, :], ALU.add).then_inc(s_mixed, 1)
            for g in range(4):
                wait_full(v, "mix", g)
                b = bank_of("mix", g)
                here = h_lat[:, 2 * g:2 * g + 2, :]
                tt(here, here, bank[b][:, :].rearrange("p (a t) -> p a t", a=2), ALU.add).then_inc(free[b], 1)
            wait_all_emptied(v, "mix", 4)
            norm(1, "norm2", h_lat, lambda k: vcol("norm2", k), lat)

            def sixteen(rows, best_of, index_of, count):
                for a in range(0, count, 4):
                    four = range(a, a + 4)
                    for n in four:
                        last = nc.vector.max(best_of(n)[:, 0:8], rows(n))
                    settle(last)
                    for n in four:
                        nc.vector.max_index(index_of(n)[:, 0:8], best_of(n)[:, 0:8], rows(n))
                        last = nc.vector.match_replace(rows(n), best_of(n)[:, 0:8], rows(n), -3.4e38)
                    settle(last)
                    for n in four:
                        last = nc.vector.max(best_of(n)[:, 8:16], rows(n))
                    settle(last)
                    for n in four:
                        last = nc.vector.max_index(index_of(n)[:, 8:16], best_of(n)[:, 8:16], rows(n))
                settle(last)

            wait_all_emptied(v, "turn_x2", 4)
            nc.vector.tensor_copy(split[0], x2_tok).then_inc(s_split, 1)
            v.wait_ge(s_split, 1)
            settle(tt(rest, x2_tok, split[0], ALU.subtract))
            nc.vector.tensor_copy(split[1], rest).then_inc(s_split, 1)
            v.wait_ge(s_split, 2)
            settle(tt(rest, rest, split[1], ALU.subtract))
            nc.vector.tensor_copy(split[2], rest).then_inc(s_split, 1)

            for t in range(2):
                sixteen(lambda n: score[:, t, n, :], lambda n: top[:, t, n, :], lambda n: top_i[:, t, n, :], 16)
                nc.vector.tensor_copy(top_f[:, t], top_i[:, t])
                pair = top[:, t].rearrange("p (h b) k -> p h b k", b=2)
                settle(tt(cand.rearrange("p h (i j) -> p h i j", i=TOPK),
                          pair[:, :, 0, :].unsqueeze(3).to_broadcast([P, PH, TOPK, TOPK]),
                          pair[:, :, 1, :].unsqueeze(2).to_broadcast([P, PH, TOPK, TOPK]), ALU.add))
                pos_h = pos.rearrange("p (h k) -> p h k", h=PH)
                sixteen(lambda n: cand[:, n, :], lambda n: best[:, t, n, :], lambda n: pos_h[:, n, :], PH)
                nc.vector.tensor_scalar(part[:, 0], pos, 4, None, ALU.logical_shift_right)
                settle(nc.vector.tensor_scalar(part[:, 1], pos, 15, None, ALU.bitwise_and))
                settle(nc.vector.tensor_copy(part_f, part))
                index = top_f[:, t].rearrange("p (h b) k -> p h b k", b=2)
                for b in range(2):
                    settle(tt(eq, spread_last(part_f[:, b], TOPK),
                              iota.unsqueeze(1).to_broadcast([P, P, TOPK]), ALU.is_equal))
                    eq_h = eq.rearrange("p (h k) m -> p h k m", h=PH)
                    settle(tt(eq_h, eq_h, index[:, :, b, :].unsqueeze(2).to_broadcast([P, PH, TOPK, TOPK]), ALU.mult))
                    settle(nc.vector.tensor_reduce(pick[:, b], eq, AX.X, ALU.add))
                nc.vector.scalar_tensor_tensor(chosen[:, t], pick[:, 0], float(KEYS), pick[:, 1], ALU.mult, ALU.add)
                last = tt(shifted[:, t], best[:, t], best[:, t, :, 0:1].to_broadcast([P, PH, TOPK]), ALU.subtract)
                settle(last)
            v.sem_inc(s_shift, 1)
            v.wait_ge(s_pexp, 1)
            settle(nc.vector.tensor_reduce(sums[:, 0], shifted, AX.X, ALU.add))
            settle(nc.vector.reciprocal(sums[:, 1], sums[:, 0]))
            last = None
            for t in range(2):
                last = tt(shifted[:, t], shifted[:, t], spread_last(sums[:, 1, t], TOPK), ALU.mult)
            last.then_inc(s_chosen, 1)

            for layer, stage in enumerate(("mod0", "mod1")):
                wait_full(v, stage, 0)
                b = bank_of(stage, 0)
                tt(mod[:, layer], bank[b][:, 0:96].rearrange("p (m s) -> p m s", s=2),
                   spread_last(modb[:, 48 * layer:48 * layer + 48], 2), ALU.add).then_inc(free[b], 1)
                wait_emptied(v, stage, 0)
                for i, name in enumerate(("mix", "ffn")):
                    a = VROWS[name] + 8 * layer
                    last = nc.vector.scalar_tensor_tensor(gmod[:, layer, i], mod[:, layer, 24 * i + 8:24 * i + 16, :],
                                                          1.0, spread_last(vec[:, a:a + 8], 2), ALU.add, ALU.mult)
                settle(last)

            layer0("ctx", 2, h_ctx, con, 1, 0)

            wait_full(v, "turn_chosen", 0)
            b = bank_of("turn_chosen", 0)
            nc.vector.tensor_copy(idx_t[:, :], bank[b][:, 0:T]).then_inc(s_index, 1)
            v.wait_ge(s_index, 2)
            nc.vector.tensor_copy(gate_t[:, :], bank[b][:, T:2 * T]).then_inc(s_index, 1)
            v.wait_ge(s_index, 3)
            v.sem_inc(free[b], 1)
            with v.Fori(0, 16) as it:
                def products(quad):
                    for s in range(4 * quad, 4 * quad + 4):
                        v.wait_ge(u_landed[s % 4], (it * 4 + quad + 1) * 16)
                        v.wait_ge(xb_full[s % 2], it * 8 + s // 2 + 1)
                        nc.vector.tensor_tensor_reduce(ubuf[s % 4], ubuf[s % 4], wide[s % 2][:, :], 1.0, 0.0,
                                                       ALU.mult, ALU.add, dots[:, s:s + 1]).then_inc(xb_free[s % 2], 1)
                    for j in range(2):
                        v.wait_ge(xb_free[j], it * 8 + 2 * quad + 3)
                    for j in range(4):
                        v.sem_inc(u_free[j], 1)
                    v.sem_inc(s_dots, 1)

                def weigh(quad):
                    v.wait_ge(s_gelu, it * 4 + quad + 1)
                    tt(wts[:, 4 * quad:4 * quad + 4], gelus[:, 4 * quad:4 * quad + 4],
                       gate_t[:, bass.ds(it * 16 + 4 * quad, 4)], ALU.mult).then_inc(s_wts, 1)

                products(0)
                products(1)
                weigh(0)
                products(2)
                weigh(1)
                products(3)
                weigh(2)
                weigh(3)
            v.wait_ge(vo_free, 34)
            settle(tt(h_lat[:, :, :], h_lat[:, :, :], peer, ALU.add))
            norm(4, "norm_final", h_lat, lambda k: vcol("final", k), lambda k: h_lat[:, k, :])

            layer0("lat", 5, h_lat, lat, 0, 2)

            mod_norm(7, "mixnorm1_ctx", 1, 0, h_ctx, con, 1)
            mod_norm(8, "mixnorm1_lat", 1, 0, h_lat, lat, 0)
            wait_all_emptied(v, "mla_in", 6)
            tt(sq[:, 0:6, :], qlat, qlat, ALU.mult).then_inc(s_sq, 1)
            apply_norm(9, "qlat_norm", 6, lambda k: qlat[:, k, :], lambda k: vcol("q_lat", k), lambda k: qlat[:, k, :])

            def square_wide(n, rows):
                return sq[rows, 2 * n:2 * n + 2, :].rearrange("p a t -> p (a t)")

            every = slice(0, P)
            for k in range(2):
                last = tt(square_wide(k, every), kvlat[:, k, :], kvlat[:, k, :], ALU.mult)
            last.then_inc(s_sq, 1)
            apply_norm(10, "kvlat_norm", 2, lambda k: kvlat[:, k, :], lambda k: vcol("kv_lat", k),
                       lambda k: kvlat[:, k, :], width=2 * T)
            rope = slice(NOPE, QH)
            tt(square_wide(0, rope), kpe[rope, :], kpe[rope, :], ALU.mult).then_inc(s_sq, 1)
            apply_norm(11, "kpe_norm", 1, lambda k: kpe[rope, :], lambda k: vcol("kn", 0)[rope, :],
                       lambda k: kpe[rope, :], width=2 * T, rows=rope)
            wait_full(v, "kpe_turn", 0)
            b = bank_of("kpe_turn", 0)
            nc.vector.tensor_tensor(std[rope, 0, 0:T], bank[b][rope, 0:T], sin[rope, :], ALU.mult).then_inc(free[b], 1)
            settle(tt(kpe[rope, T:2 * T], kpe[rope, T:2 * T], cos[rope, :], ALU.mult))
            tt(kpe[rope, T:2 * T], kpe[rope, T:2 * T], std[rope, 0, 0:T], ALU.add).then_inc(s_kpe, 1)
            v.wait_ge(s_kpe, 1)

            def head_norms(n_heads, rows, raw_ready, x, gain, squared, root_stage, done):
                for n in range(n_heads + 1):
                    if n < n_heads:
                        raw_ready(n)
                        tt(square_wide(n % 4, rows), x(n), x(n), ALU.mult).then_inc(squared, 1)
                    if n >= 1:
                        m = n - 1
                        wait_emptied(v, root_stage, m)
                        settle(nc.vector.reciprocal(rstd[rows, m % 2, :], std[rows, m % 2, :]))
                        nc.vector.scalar_tensor_tensor(x(m), x(m), gain, rstd[rows, m % 2, :], ALU.mult, ALU.mult)\
                            .then_inc(done, 1)

            head_norms(MH, slice(0, NOPE), lambda n: wait_emptied(v, "kv_up", 12 * (n // 8) + n % 8),
                       lambda n: kcat[0:NOPE, n, :], vcol("kn", 0)[0:NOPE, :], s_ksq, "k_norm", s_kn)
            head_norms(8, slice(0, QH), lambda n: wait_emptied(v, "q_up", n),
                       lambda n: q[0:QH, 2 * n:2 * n + 2, :].rearrange("p a t -> p (a t)"),
                       vcol("qn", 0)[0:QH, :], s_qsq, "q_norm", s_qn)
            for n in range(8):
                wait_full(v, "q_turn", n)
                b = bank_of("q_turn", n)
                pair = q[0:QH, 2 * n:2 * n + 2, :]
                turned = sq[0:QH, 2 * (n % 4):2 * (n % 4) + 2, :]
                tt(turned, bank[b][0:QH, :].rearrange("p (a t) -> p a t", a=2),
                   sin[0:QH, :].unsqueeze(1).to_broadcast([QH, 2, T]), ALU.mult).then_inc(free[b], 1)
                settle(tt(pair, pair, cos[0:QH, :].unsqueeze(1).to_broadcast([QH, 2, T]), ALU.mult))
                tt(pair, pair, turned, ALU.add).then_inc(s_qr, 1)
            for s in range(MH + 1):
                if s < MH:
                    for t in range(2):
                        n = 2 * s + t
                        v.wait_ge(sc_full[n % 4], 4 + n // 4 + 1)
                        last = nc.vector.tensor_reduce(msmall[:, s, 4 + t:5 + t], sbank[n % 4], AX.X, ALU.max, negate=True)
                    settle(last)
                    nc.vector.tensor_scalar(msmall[:, s, 0:2], msmall[:, s, 4:6], QH ** -0.5, None, ALU.mult)\
                        .then_inc(s_soft_in, 1)
                if s >= 1:
                    m = s - 1
                    for t in range(2):
                        v.wait_ge(sc_free[(2 * m + t) % 4], 4 + (2 * m + t) // 4 + 2)
                    settle(nc.vector.reciprocal(msmall[:, m, 6:8], msmall[:, m, 2:4]))
                    for t in range(2):
                        last = nc.vector.tensor_scalar(mprob[:, m % 2, t, :], mprob[:, m % 2, t, :],
                                                       msmall[:, m, 6 + t:7 + t], None, ALU.mult)
                    last.then_inc(s_prob_v, 1)
            residual("mla_out", 1, 0, h_lat, 0, 4)
            mod_norm(12, "ffnnorm1", 1, 1, h_lat, lat, 0)
            hidden("up_1")
            residual("down_1", 1, 1, h_lat, 0, 5)


_INS = ["x", "norm1_g", "w_in", "w_out_moba", "w_out_sb", "w_mix_out", "norm2_g", "peer_w_q", "peer_sub_keys",
        "peer_u", "peer_v", "final_norm_g", "c_2", "ctx_2", "c_ctx_2", "norm_mix_g_2", "norm_ffn_g_2", "mod_w_2",
        "mod_b_2", "ffn_w_gate_2", "ffn_w_up_2", "ffn_w_down_2", "conv_w_in_2", "conv_k_2", "conv_b_2",
        "conv_w_out_2", "mla_w_in_2", "mla_q_norm_g_2", "mla_w_q_up_2", "mla_kv_norm_g_2", "mla_w_kv_up_2",
        "mla_qn_nope_g_2", "mla_qn_rope_g_2", "mla_kn_nope_g_2", "mla_kn_rope_g_2", "mla_w_out_2"]


def kernel(**inputs):
    import concourse.bacc as bacc
    from concourse.bass_utils import run_bass_kernel_spmd

    nc = bacc.Bacc("TRN2", target_bir_lowering=False, num_devices=1)
    arrays, w = {}, {}
    for name in _INS:
        a = np.ascontiguousarray(inputs[name])
        arrays[f"in_{name}_dram"] = a
        w[name] = nc.dram_tensor(f"in_{name}_dram", a.shape, mybir.dt.from_np(a.dtype), kind="ExternalInput").ap()
    arrays["in_consts_dram"] = constants()
    consts = nc.dram_tensor("in_consts_dram", arrays["in_consts_dram"].shape, F32, kind="ExternalInput").ap()
    out = nc.dram_tensor("out_0_dram", (1, T, D), F32, kind="ExternalOutput").ap()
    program(nc, w, consts, out)
    r = run_bass_kernel_spmd(nc, [arrays], core_ids=[0])
    return r.results[0]["out_0_dram"]
```

```python
from contextlib import ExitStack
from itertools import chain

import numpy as np

import concourse.bass as bass
from concourse import mybir

P = 128
T = 256
D = 1024
KD = D // P
HID = 2816
KH = HID // P
HEADS = 8
DH = 64
PH, KEYS, TOPK = 8, 128, 16
MH, NOPE, ROPE, MV = 16, 64, 32, 64
QH = NOPE + ROPE
QLAT, KVLAT = 768, 256
SLOTS = 4
SLOT = 2048
WIDE = SLOT // KD
BANKS = 4
EPS = 1e-6
BIG = 1e30

F32 = mybir.dt.float32
BF16 = mybir.dt.bfloat16
U32 = mybir.dt.uint32
ALU = mybir.AluOpType
ACT = mybir.ActivationFunctionType
AX = mybir.AxisListType


def firsts(table):
    out, at = {}, 0
    for name, n in table:
        out[name] = at
        at += n
    return out


HALVES = 2 * HEADS
MODS = 24
MOD_STEP = [[] for _ in range(HALVES + 3)]
for _j in range(MODS):
    MOD_STEP[_j // 2 if _j < 10 else _j - 5].append(_j)
ATT = []
for _s in range(HALVES + 3):
    ATT += [("mod", _j) for _j in MOD_STEP[_s]]
    if 2 <= _s < HALVES + 2:
        ATT.append(("turn", _s - 2))
    if _s >= 3 and (_s - 3) % 2 == 1:
        ATT.append(("value", (_s - 3) // 2))
MATT = []
for _s in range(1, MH + 2):
    if _s >= 2 and _s % 2 == 0:
        MATT.append(("value", (_s - 2) // 2))
    if _s - 1 < MH:
        MATT += [("turn", 2 * (_s - 1)), ("turn", 2 * (_s - 1) + 1)]
LOADED = ([("key", _n) for _n in range(8)] + [("value", _n) for _n in range(4)]
          + [("key", _n) for _n in range(8, 16)] + [("value", _n) for _n in range(4, 8)]
          + [("query", _n) for _n in range(8)])
HEAD = []
_norms = [("key_mean", _n) for _n in range(MH)]
for _n, _x in enumerate(LOADED):
    HEAD.append(_x)
    if _n >= 2 and (_n % 2 == 0 or _n >= 24) and _norms:
        HEAD.append(_norms.pop(0))
    elif _n >= 24:
        HEAD.append(("query_mean", _n - 29))
HEAD = [_x for _x in HEAD if _x[0] != "query_mean"]
HEAD += _norms
for _n in range(9):
    if _n < 8:
        HEAD.append(("query_mean", _n))
    if _n >= 1:
        HEAD.append(("query_turn", _n - 1))
SQUARE = {_x: _n for _n, _x in enumerate([("key", _n) for _n in range(MH)] + [("query", _n) for _n in range(8)])}


def layer0(s):
    return ([(f"mixnorm_{s}", 0, 1), (f"conv_in_{s}", 12, 12), (f"conv_out_{s}", 4, 4)]
            + [(f"ffnnorm_{s}", 0, 1), (f"up_{s}", 22, 22), (f"down_{s}", 11, 4)])


STAGES = ([("vectors", 0, 2), ("turn_x", 0, 4), ("turn_ctx", 0, 4), ("norm1", 0, 1), ("qkv", 12, 12),
           ("gates", 8, 8), ("attention", MODS, len(ATT)), ("out_moba", 2, 4), ("out_sb", 2, 4), ("mix", 4, 4),
           ("norm2", 0, 1), ("peer_q", 8, 8), ("turn_keys", 0, 4), ("peer_scores", 0, 8),
           ("turn_x2", 0, 4), ("mod1", MODS, MODS), ("turn_chosen", 0, 1)]
          + layer0("ctx") + [("norm_final", 0, 1)] + layer0("lat")
          + [("mixnorm1_ctx", 0, 1), ("mixnorm1_lat", 0, 1), ("mla_in", 5, 6), ("qlat_norm", 0, 1),
             ("kvlat_norm", 0, 1), ("kpe_norm", 0, 1), ("kpe_turn", 0, 1), ("heads", 10, len(HEAD)),
             ("mla_attention", 0, len(MATT)), ("mla_out", 4, 4), ("ffnnorm1", 0, 1), ("up_1", 22, 22),
             ("down_1", 11, 4), ("turn_out", 0, 4)])
CHUNK = firsts([(n, c) for n, c, _ in STAGES])
GROUP = firsts([(n, g) for n, _, g in STAGES])

TURNS = [(0, 3, "conv_in", 0), (3, 1, "conv", 0), (4, 1, "conv_out", 0), (5, 1, "norm", 0), (6, 2, "up", 0),
         (8, 3, "up", 8), (11, 1, "up", 20), (12, 1, "down", 0), (13, 2, "down", 1), (15, 1, "down", 9)]
SCORED = [6, 5, 5, 0]

VROWS = firsts([("norm1", 8), ("norm2", 8), ("final", 8), ("mix", 16), ("ffn", 16), ("conv_k", 24),
                ("conv_b", 8), ("q_lat", 6), ("kv_lat", 2), ("c", 8), ("c_ctx", 8), ("qn", 1), ("kn", 1),
                ("end", 0)])

CCOLS = firsts([("ident", 128), ("ones", 256), ("mean", 128), ("turn", 128), ("cos", T), ("sin", T),
                ("iota", 16), ("row", 32), ("eps", 1), ("end", 0),
                ("dist", 2 * T), ("strict", 2 * T), ("all", 0)])


def constants():
    c = np.zeros((P, CCOLS["all"]), np.float32)

    def put(name, a):
        c[:a.shape[0], CCOLS[name]:CCOLS[name] + a.shape[1]] = a

    put("ident", np.eye(P))
    put("ones", np.ones((P, 256)))
    mean = np.zeros((QH, QH))
    mean[:NOPE, :NOPE] = 1.0 / NOPE
    mean[NOPE:, NOPE:] = 1.0 / ROPE
    put("mean", mean)
    axis, half = ROPE // 2, ROPE // 4
    turn = np.zeros((QH, QH))
    for a in range(2):
        for j in range(half):
            lo = NOPE + a * axis + j
            turn[lo, lo + half] = -1.0
            turn[lo + half, lo] = 1.0
    put("turn", turn.T)
    inv = np.float32(10000.0) ** (-np.arange(0, axis, 2, dtype=np.float32) / np.float32(axis))
    t = np.arange(T)
    ang = np.concatenate([(t // 64).astype(np.float32)[:, None] * inv] * 2
                         + [(t % 64).astype(np.float32)[:, None] * inv] * 2, axis=1)
    cos, sin = np.ones((QH, T)), np.zeros((QH, T))
    cos[NOPE:], sin[NOPE:] = np.cos(ang).T, np.sin(ang).T
    put("cos", cos)
    put("sin", sin)
    s = np.arange(T)[None, :]
    for tile in range(2):
        q = (tile * P + np.arange(P))[:, None]
        c[:, CCOLS["dist"] + tile * T:CCOLS["dist"] + (tile + 1) * T] = np.where(s <= q, q - s, BIG)
        c[:, CCOLS["strict"] + tile * T:CCOLS["strict"] + (tile + 1) * T] = np.where(s < q, 0.0, -BIG)
    c[:, CCOLS["iota"]:CCOLS["iota"] + 16] = np.arange(16)
    put("row", (np.arange(96)[:, None] % 32 == np.arange(32)[None, :]).astype(np.float32))
    c[:, CCOLS["eps"]] = EPS
    return c


def program(nc, w, consts_dram, out_dram):
    with ExitStack() as ctx:
        def sb(name, shape, dt=F32):
            return ctx.enter_context(nc.sbuf_tensor(name, shape, dt))

        def sem(name):
            return ctx.enter_context(nc.semaphore(name))

        bank = [ctx.enter_context(nc.psum_tensor(f"bank{b}", [P, 512], F32)) for b in range(BANKS)]
        wide = [ctx.enter_context(nc.psum_tensor(f"wide{b}", [P, 1024], F32)) for b in range(2)]
        sbank = [wide[b // 2][:, 512 * (b % 2):512 * (b % 2) + 512] for b in range(4)]

        ring = [sb(f"weights{s}", [P, SLOT]) for s in range(SLOTS)]
        consts = sb("consts", [P, CCOLS["end"]])
        vec = sb("vec", [P, VROWS["end"]])
        cvec = sb("cvec", [P, KD, 2])
        modb = sb("modb", [P, 96])
        mod = sb("mod", [P, 2, 48, 2])
        gmod = sb("gmod", [P, 2, 2, KD, 2])
        h_lat = sb("h_lat", [P, KD, T])
        h_ctx = sb("h_ctx", [P, KD, T])
        nrm = sb("nrm", [P, KD, 2 * T])
        sq = sb("sq", [P, KD, T])
        std = sb("std", [P, 2, 2 * T])
        rstd = sb("rstd", [P, 2, 2 * T])
        idx_t = sb("idx_t", [P, T], U32)
        gate_t = sb("gate_t", [P, T])
        idx8 = sb("idx8", [P, 2, 8], U32)
        halves = sb("halves", [P, 2, 16])
        dots = sb("dots", [P, 16])
        gelus = sb("gelus", [P, 16])
        wts = sb("wts", [P, 16 * 16])
        rows16 = sb("rows16", [16, D])
        big = sb("big", [P, 10368])
        more = sb("more", [P, 18432])

        def view(a, at, *dims, dt=None):
            n = int(np.prod(dims))
            if dt is BF16:
                v = a[:, at:at + n // 2].bitcast(BF16)
            elif dt is U32:
                v = a[:, at:at + n].bitcast(U32)
            else:
                v = a[:, at:at + n]
            names = "abcd"[:len(dims)]
            return v.rearrange(f"p ({' '.join(names)}) -> p {' '.join(names)}",
                               **{x: d for x, d in zip(names, dims)})

        qk = view(big, 0, 16, T)
        gate = view(big, 4096, 16, T)
        vtok = view(big, 8192, 2, 1024)
        logit = view(more, 0, 3, 2, T)
        prob = view(more, 1536, 3, 2, T)
        expo = view(more, 3072, 3, 2, T)
        soft = view(more, 4608, 3, 2, T)
        prob_t = view(more, 6144, 2, 2, T)
        o_t = view(more, 7168, 8, T)
        small = view(more, 9216, 16, 8)
        x_tok = view(more, 9472, 2, D)
        ctx_tok = view(more, 11520, 2, D)
        masks = view(more, 13824, 4 * T)
        vrows = view(more, 13568, P)
        brows = view(more, 13696, P)
        pq = view(big, 0, 16, T)
        keys_t = view(big, 4096, 16, P)
        keys = view(big, 6144, 16, P)
        x2_tok = view(big, 8320, 2, D)
        score = view(more, 0, 2, 16, P)
        top = view(more, 4096, 2, 16, TOPK)
        top_i = view(more, 4608, 2, 16, TOPK, dt=U32)
        top_f = view(more, 5120, 2, 16, TOPK)
        cand = view(more, 5632, 8, 256)
        eq = view(more, 7680, P, TOPK)
        best = view(more, 9728, 2, PH, TOPK)
        pos = view(more, 9984, P, dt=U32)
        part = view(more, 10112, 2, P, dt=U32)
        part_f = view(more, 10368, 2, P)
        pick = view(more, 10624, 2, P)
        chosen = view(more, 10880, 2, P)
        shifted = view(more, 11136, 2, PH, TOPK)
        sums = view(more, 11392, 2, 2, PH)
        split = [view(big, 1024 * j, 2, D, dt=BF16) for j in range(3)]
        rest = view(big, 3072, 2, D)
        ubuf = [view(more, 1024 * j, D) for j in range(4)]
        vbuf = [view(more, 4096 + 1024 * j, D) for j in range(8)]
        xs = view(more, 12288, 8, D, dt=BF16)[0:96]
        sel = view(more, 16384, 32, P, dt=BF16)[0:96]
        peer = nrm[:, :, T:2 * T]
        mrow = rows16[0:2, :].rearrange("p (j n) -> p j n", j=4)
        cproj = view(big, 0, 24, T)
        z = view(big, 6144, KD, T + 2)
        hid = view(big, 0, KH, T)
        qlat = view(big, 0, 6, T)
        kvlat = view(big, 1536, 2, 2 * T)
        q = view(big, 2560, MH, T)
        msmall = view(big, 6656, 16, 8)
        kpe = view(big, 6784, 512)
        kcat = view(more, 0, MH, 2 * T)
        vmla = view(more, 8192, 4, MH * MV)
        o_mla = view(more, 12288, KD, T)
        squares = view(more, 12288, 12, 2 * T)
        mprob = view(more, 14336, 2, 2, 2 * T)
        mprob_t = view(more, 16384, 2, 4, T)
        out_tok = view(big, 0, 2, D)

        ident = consts[:, CCOLS["ident"]:CCOLS["ident"] + P]
        ones = consts[:, CCOLS["ones"]:CCOLS["ones"] + 256]
        mean = consts[:, CCOLS["mean"]:CCOLS["mean"] + P]
        turn = consts[:, CCOLS["turn"]:CCOLS["turn"] + P]
        cos = consts[:, CCOLS["cos"]:CCOLS["cos"] + T]
        sin = consts[:, CCOLS["sin"]:CCOLS["sin"] + T]
        dist = masks[:, 0:2 * T].rearrange("p (a t) -> p a t", a=2)
        strict = masks[:, 2 * T:4 * T].rearrange("p (a t) -> p a t", a=2)
        iota = consts[:, CCOLS["iota"]:CCOLS["iota"] + 16]
        row32 = consts[0:96, CCOLS["row"]:CCOLS["row"] + 32]
        eps = consts[:, CCOLS["eps"]:CCOLS["eps"] + 1]

        def vcol(name, k):
            return vec[:, VROWS[name] + k:VROWS[name] + k + 1]

        s_start = sem("constants_and_tokens_landed")
        s_keys = sem("keys_landed")
        w_landed = [sem(f"weights_landed{s}") for s in range(SLOTS)]
        w_free = [sem(f"weights_free{s}") for s in range(SLOTS)]
        full = [sem(f"bank_full{b}") for b in range(BANKS)]
        free = [sem(f"bank_free{b}") for b in range(BANKS)]
        sc_full = [sem(f"scores_full{b}") for b in range(4)]
        sc_free = [sem(f"scores_free{b}") for b in range(4)]
        s_step = sem("vector_step")
        a_step = sem("scalar_step")
        s_sq = sem("squares_ready")
        s_norm = sem("norm_ready")
        s_soft_in = sem("softmax_in_ready")
        s_soft_exp = sem("softmax_exp_done")
        s_arg = sem("stick_argument_ready")
        s_mod = sem("modulation_turned")
        s_vo = sem("token_rows_copied")
        vo_full = sem("token_rows_turned")
        s_prob_v = sem("probs_ready_by_vector")
        s_prob_s = sem("probs_ready_by_scalar")
        s_mixed = sem("mixed_ready")
        s_shift = sem("peer_shifted_ready")
        s_pexp = sem("peer_exp_done")
        s_chosen = sem("chosen_ready")
        s_index = sem("indices_ready")
        s_split = sem("split_ready")
        s_xs = sem("split_landed")
        s_idx8 = sem("indices_staged")
        s_turn = sem("gather_may_start")
        u_landed = [sem(f"u_landed{j}") for j in range(4)]
        v_landed = [sem(f"v_landed{j}") for j in range(8)]
        v_free = [sem(f"v_free{j}") for j in range(8)]
        xb_full = [sem(f"x_broadcast_full{j}") for j in range(2)]
        xb_free = [sem(f"x_broadcast_free{j}") for j in range(2)]
        s_dots = sem("dots_ready")
        s_gelu = sem("gelus_ready")
        s_wts = sem("expert_weights_ready")
        vo_free = sem("peer_out_free")
        s_conv = sem("conv_ready")
        s_cvec = sem("conditioning_ready")
        s_kpe = sem("kpe_ready")
        s_kn = sem("k_normed")
        s_qn = sem("q_normed")
        s_qr = sem("q_rotated")
        s_kcat = sem("kpe_spread")
        s_out = sem("out_stored")

        def steps(eng, first, count, size=4):
            runs = count // size
            if runs >= 2:
                with eng.Fori(0, runs) as i:
                    for s in range(size):
                        yield i * size + (first + s), first + s, i
            else:
                runs = 0
            for s in range(runs * size, count):
                yield first + s, first + s, 0

        def slot_of(stage, s):
            return (CHUNK[stage] + s) % SLOTS

        def bank_of(stage, s):
            return (GROUP[stage] + s) % BANKS

        def wait_weights(eng, stage, s, i=0):
            c = CHUNK[stage] + s
            eng.wait_ge(w_landed[c % SLOTS], i * 16 + 16 * (c // SLOTS + 1))

        def wait_slot(eng, stage, s, i=0):
            c = CHUNK[stage] + s
            eng.wait_ge(w_free[c % SLOTS], i + (c // SLOTS + 1))

        def wait_full(eng, stage, s, i=0):
            g = GROUP[stage] + s
            eng.wait_ge(full[g % BANKS], i + (g // BANKS + 1))

        def wait_free(eng, stage, s, i=0):
            g = GROUP[stage] + s
            eng.wait_ge(free[g % BANKS], i + (g // BANKS + 1))

        def wait_emptied(eng, stage, s, i=0):
            g = GROUP[stage] + s
            eng.wait_ge(free[g % BANKS], i + (g // BANKS + 2))

        def wait_all_emptied(eng, stage, n):
            for s in range(max(0, n - BANKS), n):
                wait_emptied(eng, stage, s)

        def at(a, n, lo, size):
            if isinstance(n, int):
                return a[:, n, lo:lo + size]
            return a[:, bass.ds(n, 1), lo:lo + size].rearrange("p a n -> p (a n)")

        def some(a, n, size):
            return a[:, n:n + size] if isinstance(n, int) else a[:, bass.ds(n, size)]

        def some2(a, n, size):
            return a[:, :, n:n + size] if isinstance(n, int) else a[:, :, bass.ds(n, size)]

        def turns_of(eng):
            for start, count, kind, first in TURNS:
                if count > 1:
                    with eng.Fori(0, count) as i:
                        yield i + start, i, start // 8, kind, first
                else:
                    yield start, 0, start // 8, kind, first

        block = ctx.enter_context(nc.Block())

        @block.sync
        def _(sp):
            def load(stage, s, i, src, shape):
                wait_slot(sp, stage, s, i)
                b = slot_of(stage, s)
                n = shape[0] * shape[1]
                sp.dma_start(ring[b][:, 0:n].rearrange("p (k n) -> p k n", k=shape[0]), src)\
                    .then_inc(w_landed[b], 16)

            def load_wide(stage, m, n, kt=KD, cols=WIDE, first=0):
                mv = m.rearrange("(k p) n -> p k n", p=P)
                for j, s, i in steps(sp, 0, n):
                    load(stage, s, i, mv[:, :, bass.ds(j * cols + first, cols)], (kt, cols))

            def load_deep(stage, m, n):
                mv = m.rearrange("(k p) n -> p k n", p=P)
                load(stage, 0, 0, mv[:, 0:2, :], (2, D))
                for j, s, i in steps(sp, 1, n - 2):
                    load(stage, s, i, mv[:, bass.ds(j * 2, 2), :], (2, D))
                load(stage, n - 1, 0, mv[:, 2 * n - 2:2 * n, :], (2, D))

            def load_ffn(up, down, layer):
                gv = w["ffn_w_gate_2"][layer].rearrange("(k p) n -> p k n", p=P)
                uv = w["ffn_w_up_2"][layer].rearrange("(k p) n -> p k n", p=P)
                for j, s, i in steps(sp, 0, 11, 2):
                    load(up, 2 * s, i, gv[:, :, bass.ds(j * WIDE, WIDE)], (KD, WIDE))
                    load(up, 2 * s + 1, i, uv[:, :, bass.ds(j * WIDE, WIDE)], (KD, WIDE))
                load_deep(down, w["ffn_w_down_2"][layer], 11)

            def load_layer0(s):
                load_wide(f"conv_in_{s}", w["conv_w_in_2"][0], 12)
                load_wide(f"conv_out_{s}", w["conv_w_out_2"][0], 4)
                load_ffn(f"up_{s}", f"down_{s}", 0)

            for b in range(SLOTS - 1):
                sp.sem_inc(w_free[b], 1)

            def start(dst, src):
                sp.dma_start(dst, src).then_inc(s_start, 16)

            start(consts[:, :], consts_dram[:, 0:CCOLS["end"]])
            start(masks, consts_dram[:, CCOLS["end"]:CCOLS["all"]])
            start(x_tok, w["x"][0].rearrange("(a p) d -> p a d", p=P))
            for name, key, rows in (("norm1", "norm1_g", 8), ("norm2", "norm2_g", 8), ("mix", "norm_mix_g_2", 16),
                                    ("ffn", "norm_ffn_g_2", 16), ("q_lat", "mla_q_norm_g_2", 6),
                                    ("kv_lat", "mla_kv_norm_g_2", 2), ("conv_b", "conv_b_2", 8),
                                    ("c", "c_2", 8)):
                a = VROWS[name]
                start(vrows[a:a + rows, :], w[key].rearrange("l (k p) -> (l k) p", p=P))
            for name, key in (("final", "final_norm_g"), ("c_ctx", "c_ctx_2")):
                start(vrows[VROWS[name]:VROWS[name] + 8, :], w[key].rearrange("(k p) -> k p", p=P))
            start(vrows[VROWS["conv_k"]:VROWS["conv_k"] + 24, :],
                  w["conv_k_2"][0].rearrange("j (k p) -> (j k) p", p=P))
            start(brows[0:96, :], w["mod_b_2"].rearrange("l (k p) -> (l k) p", p=P))
            for name, a, b in (("qn", "mla_qn_nope_g_2", "mla_qn_rope_g_2"), ("kn", "mla_kn_nope_g_2", "mla_kn_rope_g_2")):
                r = VROWS[name]
                start(vrows[r:r + 1, 0:NOPE], w[a])
                start(vrows[r:r + 1, NOPE:QH], w[b])
                start(vrows[r:r + 1, QH:P], w[b])
            start(ctx_tok, w["ctx_2"][0].rearrange("(a p) d -> p a d", p=P))

            wi = w["w_in"][0].rearrange("(k p) n -> p k n", p=P)
            for s in range(12):
                load("qkv", s, 0, wi[:, :, s * WIDE:(s + 1) * WIDE], (KD, WIDE))
            load_wide("gates", w["w_in"][0], 8, first=12 * WIDE)
            load_wide("attention", w["mod_w_2"][0], MODS)
            for stage, key in (("out_moba", "w_out_moba"), ("out_sb", "w_out_sb")):
                mv = w[key][0].rearrange("(k p) n -> p k n", p=P)
                for s in range(2):
                    load(stage, s, 0, mv[:, :, s * 512:(s + 1) * 512], (4, 512))
            load_wide("mix", w["w_mix_out"][0], 4)
            load_wide("peer_q", w["peer_w_q"][0], 8)
            sp.wait_ge(s_mixed, 1)
            sp.dma_start(keys, w["peer_sub_keys"][0].rearrange("h b n c -> n (h b) c")).then_inc(s_keys, 16)
            load_wide("mod1", w["mod_w_2"][1], MODS)
            load_layer0("ctx")
            load_layer0("lat")
            load_wide("mla_in", w["mla_w_in_2"][0], 4)
            mv = w["mla_w_in_2"][0].rearrange("(k p) n -> p k n", p=P)
            load("mla_in", 4, 0, mv[:, :, QLAT + KVLAT:QLAT + KVLAT + ROPE], (KD, ROPE))
            mv = w["mla_w_kv_up_2"][0].rearrange("(k p) n -> p k n", p=P)
            for s in range(2):
                load("heads", s, 0, mv[:, :, 1024 * s:1024 * s + 1024], (2, 1024))
            mv = w["mla_w_q_up_2"][0].rearrange("(k p) n -> p k n", p=P)
            for s in range(8):
                load("heads", 2 + s, 0, mv[:, :, 2 * QH * s:2 * QH * (s + 1)], (6, 2 * QH))
            load_wide("mla_out", w["mla_w_out_2"][0], 4)
            load_ffn("up_1", "down_1", 1)
            wait_all_emptied(sp, "turn_out", 4)
            sp.dma_start(out_dram[0].rearrange("(a p) d -> p a d", p=P), out_tok).then_inc(s_out, 16)
            sp.wait_ge(s_out, 16)

        N_START = 16 * 22

        @block.gpsimd
        def _(pool):
            pool.wait_ge(s_split, 3)
            for n in range(16):
                for j in range(3):
                    lo = 32 * j + 16 * (n // 8)
                    nc.gpsimd.dma_start(xs[lo:lo + 16, n % 8, :], split[j][16 * (n % 8):16 * (n % 8) + 16, n // 8, :])\
                        .then_inc(s_xs, 16)
            pool.wait_ge(s_index, 3)
            pool.wait_ge(s_xs, 16 * 48)
            def stage_indices(half, it, done):
                for j in range(8):
                    pool.wait_ge(v_free[j], done)
                pool.sem_inc(s_turn, 1)
                nc.gpsimd.tensor_copy(idx8[:, half, :], idx_t[:, bass.ds(it * 16 + 8 * half, 8)]).then_inc(s_idx8, 1)
                pool.wait_ge(s_idx8, it * 2 + half + 1)
                pool.sem_inc(s_turn, 1)

            def fetch(table, s, dst, landed):
                at = bass.IndirectOffsetOnAxis(ap=idx8[:, s // 8, s % 8:s % 8 + 1], axis=0)
                nc.gpsimd.indirect_dma_start(out=dst, out_offset=None, in_=w[table][0], in_offset=at)\
                    .then_inc(landed, 16)

            def fetch_u(s, it):
                pool.wait_ge(xb_free[1], it * 16 + s + 1)
                pool.sem_inc(s_turn, 1)
                fetch("peer_u", s, ubuf[s % 4], u_landed[s % 4])

            def fetch_v(s, it):
                pool.wait_ge(v_free[s % 8], it * 2 + s // 8 + 2)
                pool.sem_inc(s_turn, 1)
                fetch("peer_v", s, vbuf[s % 8], v_landed[s % 8])

            def turn_of(it, last):
                for s in range(16):
                    if s == 4:
                        stage_indices(1, it, it * 2 + 2)
                    if s == 12 and not last:
                        stage_indices(0, it + 1, it * 2 + 3)
                    fetch_v(s, it)
                    if s < 12:
                        fetch_u(s + 4, it)
                    elif not last:
                        fetch_u(s - 12, it + 1)

            stage_indices(0, 0, 1)
            for s in range(4):
                fetch_u(s, 0)
            with pool.Fori(0, 15) as it:
                turn_of(it, False)
            turn_of(15, True)
            pool.wait_ge(s_kpe, 1)
            nc.gpsimd.tensor_copy(kcat[NOPE:QH], kpe[NOPE:QH, :].unsqueeze(1).to_broadcast([ROPE, MH, 2 * T]))\
                .then_inc(s_kcat, 1)

        @block.tensor
        def _(pe):
            for j in range(8):
                pe.sem_inc(v_free[j], 2)

            def product(stage, rhs, kt, i, s, cols=WIDE, width=T, group=None, first=0):
                wt = ring[slot_of(stage, s)][:, 0:kt * cols].rearrange("p (k n) -> p k n", k=kt)
                g = s if group is None else group
                wait_weights(pe, stage, s, i)
                wait_free(pe, stage, g, i)
                b = bank[bank_of(stage, g)]
                for m in range(cols // P):
                    for k in range(kt):
                        mm = nc.tensor.matmul(b[:, m * width:(m + 1) * width], wt[:, k, m * P:(m + 1) * P],
                                              rhs(k), start=(k == 0), stop=(k == kt - 1))
                        if m == k == 0:
                            opens(stage, s, mm)
                mm.then_inc(full[bank_of(stage, g)], 1)

            def opens(stage, s, mm):
                mm.then_inc(w_free[(CHUNK[stage] + s - 1) % SLOTS], 1)

            def products(stage, rhs, n, kt=KD):
                for j, s, i in steps(pe, 0, n):
                    product(stage, rhs, kt, i, s)

            def turns(stage, g, pieces):
                wait_free(pe, stage, g)
                b = bank[bank_of(stage, g)]
                for col, src in pieces:
                    n, m = src.shape[0], src.shape[1]
                    mm = nc.tensor.transpose(b[0:m, col:col + n], src, ident[0:n, 0:n])
                mm.then_inc(full[bank_of(stage, g)], 1)

            def norm(r, stage, kt=KD, width=T, src=None):
                pe.wait_ge(s_sq, r + 1)
                wait_free(pe, stage, 0)
                b = bank[bank_of(stage, 0)]
                for k in range(kt):
                    mm = nc.tensor.matmul(b[:, 0:width], ones[:, 0:P], sq[:, k, 0:T] if src is None else src(k),
                                          start=(k == 0), stop=(k == kt - 1))
                mm.then_inc(full[bank_of(stage, 0)], 1)

            def down_opens(stage):
                for g in range(4):
                    wait_free(pe, stage, g)

            def down_chunk(stage, j, s, i, first, last):
                wait_weights(pe, stage, s, i)
                wt = ring[slot_of(stage, s)].rearrange("p (k n) -> p k n", k=2)
                for k in range(2):
                    for m in range(KD):
                        b = bank_of(stage, m // 2)
                        mm = nc.tensor.matmul(
                            bank[b][:, (m % 2) * T:(m % 2) * T + T], wt[:, k, m * P:(m + 1) * P],
                            at(hid, j * 2 + k, 0, T),
                            start=(first and k == 0 and m % 2 == 0), stop=(last and k == 1),
                            skip_group_check=True)
                        if m == k == 0:
                            opens(stage, s, mm)
                        if last and k == 1 and m % 2 == 1:
                            mm.then_inc(full[b], 1)

            def down(stage):
                down_opens(stage)
                down_chunk(stage, 0, 0, 0, True, False)
                for j, s, i in steps(pe, 1, 9):
                    down_chunk(stage, j, s, i, False, False)
                down_chunk(stage, 10, 10, 0, False, True)

            def ffn(up, dn, x, r):
                pe.wait_ge(s_norm, r + 1)
                for j, s, i in steps(pe, 0, 11, 2):
                    for half in range(2):
                        product(up, x, KD, i, 2 * s + half)
                wait_all_emptied(pe, up, 22)
                down(dn)

            def mod_chunk(stage, s, i=0, group=None):
                g = s if group is None else group
                wait_weights(pe, stage, s, i)
                wait_free(pe, stage, g, i)
                wt = ring[slot_of(stage, s)].rearrange("p (k n) -> p k n", k=KD)
                for k in range(KD):
                    mm = nc.tensor.matmul(bank[bank_of(stage, g)][0:2, 0:WIDE], cvec[:, k, :], wt[:, k, :],
                                          start=(k == 0), stop=(k == KD - 1))
                    if k == 0:
                        opens(stage, s, mm)
                mm.then_inc(full[bank_of(stage, g)], 1)

            def mod_turn(stage, s, layer, j, i=0, group=None):
                wait_emptied(pe, stage, s if group is None else group, i)
                for m in range(2):
                    mm = nc.tensor.matmul(sbank[3][:, bass.ds(j * 4 + 96 * layer + 2 * m, 2)],
                                          mrow[:, s % 4, m * P:(m + 1) * P], ident[0:2, 0:2], start=True, stop=True)
                mm.then_inc(s_mod, 1)

            def layer0(name, r, x, n):
                norm(r, f"mixnorm_{name}")
                pe.wait_ge(s_norm, r + 1)
                products(f"conv_in_{name}", x, 12)
                pe.wait_ge(s_conv, n + 1)
                products(f"conv_out_{name}", lambda k: cproj[:, k, :], 4)
                norm(r + 1, f"ffnnorm_{name}")
                ffn(f"up_{name}", f"down_{name}", x, r + 1)

            def lat(k):
                return nrm[:, k, T:2 * T]

            def con(k):
                return nrm[:, k, 0:T]

            pe.wait_ge(s_start, N_START)
            turns("vectors", 0, [(0, vrows[0:VROWS["end"], :])])
            turns("vectors", 1, [(0, brows[0:96, :])])
            for stage, src in (("turn_x", x_tok), ("turn_ctx", ctx_tok)):
                for g in range(4):
                    turns(stage, g, [(256 * a + 128 * t, src[:, t, (2 * g + a) * P:(2 * g + a + 1) * P])
                                     for a in range(2) for t in range(2)])

            norm(0, "norm1")
            pe.wait_ge(s_norm, 1)
            for s in range(12):
                if s % 6 < 4:
                    product("qkv", lat, KD, 0, s)
                else:
                    wait_weights(pe, "qkv", s)
                    wait_free(pe, "qkv", s)
                    wt = ring[slot_of("qkv", s)].rearrange("p (k n) -> p k n", k=KD)
                    for t in range(2):
                        for k in range(KD):
                            mm = nc.tensor.matmul(bank[bank_of("qkv", s)][:, t * WIDE:(t + 1) * WIDE],
                                                  nrm[:, k, T + t * P:T + (t + 1) * P], wt[:, k, :],
                                                  start=(k == 0), stop=(k == KD - 1))
                            if t == k == 0:
                                opens("qkv", s, mm)
                    mm.then_inc(full[bank_of("qkv", s)], 1)
            products("gates", lat, 8)

            wait_all_emptied(pe, "qkv", 12)
            pe.wait_ge(s_cvec, 2)
            for s in range(HALVES + 3):
                if s < HALVES:
                    b, kind, h = s % 3, s // HEADS, s % HEADS
                    pe.wait_ge(sc_free[b], s // 3 + 1)
                    lo = DH * (h % 2)
                    for t in range(2):
                        mm = nc.tensor.matmul(sbank[b][:, t * T:(t + 1) * T],
                                              qk[lo:lo + DH, 8 * kind + h // 2, t * P:(t + 1) * P],
                                              qk[lo:lo + DH, 8 * kind + 4 + h // 2, :], start=True, stop=True)
                    mm.then_inc(sc_full[b], 1)
                for j in MOD_STEP[s]:
                    mod_chunk("attention", j, group=ATT.index(("mod", j)))
                    if j:
                        mod_turn("attention", j - 1, 0, j - 1, group=ATT.index(("mod", j - 1)))
                if 2 <= s < HALVES + 2:
                    n = s - 2
                    if n < HEADS:
                        pe.wait_ge(s_prob_v, n + 1)
                    else:
                        pe.wait_ge(s_prob_s, n - HEADS + 1)
                    turns("attention", ATT.index(("turn", n)),
                          [(256 * a + 128 * t, prob[:, n % 3, t, a * P:(a + 1) * P])
                           for a in range(2) for t in range(2)])
                if s >= 3:
                    n = s - 3
                    kind, h = n // HEADS, n % HEADS
                    g = ATT.index(("value", n // 2))
                    b = bank[bank_of("attention", g)]
                    wait_emptied(pe, "attention", ATT.index(("turn", n)))
                    if n % 2 == 0:
                        wait_free(pe, "attention", g)
                    lo = DH * (n % 2)
                    for a in range(2):
                        mm = nc.tensor.matmul(b[lo:lo + DH, 0:T], vtok[:, a, 512 * kind + DH * h:512 * kind + DH * h + DH],
                                              prob_t[:, n % 2, a, :], start=(a == 0), stop=(a == 1))
                    if n % 2 == 1:
                        mm.then_inc(full[bank_of("attention", g)], 1)

            mod_turn("attention", MODS - 1, 0, MODS - 1, group=ATT.index(("mod", MODS - 1)))
            wait_all_emptied(pe, "attention", len(ATT))
            for n, stage in enumerate(("out_moba", "out_sb")):
                for s in range(2):
                    wt = ring[slot_of(stage, s)].rearrange("p (k n) -> p k n", k=4)
                    wait_weights(pe, stage, s)
                    for g in range(2 * s, 2 * s + 2):
                        wait_free(pe, stage, g)
                        for m in range(2):
                            col = (g % 2) * 256 + m * P
                            for k in range(4):
                                mm = nc.tensor.matmul(bank[bank_of(stage, g)][:, m * T:(m + 1) * T],
                                                      wt[:, k, col:col + P], o_t[:, 4 * n + k, :],
                                                      start=(k == 0), stop=(k == 3))
                                if g == 2 * s and m == k == 0:
                                    opens(stage, s, mm)
                        mm.then_inc(full[bank_of(stage, g)], 1)
            pe.wait_ge(s_mixed, 1)
            products("mix", lambda k: gate[:, k, :], 4)

            norm(1, "norm2")
            pe.wait_ge(s_norm, 2)
            products("peer_q", lat, 8)
            pe.wait_ge(s_keys, 16)
            for g in range(4):
                turns("turn_keys", g, [(P * a, keys[:, 4 * g + a, :]) for a in range(4)])
            wait_all_emptied(pe, "peer_q", 8)
            wait_all_emptied(pe, "turn_keys", 4)
            for g in range(8):
                t, n = g // 4, g % 4
                wait_free(pe, "peer_scores", g)
                for a in range(4):
                    mm = nc.tensor.matmul(bank[bank_of("peer_scores", g)][:, a * P:(a + 1) * P],
                                          pq[:, 4 * n + a, t * P:(t + 1) * P], keys_t[:, 4 * n + a, :],
                                          start=True, stop=True)
                mm.then_inc(full[bank_of("peer_scores", g)], 1)
            for g in range(4):
                turns("turn_x2", g, [(P * a, lat(4 * (g % 2) + a)[:, (g // 2) * P:(g // 2) * P + P]) for a in range(4)])

            for j, s, i in steps(pe, 0, MODS):
                mod_chunk("mod1", s, i)
                if s % 4:
                    mod_turn("mod1", s - 1, 1, j - 1, i)
                if s % 4 == 3:
                    mod_turn("mod1", s, 1, j, i)

            pe.wait_ge(s_chosen, 1)
            turns("turn_chosen", 0, [(P * t, chosen[:, t, :]) for t in range(2)]
                  + [(256 + P * t, shifted[:, t].rearrange("p h k -> p (h k)")) for t in range(2)])
            pe.wait_ge(s_xs, 16 * 48)
            norm(2, "mixnorm_ctx")

            vo = wide[1]

            def gather(it, i, half, kind, first):
                def spread(s):
                    for c in range(2):
                        pe.wait_ge(xb_free[c], it * 16 + s + (1 if c == 0 else 4))
                        nc.tensor.matmul(sbank[c], sel[:, 16 * half + s, :],
                                         at(xs, it - 8 * half, 512 * c, 512), start=True, stop=True)\
                            .then_inc(xb_full[c], 1)

                def experts(s):
                    if s == 0:
                        pe.wait_ge(vo_free, it + 1)
                    if s % 4 == 0:
                        pe.wait_ge(s_wts, it * 4 + s // 4 + 1)
                    pe.wait_ge(v_landed[s % 8], (it * 2 + s // 8 + 1) * 16)
                    for c in range(2):
                        mm = nc.tensor.matmul(vo[0:16, 512 * c:512 * c + 512], wts[:, 16 * s:16 * s + 16],
                                              vbuf[s % 8][:, 512 * c:512 * c + 512],
                                              start=(s == 0), stop=(s == 15))
                    mm.then_inc(v_free[s % 8], 1)

                def both(quad):
                    for s in range(4 * quad, 4 * quad + 4):
                        spread(s)
                        experts(s - 4)

                def extra(k):
                    s = first + k
                    if kind == "conv_in":
                        product("conv_in_ctx", con, KD, i, s)
                    if kind == "conv_out":
                        if k == 0:
                            pe.wait_ge(s_conv, 1)
                        product("conv_out_ctx", lambda n: cproj[:, n, :], KD, 0, s)
                    if kind == "norm" and k == 0:
                        norm(3, "ffnnorm_ctx")
                    if kind == "up" and s < 22:
                        if s == 0:
                            pe.wait_ge(s_norm, 4)
                        product("up_ctx", con, KD, i, s)
                    if kind == "down" and s < 11 and (s > 0 or k == 0) and (first > 0 or k == 0):
                        if s == 0:
                            wait_all_emptied(pe, "up_ctx", 22)
                            down_opens("down_ctx")
                        down_chunk("down_ctx", i * 4 + s, s, i, s == 0, s == 10)

                for s in range(4):
                    spread(s)
                extra(0)
                both(1)
                extra(1)
                both(2)
                both(3)
                extra(2)
                for s in range(12, 16):
                    experts(s)
                extra(3)
                pe.wait_ge(s_vo, it + 1)
                for m in range(KD):
                    mm = nc.tensor.matmul(vo[:, 16 * m:16 * m + 16], rows16[:, m * P:(m + 1) * P], ident[0:16, 0:16],
                                          start=True, stop=True)
                mm.then_inc(vo_full, 1)

            pe.wait_ge(s_index, 3)
            pe.wait_ge(s_norm, 3)
            for it, i, half, kind, first in turns_of(pe):
                gather(it, i, half, kind, first)
            pe.wait_ge(vo_free, 17)

            norm(4, "norm_final")
            layer0("lat", 5, lat, 1)

            norm(7, "mixnorm1_ctx")
            norm(8, "mixnorm1_lat")
            pe.wait_ge(s_norm, 9)
            for s in range(3):
                product("mla_in", lat, KD, 0, s)
            wait_weights(pe, "mla_in", 3)
            wt = ring[slot_of("mla_in", 3)].rearrange("p (k n) -> p k n", k=KD)
            for m in range(2):
                wait_free(pe, "mla_in", 3 + m)
                for k in range(KD):
                    mm = nc.tensor.matmul(bank[bank_of("mla_in", 3 + m)][:, :], wt[:, k, m * P:(m + 1) * P],
                                          nrm[:, k, :], start=(k == 0), stop=(k == KD - 1))
                    if m == k == 0:
                        opens("mla_in", 3, mm)
                mm.then_inc(full[bank_of("mla_in", 3 + m)], 1)
            wait_weights(pe, "mla_in", 4)
            wait_free(pe, "mla_in", 5)
            wt = ring[slot_of("mla_in", 4)][:, 0:KD * ROPE].rearrange("p (k n) -> p k n", k=KD)
            for k in range(KD):
                mm = nc.tensor.matmul(bank[bank_of("mla_in", 5)][NOPE:QH, :], wt[:, k, :], nrm[:, k, :],
                                      start=(k == 0), stop=(k == KD - 1))
                if k == 0:
                    opens("mla_in", 4, mm)
            mm.then_inc(full[bank_of("mla_in", 5)], 1)

            def square_wide(k):
                return sq[:, 2 * k:2 * k + 2, :].rearrange("p a t -> p (a t)")

            norm(9, "qlat_norm", 6)
            norm(10, "kvlat_norm", 2, 2 * T, square_wide)
            pe.wait_ge(s_sq, 12)
            wait_free(pe, "kpe_norm", 0)
            nc.tensor.matmul(bank[bank_of("kpe_norm", 0)][NOPE:QH, :], mean[NOPE:QH, NOPE:QH],
                             square_wide(0)[NOPE:QH, :], start=True, stop=True)\
                .then_inc(full[bank_of("kpe_norm", 0)], 1)
            pe.wait_ge(s_norm, 12)
            wait_free(pe, "kpe_turn", 0)
            nc.tensor.matmul(bank[bank_of("kpe_turn", 0)][NOPE:QH, 0:T], turn[NOPE:QH, NOPE:QH],
                             kpe[NOPE:QH, T:2 * T], start=True, stop=True)\
                .then_inc(full[bank_of("kpe_turn", 0)], 1)
            for g, (kind, n) in enumerate(HEAD):
                if kind in ("key_mean", "query_mean"):
                    wait_emptied(pe, "heads", HEAD.index((kind.split("_")[0], n)))
                if kind == "query_turn":
                    pe.wait_ge(s_qn, n + 1)
                wait_free(pe, "heads", g)
                b = bank[bank_of("heads", g)]
                if kind in ("key", "value"):
                    s = n // 8 if kind == "key" else n // 4
                    wait_weights(pe, "heads", s)
                    wt = ring[slot_of("heads", s)].rearrange("p (k n) -> p k n", k=2)
                if kind == "key":
                    at_n = P * (n % 8)
                    for k in range(2):
                        mm = nc.tensor.matmul(b[0:NOPE, :], wt[:, k, at_n:at_n + NOPE], kvlat[:, k, :],
                                              start=(k == 0), stop=(k == 1))
                        if n % 8 == k == 0:
                            opens("heads", s, mm)
                if kind == "value":
                    t = n % 4
                    for k in range(2):
                        mm = nc.tensor.matmul(b[:, :], kvlat[:, k, t * P:(t + 1) * P],
                                              wt[:, k, :].rearrange("p (h c) -> p h c", h=8)[:, :, NOPE:P],
                                              start=(k == 0), stop=(k == 1))
                if kind == "query":
                    wait_weights(pe, "heads", 2 + n)
                    wt = ring[slot_of("heads", 2 + n)][:, 0:12 * QH].rearrange("p (k n) -> p k n", k=6)
                    for m in range(2):
                        for k in range(6):
                            mm = nc.tensor.matmul(b[0:QH, m * T:(m + 1) * T], wt[:, k, m * QH:(m + 1) * QH],
                                                  qlat[:, k, :], start=(k == 0), stop=(k == 5))
                            if m == k == 0:
                                opens("heads", 2 + n, mm)
                if kind in ("key_mean", "query_mean"):
                    rows = NOPE if kind == "key_mean" else QH
                    mm = nc.tensor.matmul(b[0:rows, :], mean[0:rows, 0:rows],
                                          squares[0:rows, SQUARE[(kind.split("_")[0], n)] % 12, :],
                                          start=True, stop=True)
                if kind == "query_turn":
                    mm = nc.tensor.matmul(b[0:QH, :], turn[0:QH, 0:QH],
                                          q[0:QH, 2 * n:2 * n + 2, :].rearrange("p a t -> p (a t)"), start=True, stop=True)
                mm.then_inc(full[bank_of("heads", g)], 1)
            pe.wait_ge(s_qr, 8)
            pe.wait_ge(s_kn, MH)
            pe.wait_ge(s_kcat, 1)
            for s in range(MH + 2):
                if s < MH:
                    for t in range(2):
                        n = 2 * s + t
                        pe.wait_ge(sc_free[n % 4], SCORED[n % 4] + n // 4 + 1)
                        nc.tensor.matmul(sbank[n % 4], q[0:QH, s, t * P:(t + 1) * P], kcat[0:QH, s, :],
                                         start=True, stop=True).then_inc(sc_full[n % 4], 1)
                if s >= 2:
                    n = s - 2
                    g = MATT.index(("value", n // 2))
                    b = bank[bank_of("mla_attention", g)]
                    for half in range(2):
                        wait_emptied(pe, "mla_attention", MATT.index(("turn", 2 * n + half)))
                    if n % 2 == 0:
                        wait_free(pe, "mla_attention", g)
                    lo = MV * (n % 2)
                    for a in range(4):
                        mm = nc.tensor.matmul(b[lo:lo + MV, 0:T], vmla[:, a, MV * n:MV * n + MV], mprob_t[:, n % 2, a, :],
                                              start=(a == 0), stop=(a == 3))
                    if n % 2 == 1:
                        mm.then_inc(full[bank_of("mla_attention", g)], 1)
                if 1 <= s <= MH:
                    n = s - 1
                    pe.wait_ge(s_prob_v, HEADS + n + 1)
                    for half in range(2):
                        turns("mla_attention", MATT.index(("turn", 2 * n + half)),
                              [(256 * a + 128 * t, mprob[:, n % 2, t, (2 * half + a) * P:(2 * half + a + 1) * P])
                               for a in range(2) for t in range(2)])
            wait_all_emptied(pe, "mla_attention", len(MATT))
            products("mla_out", lambda k: o_mla[:, k, :], 4)
            norm(12, "ffnnorm1")
            ffn("up_1", "down_1", lat, 12)
            wait_all_emptied(pe, "down_1", 4)
            for g in range(4):
                turns("turn_out", g, [(P * a, h_lat[:, 4 * (g % 2) + a, (g // 2) * P:(g // 2) * P + P]) for a in range(4)])

        @block.scalar
        def _(act):
            for b in range(BANKS):
                act.sem_inc(free[b], 1)
            act.sem_inc(vo_free, 1)

            def leave(stage, g, dst, i=0, cols=slice(0, 512), rows=slice(0, P), func=ACT.Copy, scale=1.0, bias=None):
                wait_full(act, stage, g, i)
                b = bank_of(stage, g)
                src = bank[b][rows, cols]
                if len(dst.shape) == 3:
                    src = src.rearrange("p (a n) -> p a n", a=dst.shape[1])
                more_args = {} if bias is None else {"bias": bias}
                nc.scalar.activation(dst, src, func, scale=scale, **more_args).then_inc(free[b], 1)

            def leaves(stage, n, dst, per=2, **kw):
                for j, s, i in steps(act, 0, n):
                    where = bass.ds(j * per, per) if not isinstance(j, int) else slice(j * per, j * per + per)
                    leave(stage, s, dst[:, where, :], i, **kw)

            def root(stage, d, width=T, rows=slice(0, P), slot=0):
                leave(stage, 0, std[rows, slot, 0:width], cols=slice(0, width), rows=rows,
                      func=ACT.Sqrt, scale=1.0 / d, bias=eps[rows, :])

            def gated(up):
                for j, s, i in steps(act, 0, 11, 2):
                    dst = hid[:, 2 * j:2 * j + 2, :] if isinstance(j, int) else hid[:, bass.ds(j * 2, 2), :]
                    leave(up, 2 * s, dst, i, func=ACT.Silu)

            def layer0(name):
                root(f"mixnorm_{name}", D)
                leaves(f"conv_in_{name}", 12, cproj)
                root(f"ffnnorm_{name}", D)
                gated(f"up_{name}")

            leave("vectors", 0, vec[:, :], cols=slice(0, VROWS["end"]))
            leave("vectors", 1, modb[:, :], cols=slice(0, 96))
            leaves("turn_x", 4, h_lat)
            leaves("turn_ctx", 4, h_ctx)
            wait_emptied(act, "vectors", 0)
            for s, name in enumerate(("c", "c_ctx")):
                nc.scalar.activation(cvec[:, :, s], vec[:, VROWS[name]:VROWS[name] + 8], ACT.Silu).then_inc(s_cvec, 1)
            root("norm1", D)
            for s in range(12):
                kind, n = s // 6, s % 6
                if n < 4:
                    leave("qkv", s, qk[:, 8 * kind + 2 * n:8 * kind + 2 * n + 2, :], scale=DH ** -0.5 if n < 2 else 1.0)
                else:
                    at = 512 * kind + 256 * (n - 4)
                    leave("qkv", s, vtok[:, :, at:at + 256])
            leaves("gates", 8, gate, func=ACT.Sigmoid)

            def mod_rows(stage, s, i=0, group=None, done=None):
                if done is not None:
                    act.wait_ge(s_mod, done)
                leave(stage, s if group is None else group, mrow[:, s % 4, :], i, cols=slice(0, WIDE), rows=slice(0, 2))

            for s in range(HALVES + 3):
                for j in MOD_STEP[s]:
                    mod_rows("attention", j, group=ATT.index(("mod", j)), done=j - 3 if j >= 4 else None)
                if s < HALVES:
                    act.wait_ge(s_soft_in, s + 1)
                    if s < HEADS:
                        for t in range(2):
                            last = nc.scalar.activation(prob[:, s % 3, t, :], logit[:, s % 3, t, :], ACT.Exp,
                                                        bias=small[:, s, t:t + 1], accum_out=small[:, s, 2 + t:3 + t])
                        last.then_inc(s_soft_exp, 1)
                    else:
                        nc.scalar.activation(expo[:, s % 3], expo[:, s % 3], ACT.Exp).then_inc(a_step, 1)
                        act.wait_ge(a_step, s - HEADS + 1)
                        nc.scalar.activation(soft[:, s % 3], expo[:, s % 3], ACT.Ln, bias=ones[:, 0:1])\
                            .then_inc(s_soft_exp, 1)
                if HEADS < s <= HALVES:
                    n = s - 1
                    act.wait_ge(s_arg, n - HEADS + 1)
                    nc.scalar.activation(prob[:, n % 3], logit[:, n % 3], ACT.Exp).then_inc(s_prob_s, 1)
                if 2 <= s < HALVES + 2:
                    leave("attention", ATT.index(("turn", s - 2)), prob_t[:, (s - 2) % 2])
                if s >= 3 and (s - 3) % 2 == 1:
                    leave("attention", ATT.index(("value", (s - 3) // 2)), o_t[:, (s - 3) // 2, :], cols=slice(0, T))

            root("norm2", D)
            leaves("peer_q", 8, pq)
            for g in range(4):
                leave("turn_keys", g, keys_t[:, 4 * g:4 * g + 4, :])
            for g in range(8):
                leave("peer_scores", g, score[:, g // 4, 4 * (g % 4):4 * (g % 4) + 4, :])
            for g in range(4):
                leave("turn_x2", g, x2_tok[:, g // 2, 512 * (g % 2):512 * (g % 2) + 512])
            for j, s, i in steps(act, 0, MODS):
                mod_rows("mod1", s, i, done=i * 4 + (MODS + s - 3))
            act.wait_ge(s_shift, 1)
            nc.scalar.activation(shifted, shifted, ACT.Exp).then_inc(s_pexp, 1)
            root("mixnorm_ctx", D)

            def gather(it, i, half, kind, first):
                def gelu(quad):
                    act.wait_ge(s_dots, it * 4 + quad + 1)
                    nc.scalar.activation(gelus[:, 4 * quad:4 * quad + 4], dots[:, 4 * quad:4 * quad + 4], ACT.Gelu)\
                        .then_inc(s_gelu, 1)

                def extra(k):
                    s = first + k
                    if kind == "conv_in":
                        leave("conv_in_ctx", s, some(cproj, (i * 4 + s) * 2, 2), i)
                    if kind == "norm" and k == 0:
                        root("ffnnorm_ctx", D)
                    if kind == "up" and s < 22 and k % 2 == 0:
                        leave("up_ctx", s, some(hid, i * 4 + s, 2), i, func=ACT.Silu)

                gelu(0)
                extra(0)
                gelu(1)
                extra(1)
                gelu(2)
                gelu(3)
                extra(2)
                act.wait_ge(v_free[7], it * 2 + 4)
                nc.scalar.activation(rows16[:, :], wide[1][0:16, :], ACT.Copy).then_inc(s_vo, 1)
                extra(3)
                act.wait_ge(vo_full, it + 1)
                nc.scalar.activation(some2(peer, it * 16, 16), wide[1][:, 0:P].rearrange("p (m t) -> p m t", m=KD),
                                     ACT.Copy).then_inc(vo_free, 1)

            for it, i, half, kind, first in turns_of(act):
                gather(it, i, half, kind, first)

            root("norm_final", D)
            layer0("lat")

            root("mixnorm1_ctx", D)
            root("mixnorm1_lat", D)
            for s in range(3):
                leave("mla_in", s, qlat[:, 2 * s:2 * s + 2, :])
            for m in range(2):
                leave("mla_in", 3 + m, kvlat[:, m, :])
            leave("mla_in", 5, kpe[NOPE:QH, :], rows=slice(NOPE, QH))
            root("qlat_norm", QLAT)
            root("kvlat_norm", KVLAT, 2 * T)
            root("kpe_norm", 1.0, 2 * T, slice(NOPE, QH))
            for g, (kind, n) in enumerate(HEAD):
                if kind == "value":
                    leave("heads", g, vmla[:, n % 4, 512 * (n // 4):512 * (n // 4) + 512])
                if kind in ("key", "query"):
                    wait_full(act, "heads", g)
                    b = bank_of("heads", g)
                    rows = slice(0, NOPE if kind == "key" else QH)
                    dst = kcat[rows, n, :] if kind == "key" else q[rows, 2 * n:2 * n + 2, :].rearrange("p a t -> p (a t)")
                    nc.scalar.activation(dst, bank[b][rows, :], ACT.Copy)
                    nc.scalar.activation(squares[rows, SQUARE[(kind, n)] % 12, :], bank[b][rows, :], ACT.Square)\
                        .then_inc(free[b], 1)
                if kind in ("key_mean", "query_mean"):
                    rows = slice(0, NOPE if kind == "key_mean" else QH)
                    m = n if kind == "key_mean" else MH + n
                    if m >= 2:
                        act.wait_ge(s_kn if m - 2 < MH else s_qn, m - 1 if m - 2 < MH else m - 1 - MH)
                    leave("heads", g, std[rows, m % 2, :], rows=rows, func=ACT.Sqrt, bias=eps[rows, :])
            for s in range(MH + 2):
                if s < MH:
                    act.wait_ge(s_soft_in, HALVES + s + 1)
                    for t in range(2):
                        n = 2 * s + t
                        nc.scalar.activation(mprob[:, s % 2, t, :], sbank[n % 4], ACT.Exp, scale=QH ** -0.5,
                                             bias=msmall[:, s, t:t + 1], accum_out=msmall[:, s, 2 + t:3 + t])\
                            .then_inc(sc_free[n % 4], 1)
                if s >= 2 and s % 2 == 1:
                    leave("mla_attention", MATT.index(("value", (s - 2) // 2)), o_mla[:, (s - 2) // 2, :],
                          cols=slice(0, T))
                if 1 <= s <= MH:
                    for half in range(2):
                        leave("mla_attention", MATT.index(("turn", 2 * (s - 1) + half)),
                              mprob_t[:, (s - 1) % 2, 2 * half:2 * half + 2, :])
            root("ffnnorm1", D)
            gated("up_1")
            for g in range(4):
                leave("turn_out", g, out_tok[:, g // 2, 512 * (g % 2):512 * (g % 2) + 512])

        @block.vector
        def _(v):
            for b in range(4):
                v.sem_inc(sc_free[b], 1)
            v.sem_inc(xb_free[0], 1)
            v.sem_inc(xb_free[1], 4)

            counted = [0]

            def settle(instruction):
                counted[0] += 1
                instruction.then_inc(s_step, 1)
                v.wait_ge(s_step, counted[0])

            def tt(out, a, b, op):
                return nc.vector.tensor_tensor(out, a, b, op)

            def spread_last(a, n):
                return a.unsqueeze(len(a.shape)).to_broadcast([*a.shape, n])

            def apply_norm(r, root_stage, kt, src, gain, dst, shift=None, width=T, rows=slice(0, P)):
                wait_emptied(v, root_stage, 0)
                settle(nc.vector.reciprocal(rstd[rows, 0, 0:width], std[rows, 0, 0:width]))
                for k in range(kt):
                    last = nc.vector.scalar_tensor_tensor(dst(k), src(k), gain(k), rstd[rows, 0, 0:width],
                                                          ALU.mult, ALU.mult)
                if shift is not None:
                    settle(last)
                    for k in range(kt):
                        last = nc.vector.tensor_scalar(dst(k), dst(k), shift(k), None, ALU.add)
                last.then_inc(s_norm, 1)
                v.wait_ge(s_norm, r + 1)

            def norm(r, stage, x, gain, dst, shift=None):
                tt(sq[:, :, :], x[:, :, :], x[:, :, :], ALU.mult).then_inc(s_sq, 1)
                apply_norm(r, stage, KD, lambda k: x[:, k, :], gain, dst, shift)

            def lat(k):
                return nrm[:, k, T:2 * T]

            def con(k):
                return nrm[:, k, 0:T]

            def mod_norm(r, stage, layer, i, x, dst, who):
                norm(r, stage, x, lambda k: gmod[:, layer, i, k, who:who + 1], dst,
                     lambda k: mod[:, layer, 24 * i + k, who:who + 1])

            def residual_bank(stage, layer, i, h, who, g):
                wait_full(v, stage, g)
                b = bank_of(stage, g)
                for m in range(2):
                    k = 2 * g + m
                    last = nc.vector.scalar_tensor_tensor(
                        h[:, k, :], bank[b][:, m * T:(m + 1) * T], mod[:, layer, 24 * i + 16 + k, who:who + 1],
                        h[:, k, :], ALU.mult, ALU.add)
                last.then_inc(free[b], 1)

            def residual(stage, layer, i, h, who, n):
                for g in range(4):
                    residual_bank(stage, layer, i, h, who, g)
                wait_all_emptied(v, stage, 4)

            def hidden_pair(up, j, s, i):
                wait_full(v, up, 2 * s + 1, i)
                wait_emptied(v, up, 2 * s, i)
                b = bank_of(up, 2 * s + 1)
                here = some(hid, j * 2, 2)
                tt(here, here, bank[b][:, :].rearrange("p (a t) -> p a t", a=2), ALU.mult).then_inc(free[b], 1)

            def hidden(up):
                for j, s, i in steps(v, 0, 11, 2):
                    hidden_pair(up, j, s, i)

            def convolve(name):
                nc.vector.memset(z[:, :, 0:1], 0.0)
                settle(nc.vector.memset(z[:, :, T + 1:T + 2], 0.0))
                wait_all_emptied(v, f"conv_in_{name}", 12)
                settle(tt(z[:, :, 1:T + 1], cproj[:, 8:16, :], cproj[:, 16:24, :], ALU.mult))
                for k in range(KD):
                    last = nc.vector.tensor_scalar(cproj[:, 8 + k, :], z[:, k, 0:T], vcol("conv_k", k),
                                                   vcol("conv_b", k), ALU.mult, ALU.add)
                settle(last)
                for tap in (1, 2):
                    for k in range(KD):
                        last = nc.vector.scalar_tensor_tensor(
                            cproj[:, 8 + k, :], z[:, k, tap:tap + T], vcol("conv_k", 8 * tap + k), cproj[:, 8 + k, :],
                            ALU.mult, ALU.add)
                    settle(last)
                tt(cproj[:, 0:8, :], cproj[:, 0:8, :], cproj[:, 8:16, :], ALU.mult).then_inc(s_conv, 1)

            def layer0(name, r, h, dst, who, n):
                mod_norm(r, f"mixnorm_{name}", 0, 0, h, dst, who)
                convolve(name)
                residual(f"conv_out_{name}", 0, 0, h, who, n)
                mod_norm(r + 1, f"ffnnorm_{name}", 0, 1, h, dst, who)
                hidden(f"up_{name}")
                residual(f"down_{name}", 0, 1, h, who, n + 1)

            wait_emptied(v, "vectors", 0)
            wait_all_emptied(v, "turn_x", 4)
            norm(0, "norm1", h_lat, lambda k: vcol("norm1", k), lat)
            settle(nc.vector.memset(wts[:, :], 0.0))
            nc.vector.tensor_copy(sel[:, :, :], spread_last(row32, P)).then_inc(s_index, 1)

            def front(n):
                b = c = n % 3
                v.wait_ge(sc_full[b], n // 3 + 1)
                scores = sbank[b].rearrange("p (t k) -> p t k", t=2)
                if n < HEADS:
                    slope = 2.0 ** (-8.0 * (n + 1) / HEADS)
                    nc.vector.scalar_tensor_tensor(logit[:, c], dist, -slope, scores, ALU.mult, ALU.add)\
                        .then_inc(sc_free[b], 1)
                    v.wait_ge(sc_free[b], n // 3 + 2)
                    nc.vector.tensor_reduce(small[:, n, 0:2], logit[:, c], AX.X, ALU.max, negate=True)\
                        .then_inc(s_soft_in, 1)
                else:
                    if n - 3 >= HEADS:
                        v.wait_ge(s_prob_s, n - 3 - HEADS + 1)
                    tt(logit[:, c], scores, strict, ALU.add).then_inc(sc_free[b], 1)
                    v.wait_ge(sc_free[b], n // 3 + 2)
                    nc.vector.scalar_tensor_tensor(expo[:, c], logit[:, c], -1.0, logit[:, c], ALU.mult, ALU.min)\
                        .then_inc(s_soft_in, 1)

            def back(n):
                c = n % 3
                v.wait_ge(s_soft_exp, n + 1)
                if n < HEADS:
                    settle(nc.vector.reciprocal(small[:, n, 4:6], small[:, n, 2:4]))
                    tt(prob[:, c], prob[:, c], spread_last(small[:, n, 4:6], T), ALU.mult).then_inc(s_prob_v, 1)
                else:
                    settle(nc.vector.scalar_tensor_tensor(soft[:, c], logit[:, c], 0.0, soft[:, c], ALU.max, ALU.add))
                    for t in range(2):
                        last = nc.vector.tensor_tensor_scan(expo[:, c, t, ::-1], ones, soft[:, c, t, ::-1], 0.0,
                                                            ALU.mult, ALU.add)
                    settle(last)
                    tt(logit[:, c], logit[:, c], expo[:, c], ALU.subtract).then_inc(s_arg, 1)

            for s in range(HALVES + 1):
                if s < HALVES:
                    front(s)
                if s >= 1:
                    back(s - 1)

            wait_all_emptied(v, "gates", 8)
            for n, stage in enumerate(("out_moba", "out_sb")):
                for g in range(4):
                    wait_full(v, stage, g)
                    b = bank_of(stage, g)
                    here = gate[:, 8 * n + 2 * g:8 * n + 2 * g + 2, :]
                    tt(here, here, bank[b][:, :].rearrange("p (a t) -> p a t", a=2), ALU.mult).then_inc(free[b], 1)
                wait_all_emptied(v, stage, 4)
            tt(gate[:, 0:8, :], gate[:, 0:8, :], gate[:, 8:16, :], ALU.add).then_inc(s_mixed, 1)
            for g in range(4):
                wait_full(v, "mix", g)
                b = bank_of("mix", g)
                here = h_lat[:, 2 * g:2 * g + 2, :]
                tt(here, here, bank[b][:, :].rearrange("p (a t) -> p a t", a=2), ALU.add).then_inc(free[b], 1)
            wait_all_emptied(v, "mix", 4)
            norm(1, "norm2", h_lat, lambda k: vcol("norm2", k), lat)

            def sixteen(rows, best_of, index_of, count):
                for a in range(0, count, 4):
                    four = range(a, a + 4)
                    for n in four:
                        last = nc.vector.max(best_of(n)[:, 0:8], rows(n))
                    settle(last)
                    for n in four:
                        nc.vector.max_index(index_of(n)[:, 0:8], best_of(n)[:, 0:8], rows(n))
                        last = nc.vector.match_replace(rows(n), best_of(n)[:, 0:8], rows(n), -3.4e38)
                    settle(last)
                    for n in four:
                        last = nc.vector.max(best_of(n)[:, 8:16], rows(n))
                    settle(last)
                    for n in four:
                        last = nc.vector.max_index(index_of(n)[:, 8:16], best_of(n)[:, 8:16], rows(n))
                settle(last)

            wait_all_emptied(v, "turn_x2", 4)
            nc.vector.tensor_copy(split[0], x2_tok).then_inc(s_split, 1)
            v.wait_ge(s_split, 1)
            settle(tt(rest, x2_tok, split[0], ALU.subtract))
            nc.vector.tensor_copy(split[1], rest).then_inc(s_split, 1)
            v.wait_ge(s_split, 2)
            settle(tt(rest, rest, split[1], ALU.subtract))
            nc.vector.tensor_copy(split[2], rest).then_inc(s_split, 1)

            for t in range(2):
                sixteen(lambda n: score[:, t, n, :], lambda n: top[:, t, n, :], lambda n: top_i[:, t, n, :], 16)
                nc.vector.tensor_copy(top_f[:, t], top_i[:, t])
                pair = top[:, t].rearrange("p (h b) k -> p h b k", b=2)
                settle(tt(cand.rearrange("p h (i j) -> p h i j", i=TOPK),
                          pair[:, :, 0, :].unsqueeze(3).to_broadcast([P, PH, TOPK, TOPK]),
                          pair[:, :, 1, :].unsqueeze(2).to_broadcast([P, PH, TOPK, TOPK]), ALU.add))
                pos_h = pos.rearrange("p (h k) -> p h k", h=PH)
                sixteen(lambda n: cand[:, n, :], lambda n: best[:, t, n, :], lambda n: pos_h[:, n, :], PH)
                nc.vector.tensor_scalar(part[:, 0], pos, 4, None, ALU.logical_shift_right)
                settle(nc.vector.tensor_scalar(part[:, 1], pos, 15, None, ALU.bitwise_and))
                settle(nc.vector.tensor_copy(part_f, part))
                index = top_f[:, t].rearrange("p (h b) k -> p h b k", b=2)
                for b in range(2):
                    settle(tt(eq, spread_last(part_f[:, b], TOPK),
                              iota.unsqueeze(1).to_broadcast([P, P, TOPK]), ALU.is_equal))
                    eq_h = eq.rearrange("p (h k) m -> p h k m", h=PH)
                    settle(tt(eq_h, eq_h, index[:, :, b, :].unsqueeze(2).to_broadcast([P, PH, TOPK, TOPK]), ALU.mult))
                    settle(nc.vector.tensor_reduce(pick[:, b], eq, AX.X, ALU.add))
                nc.vector.scalar_tensor_tensor(chosen[:, t], pick[:, 0], float(KEYS), pick[:, 1], ALU.mult, ALU.add)
                last = tt(shifted[:, t], best[:, t], best[:, t, :, 0:1].to_broadcast([P, PH, TOPK]), ALU.subtract)
                settle(last)
            v.sem_inc(s_shift, 1)
            v.wait_ge(s_pexp, 1)
            settle(nc.vector.tensor_reduce(sums[:, 0], shifted, AX.X, ALU.add))
            settle(nc.vector.reciprocal(sums[:, 1], sums[:, 0]))
            last = None
            for t in range(2):
                last = tt(shifted[:, t], shifted[:, t], spread_last(sums[:, 1, t], TOPK), ALU.mult)
            last.then_inc(s_chosen, 1)

            wait_full(v, "turn_chosen", 0)
            b = bank_of("turn_chosen", 0)
            nc.vector.tensor_copy(idx_t[:, :], bank[b][:, 0:T]).then_inc(s_index, 1)
            v.wait_ge(s_index, 2)
            nc.vector.tensor_copy(gate_t[:, :], bank[b][:, T:2 * T]).then_inc(s_index, 1)
            v.wait_ge(s_index, 3)
            v.sem_inc(free[b], 1)
            v.wait_ge(s_mod, 2 * MODS)
            for layer in range(2):
                last = tt(mod[:, layer], sbank[3][:, 96 * layer:96 * layer + 96].rearrange("p (m s) -> p m s", s=2),
                          spread_last(modb[:, 48 * layer:48 * layer + 48], 2), ALU.add)
            settle(last)
            for layer in range(2):
                for i, name in enumerate(("mix", "ffn")):
                    a = VROWS[name] + 8 * layer
                    last = nc.vector.scalar_tensor_tensor(gmod[:, layer, i], mod[:, layer, 24 * i + 8:24 * i + 16, :],
                                                          1.0, spread_last(vec[:, a:a + 8], 2), ALU.add, ALU.mult)
            settle(last)
            mod_norm(2, "mixnorm_ctx", 0, 0, h_ctx, con, 1)

            def gather(it, i, half, kind, first):
                def products(quad):
                    for s in range(4 * quad, 4 * quad + 4):
                        v.wait_ge(u_landed[s % 4], (it * 4 + quad + 1) * 16)
                        for c in range(2):
                            v.wait_ge(xb_full[c], it * 16 + s + 1)
                            u = ubuf[s % 4][:, 512 * c:512 * c + 512]
                            nc.vector.tensor_tensor_reduce(u, u, sbank[c], 1.0, 0.0, ALU.mult, ALU.add,
                                                           halves[:, c, s:s + 1]).then_inc(xb_free[c], 1)
                    v.wait_ge(xb_free[1], it * 16 + 4 * quad + 8)
                    four = slice(4 * quad, 4 * quad + 4)
                    tt(dots[:, four], halves[:, 0, four], halves[:, 1, four], ALU.add).then_inc(s_dots, 1)

                def weigh(quad):
                    v.wait_ge(s_gelu, it * 4 + quad + 1)
                    tt(wts[:, 68 * quad:68 * quad + 52:17], gelus[:, 4 * quad:4 * quad + 4],
                       some(gate_t, it * 16 + 4 * quad, 4), ALU.mult).then_inc(s_wts, 1)

                def extra(k):
                    s = first + k
                    if kind == "conv" and k == 3:
                        convolve("ctx")
                    if kind == "conv_out":
                        residual_bank("conv_out_ctx", 0, 0, h_ctx, 1, k)
                    if kind == "norm":
                        if k == 0:
                            apply_norm(3, "ffnnorm_ctx", KD, lambda n: h_ctx[:, n, :],
                                       lambda n: gmod[:, 0, 1, n, 1:2], con, lambda n: mod[:, 0, 24 + n, 1:2])
                    if kind == "up" and s < 22 and k % 2 == 1:
                        hidden_pair("up_ctx", i * 2 + s // 2, s // 2, i)

                if kind == "norm":
                    wait_all_emptied(v, "conv_out_ctx", 4)
                    tt(sq[:, :, :], h_ctx[:, :, :], h_ctx[:, :, :], ALU.mult).then_inc(s_sq, 1)
                products(0)
                weigh(0)
                extra(0)
                products(1)
                weigh(1)
                extra(1)
                products(2)
                weigh(2)
                products(3)
                weigh(3)
                extra(2)
                extra(3)

            for it, i, half, kind, first in turns_of(v):
                gather(it, i, half, kind, first)
            residual("down_ctx", 0, 1, h_ctx, 1, 1)
            v.wait_ge(vo_free, 17)
            settle(tt(h_lat[:, :, :], h_lat[:, :, :], peer, ALU.add))
            norm(4, "norm_final", h_lat, lambda k: vcol("final", k), lambda k: h_lat[:, k, :])

            layer0("lat", 5, h_lat, lat, 0, 2)

            mod_norm(7, "mixnorm1_ctx", 1, 0, h_ctx, con, 1)
            mod_norm(8, "mixnorm1_lat", 1, 0, h_lat, lat, 0)
            wait_all_emptied(v, "mla_in", 6)
            tt(sq[:, 0:6, :], qlat, qlat, ALU.mult).then_inc(s_sq, 1)
            apply_norm(9, "qlat_norm", 6, lambda k: qlat[:, k, :], lambda k: vcol("q_lat", k), lambda k: qlat[:, k, :])

            def square_wide(n, rows):
                return sq[rows, 2 * n:2 * n + 2, :].rearrange("p a t -> p (a t)")

            every = slice(0, P)
            for k in range(2):
                last = tt(square_wide(k, every), kvlat[:, k, :], kvlat[:, k, :], ALU.mult)
            last.then_inc(s_sq, 1)
            apply_norm(10, "kvlat_norm", 2, lambda k: kvlat[:, k, :], lambda k: vcol("kv_lat", k),
                       lambda k: kvlat[:, k, :], width=2 * T)
            rope = slice(NOPE, QH)
            tt(square_wide(0, rope), kpe[rope, :], kpe[rope, :], ALU.mult).then_inc(s_sq, 1)
            apply_norm(11, "kpe_norm", 1, lambda k: kpe[rope, :], lambda k: vcol("kn", 0)[rope, :],
                       lambda k: kpe[rope, :], width=2 * T, rows=rope)
            wait_full(v, "kpe_turn", 0)
            b = bank_of("kpe_turn", 0)
            nc.vector.tensor_tensor(std[rope, 0, 0:T], bank[b][rope, 0:T], sin[rope, :], ALU.mult).then_inc(free[b], 1)
            settle(tt(kpe[rope, T:2 * T], kpe[rope, T:2 * T], cos[rope, :], ALU.mult))
            tt(kpe[rope, T:2 * T], kpe[rope, T:2 * T], std[rope, 0, 0:T], ALU.add).then_inc(s_kpe, 1)
            v.wait_ge(s_kpe, 1)

            def head_norm(m, mean_at, x, rows, gain, done):
                wait_emptied(v, "heads", HEAD.index(mean_at))
                settle(nc.vector.reciprocal(rstd[rows, m % 2, :], std[rows, m % 2, :]))
                nc.vector.scalar_tensor_tensor(x, x, gain[rows], rstd[rows, m % 2, :], ALU.mult, ALU.mult)\
                    .then_inc(done, 1)

            for n in range(MH):
                head_norm(n, ("key_mean", n), kcat[0:NOPE, n, :], slice(0, NOPE), vcol("kn", 0), s_kn)
            for s in range(9):
                if s < 8:
                    head_norm(MH + s, ("query_mean", s), q[0:QH, 2 * s:2 * s + 2, :].rearrange("p a t -> p (a t)"),
                              slice(0, QH), vcol("qn", 0), s_qn)
                if s >= 1:
                    n = s - 1
                    g = HEAD.index(("query_turn", n))
                    wait_full(v, "heads", g)
                    b = bank_of("heads", g)
                    pair = q[0:QH, 2 * n:2 * n + 2, :]
                    turned = sq[0:QH, 2 * (n % 4):2 * (n % 4) + 2, :]
                    tt(turned, bank[b][0:QH, :].rearrange("p (a t) -> p a t", a=2),
                       sin[0:QH, :].unsqueeze(1).to_broadcast([QH, 2, T]), ALU.mult).then_inc(free[b], 1)
                    settle(tt(pair, pair, cos[0:QH, :].unsqueeze(1).to_broadcast([QH, 2, T]), ALU.mult))
                    tt(pair, pair, turned, ALU.add).then_inc(s_qr, 1)
            for s in range(MH + 1):
                if s < MH:
                    for t in range(2):
                        n = 2 * s + t
                        v.wait_ge(sc_full[n % 4], SCORED[n % 4] + n // 4 + 1)
                        last = nc.vector.tensor_reduce(msmall[:, s, 4 + t:5 + t], sbank[n % 4], AX.X, ALU.max, negate=True)
                    settle(last)
                    nc.vector.tensor_scalar(msmall[:, s, 0:2], msmall[:, s, 4:6], QH ** -0.5, None, ALU.mult)\
                        .then_inc(s_soft_in, 1)
                if s >= 1:
                    m = s - 1
                    for t in range(2):
                        n = 2 * m + t
                        v.wait_ge(sc_free[n % 4], SCORED[n % 4] + n // 4 + 2)
                    settle(nc.vector.reciprocal(msmall[:, m, 6:8], msmall[:, m, 2:4]))
                    for t in range(2):
                        last = nc.vector.tensor_scalar(mprob[:, m % 2, t, :], mprob[:, m % 2, t, :],
                                                       msmall[:, m, 6 + t:7 + t], None, ALU.mult)
                    last.then_inc(s_prob_v, 1)
            residual("mla_out", 1, 0, h_lat, 0, 4)
            mod_norm(12, "ffnnorm1", 1, 1, h_lat, lat, 0)
            hidden("up_1")
            residual("down_1", 1, 1, h_lat, 0, 5)


_INS = ["x", "norm1_g", "w_in", "w_out_moba", "w_out_sb", "w_mix_out", "norm2_g", "peer_w_q", "peer_sub_keys",
        "peer_u", "peer_v", "final_norm_g", "c_2", "ctx_2", "c_ctx_2", "norm_mix_g_2", "norm_ffn_g_2", "mod_w_2",
        "mod_b_2", "ffn_w_gate_2", "ffn_w_up_2", "ffn_w_down_2", "conv_w_in_2", "conv_k_2", "conv_b_2",
        "conv_w_out_2", "mla_w_in_2", "mla_q_norm_g_2", "mla_w_q_up_2", "mla_kv_norm_g_2", "mla_w_kv_up_2",
        "mla_qn_nope_g_2", "mla_qn_rope_g_2", "mla_kn_nope_g_2", "mla_kn_rope_g_2", "mla_w_out_2"]


def kernel(**inputs):
    import concourse.bacc as bacc
    from concourse.bass_utils import run_bass_kernel_spmd

    nc = bacc.Bacc("TRN2", target_bir_lowering=False, num_devices=1)
    arrays, w = {}, {}
    for name in _INS:
        a = np.ascontiguousarray(inputs[name])
        arrays[f"in_{name}_dram"] = a
        w[name] = nc.dram_tensor(f"in_{name}_dram", a.shape, mybir.dt.from_np(a.dtype), kind="ExternalInput").ap()
    arrays["in_consts_dram"] = constants()
    consts = nc.dram_tensor("in_consts_dram", arrays["in_consts_dram"].shape, F32, kind="ExternalInput").ap()
    out = nc.dram_tensor("out_0_dram", (1, T, D), F32, kind="ExternalOutput").ap()
    program(nc, w, consts, out)
    r = run_bass_kernel_spmd(nc, [arrays], core_ids=[0])
    return r.results[0]["out_0_dram"]
```

```python
from contextlib import ExitStack
from itertools import chain

import numpy as np

import concourse.bass as bass
from concourse import mybir

P = 128
T = 256
D = 1024
KD = D // P
HID = 2816
KH = HID // P
HEADS = 8
DH = 64
PH, KEYS, TOPK = 8, 128, 16
MH, NOPE, ROPE, MV = 16, 64, 32, 64
QH = NOPE + ROPE
QLAT, KVLAT = 768, 256
SLOTS = 4
SLOT = 2048
WIDE = SLOT // KD
BANKS = 4
EPS = 1e-6
BIG = 1e30

F32 = mybir.dt.float32
F32R = mybir.dt.float32r
BF16 = mybir.dt.bfloat16
U32 = mybir.dt.uint32
ALU = mybir.AluOpType
ACT = mybir.ActivationFunctionType
AX = mybir.AxisListType


def firsts(table):
    out, at = {}, 0
    for name, n in table:
        out[name] = at
        at += n
    return out


HALVES = 2 * HEADS
MODS = 24
MOD_STEP = [[] for _ in range(HALVES + 3)]
for _j in range(MODS):
    MOD_STEP[_j // 2 if _j < 10 else _j - 5].append(_j)
ATT = []
for _s in range(HALVES + 3):
    ATT += [("mod", _j) for _j in MOD_STEP[_s]]
    if 2 <= _s < HALVES + 2:
        ATT.append(("turn", _s - 2))
    if _s >= 3 and (_s - 3) % 2 == 1:
        ATT.append(("value", (_s - 3) // 2))
MATT = []
for _s in range(1, MH + 2):
    if _s >= 2 and _s % 2 == 0:
        MATT.append(("value", (_s - 2) // 2))
    if _s - 1 < MH:
        MATT += [("turn", 2 * (_s - 1)), ("turn", 2 * (_s - 1) + 1)]
LOADED = ([("key", _n) for _n in range(8)] + [("value", _n) for _n in range(4)]
          + [("key", _n) for _n in range(8, 16)] + [("value", _n) for _n in range(4, 8)]
          + [("query", _n) for _n in range(8)])
HEAD = []
_means = [("key_mean", _n) for _n in range(MH)]
for _n, _x in enumerate(LOADED):
    HEAD.append(_x)
    if _n >= 2 and (_n % 2 == 0 or _n >= 24) and _means:
        HEAD.append(_means.pop(0))
HEAD += _means
for _n in range(9):
    if _n < 8:
        HEAD.append(("query_mean", _n))
    if _n >= 1:
        HEAD.append(("query_turn", _n - 1))
SQUARE = {_x: _n for _n, _x in enumerate([("key", _n) for _n in range(MH)] + [("query", _n) for _n in range(8)])}


def layer0(s, first):
    return first + [(f"conv_out_{s}", 4, 4), (f"ffnnorm_{s}", 0, 1), (f"up_{s}", 22, 22), (f"down_{s}", 11, 4)]


STAGES = ([("vectors", 0, 2), ("turn_x", 0, 4), ("turn_ctx", 0, 4), ("norm1", 0, 1), ("qkv", 12, 12),
           ("gates", 8, 8), ("attention", MODS, len(ATT)), ("out_moba", 2, 4), ("out_sb", 2, 4), ("mix", 4, 4),
           ("norm2", 0, 1), ("peer_q", 8, 8), ("mixnorm_ctx", 0, 1), ("turn_keys", 0, 4), ("peer_scores", 0, 8),
           ("turn_x2", 0, 4), ("mod1", MODS, MODS), ("early_ctx", 2, 2), ("turn_chosen", 0, 1), ("late_ctx", 2, 2)]
          + layer0("ctx", [("conv_in_ctx", 8, 8)]) + [("norm_final", 0, 1)]
          + layer0("lat", [("mixnorm_lat", 0, 1), ("conv_in_lat", 12, 12), ("mixnorm1_ctx", 0, 1)])
          + [("mixnorm1_lat", 0, 1), ("mla_in", 5, 6), ("qlat_norm", 0, 1),
             ("kvlat_norm", 0, 1), ("kpe_norm", 0, 1), ("kpe_turn", 0, 1), ("heads", 10, len(HEAD)),
             ("mla_attention", 0, len(MATT)), ("mla_out", 4, 4), ("ffnnorm1", 0, 1), ("up_1", 22, 22),
             ("down_1", 11, 4), ("turn_out", 0, 4)])
CHUNK = firsts([(n, c) for n, c, _ in STAGES])
GROUP = firsts([(n, g) for n, _, g in STAGES])

RUNS = [("qkv", 20), ("conv_in_lat", 12), ("up_lat", 33), ("up_1", 33)]
RUN_OF = {"qkv": ("qkv", 0), "gates": ("qkv", 12), "conv_in_lat": ("conv_in_lat", 0), "up_lat": ("up_lat", 0), "down_lat": ("up_lat", 22),
          "up_1": ("up_1", 0), "down_1": ("up_1", 22)}
SPLIT_BEFORE = {}
_count = [0] * SLOTS
for _run, _n in RUNS:
    SPLIT_BEFORE[_run] = list(_count)
    for _j in range(_n):
        _count[(CHUNK[_run] + _j) % SLOTS] += 1
TURNS = [(0, 2, "conv_in", 0), (2, 1, "conv", 0), (3, 1, "conv_out", 0), (4, 1, "norm", 0), (5, 3, "up", 0),
         (8, 2, "up", 12), (10, 1, "up", 20), (11, 1, "down", 0), (12, 2, "down", 1), (14, 1, "down", 9),
         (15, 1, "none", 0)]
SCORED = [6, 5, 5, 0]

VROWS = firsts([("norm1", 8), ("norm2", 8), ("final", 8), ("mix", 16), ("ffn", 16), ("conv_k", 24),
                ("conv_b", 8), ("q_lat", 6), ("kv_lat", 2), ("c", 8), ("c_ctx", 8), ("qn", 1), ("kn", 1),
                ("end", 0)])

CCOLS = firsts([("ident", 128), ("ones", 256), ("mean", 128), ("turn", 128), ("cos", T), ("sin", T),
                ("iota", 16), ("row", 32), ("eps", 1), ("end", 0),
                ("dist", 2 * T), ("strict", 2 * T), ("all", 0)])


def constants():
    c = np.zeros((P, CCOLS["all"]), np.float32)

    def put(name, a):
        c[:a.shape[0], CCOLS[name]:CCOLS[name] + a.shape[1]] = a

    put("ident", np.eye(P))
    put("ones", np.ones((P, 256)))
    mean = np.zeros((QH, QH))
    mean[:NOPE, :NOPE] = 1.0 / NOPE
    mean[NOPE:, NOPE:] = 1.0 / ROPE
    put("mean", mean)
    axis, half = ROPE // 2, ROPE // 4
    turn = np.zeros((QH, QH))
    for a in range(2):
        for j in range(half):
            lo = NOPE + a * axis + j
            turn[lo, lo + half] = -1.0
            turn[lo + half, lo] = 1.0
    put("turn", turn.T)
    inv = np.float32(10000.0) ** (-np.arange(0, axis, 2, dtype=np.float32) / np.float32(axis))
    t = np.arange(T)
    ang = np.concatenate([(t // 64).astype(np.float32)[:, None] * inv] * 2
                         + [(t % 64).astype(np.float32)[:, None] * inv] * 2, axis=1)
    cos, sin = np.ones((QH, T)), np.zeros((QH, T))
    cos[NOPE:], sin[NOPE:] = np.cos(ang).T, np.sin(ang).T
    put("cos", cos)
    put("sin", sin)
    s = np.arange(T)[None, :]
    for tile in range(2):
        q = (tile * P + np.arange(P))[:, None]
        c[:, CCOLS["dist"] + tile * T:CCOLS["dist"] + (tile + 1) * T] = np.where(s <= q, q - s, BIG)
        c[:, CCOLS["strict"] + tile * T:CCOLS["strict"] + (tile + 1) * T] = np.where(s < q, 0.0, -BIG)
    c[:, CCOLS["iota"]:CCOLS["iota"] + 16] = np.arange(16)
    put("row", (np.arange(96)[:, None] % 32 == np.arange(32)[None, :]).astype(np.float32))
    c[:, CCOLS["eps"]] = EPS
    return c


def program(nc, w, consts_dram, out_dram):
    with ExitStack() as ctx:
        def sb(name, shape, dt=F32):
            return ctx.enter_context(nc.sbuf_tensor(name, shape, dt))

        def sem(name):
            return ctx.enter_context(nc.semaphore(name))

        bank = [ctx.enter_context(nc.psum_tensor(f"bank{b}", [P, 512], F32)) for b in range(BANKS)]
        wide = [ctx.enter_context(nc.psum_tensor(f"wide{b}", [P, 1024], F32)) for b in range(2)]
        sbank = [wide[b // 2][:, 512 * (b % 2):512 * (b % 2) + 512] for b in range(4)]

        ring, ring_at = [], []
        for s in range(SLOTS):
            ring.append(sb(f"weights{s}", [P, SLOT]))
            ring_at.append(nc.sbuf_base - 4 * SLOT)
        consts = sb("consts", [P, CCOLS["end"]])
        vec = sb("vec", [P, VROWS["end"]])
        cvec = sb("cvec", [P, KD, 2])
        modb = sb("modb", [P, 96])
        mod = sb("mod", [P, 2, 48, 2])
        gmod = sb("gmod", [P, 2, 2, KD, 2])
        h_lat = sb("h_lat", [P, KD, T])
        h_ctx = sb("h_ctx", [P, KD, T])
        nrm = sb("nrm", [P, KD, 2 * T])
        sq = sb("sq", [P, KD, T])
        std = sb("std", [P, 2, 2 * T])
        rstd = sb("rstd", [P, 2, 2 * T])
        idx_t = sb("idx_t", [P, T], U32)
        gate_t = sb("gate_t", [P, T])
        idx8 = sb("idx8", [P, 2, 8], U32)
        halves = sb("halves", [P, 2, 16])
        dots = sb("dots", [P, 16])
        gelus = sb("gelus", [P, 16])
        wts = sb("wts", [P, 16 * 16])
        rows16 = sb("rows16", [16, D])
        big = sb("big", [P, 10368])
        big_at = nc.sbuf_base - 4 * 10368
        more = sb("more", [P, 18432])
        more_at = nc.sbuf_base - 4 * 18432

        def over(name, shape, at):
            return nc.alloc_sbuf_tensor_at(name, shape, F32R, offset=at)

        def view(a, at, *dims, dt=None):
            n = int(np.prod(dims))
            if dt is BF16:
                v = a[:, at:at + n // 2].bitcast(BF16)
            elif dt is not None:
                v = a[:, at:at + n].bitcast(dt)
            else:
                v = a[:, at:at + n]
            names = "abcd"[:len(dims)]
            return v.rearrange(f"p ({' '.join(names)}) -> p {' '.join(names)}",
                               **{x: d for x, d in zip(names, dims)})

        qk = view(big, 0, 16, T)
        gate = view(big, 4096, 16, T)
        vtok = view(big, 8192, 2, 1024)
        logit = view(more, 0, 3, 2, T)
        prob = view(more, 1536, 3, 2, T)
        expo = view(more, 3072, 3, 2, T)
        soft = view(more, 4608, 3, 2, T)
        prob_t = view(more, 6144, 2, 2, T)
        o_t = view(more, 7168, 8, T)
        small = view(more, 9216, 16, 8)
        x_tok = view(more, 9472, 2, D)
        ctx_tok = view(more, 11520, 2, D)
        masks = view(more, 13824, 4 * T)
        vrows = view(more, 13568, P)
        brows = view(more, 13696, P)
        pq = view(big, 0, 16, T)
        keys_t = view(big, 4096, 16, P)
        keys = view(big, 6144, 16, P)
        x2_tok = view(big, 8320, 2, D)
        score = view(more, 0, 2, 16, P)
        top = view(more, 4096, 2, 16, TOPK)
        top_i = view(more, 4608, 2, 16, TOPK, dt=U32)
        top_f = view(more, 5120, 2, 16, TOPK)
        cand = view(more, 5632, 8, 256)
        eq = view(more, 7680, P, TOPK)
        best = view(more, 9728, 2, PH, TOPK)
        pos = view(more, 9984, P, dt=U32)
        part = view(more, 10112, 2, P, dt=U32)
        part_f = view(more, 10368, 2, P)
        pick = view(more, 10624, 2, P)
        chosen = view(more, 10880, 2, P)
        shifted = view(more, 11136, 2, PH, TOPK)
        sums = view(more, 11392, 2, 2, PH)
        split = [view(big, 1024 * j, 2, D, dt=BF16) for j in range(3)]
        rest = view(big, 3072, 2, D)
        ubuf = [view(more, 1024 * j, D) for j in range(4)]
        vbuf = [view(more, 4096 + 1024 * j, D) for j in range(8)]
        xs = view(more, 12288, 8, D, dt=BF16)[0:96]
        sel = view(more, 16384, 32, P, dt=BF16)[0:96]
        peer = nrm[:, :, T:2 * T]
        mrow = rows16[0:2, :].rearrange("p (j n) -> p j n", j=4)
        cproj = view(big, 0, 24, T)
        z = view(big, 6144, KD, T + 2)
        hid = view(big, 0, KH, T)
        w_hi = [over(f"high_weights{b}", [P, SLOT], more_at + 4 * SLOT * b) for b in range(SLOTS)]
        w_lo = [over(f"low_weights{b}", [P, SLOT], ring_at[b]) for b in range(SLOTS)]
        x_hi = over("high_input", [P, KD, T], more_at + 4 * 8192)
        x_lo = over("low_input", [P, KD, T], more_at + 4 * 10240)
        hid_lo = over("low_hidden", [P, KH, T], more_at + 4 * 12288)
        hid_hi = over("high_hidden", [P, KH, T], big_at)
        hid_raw = view(big, 5632, 2, 2, T)
        qlat = view(big, 0, 6, T)
        kvlat = view(big, 1536, 2, 2 * T)
        q = view(big, 2560, MH, T)
        msmall = view(big, 6656, 16, 8)
        kpe = view(big, 6784, 512)
        kcat = view(more, 0, MH, 2 * T)
        vmla = view(more, 8192, 4, MH * MV)
        o_mla = view(more, 12288, KD, T)
        squares = view(more, 12288, 12, 2 * T)
        mprob = view(more, 14336, 2, 2, 2 * T)
        mprob_t = view(more, 16384, 2, 4, T)
        out_tok = view(big, 0, 2, D)

        ident = consts[:, CCOLS["ident"]:CCOLS["ident"] + P]
        ones = consts[:, CCOLS["ones"]:CCOLS["ones"] + 256]
        mean = consts[:, CCOLS["mean"]:CCOLS["mean"] + P]
        turn = consts[:, CCOLS["turn"]:CCOLS["turn"] + P]
        cos = consts[:, CCOLS["cos"]:CCOLS["cos"] + T]
        sin = consts[:, CCOLS["sin"]:CCOLS["sin"] + T]
        dist = masks[:, 0:2 * T].rearrange("p (a t) -> p a t", a=2)
        strict = masks[:, 2 * T:4 * T].rearrange("p (a t) -> p a t", a=2)
        iota = consts[:, CCOLS["iota"]:CCOLS["iota"] + 16]
        row32 = consts[0:96, CCOLS["row"]:CCOLS["row"] + 32]
        eps = consts[:, CCOLS["eps"]:CCOLS["eps"] + 1]

        def vcol(name, k):
            return vec[:, VROWS[name] + k:VROWS[name] + k + 1]

        s_start = sem("constants_and_tokens_landed")
        s_keys = sem("keys_landed")
        w_landed = [sem(f"weights_landed{s}") for s in range(SLOTS)]
        w_free = [sem(f"weights_free{s}") for s in range(SLOTS)]
        full = [sem(f"bank_full{b}") for b in range(BANKS)]
        free = [sem(f"bank_free{b}") for b in range(BANKS)]
        sc_full = [sem(f"scores_full{b}") for b in range(4)]
        sc_free = [sem(f"scores_free{b}") for b in range(4)]
        s_step = sem("vector_step")
        a_step = sem("scalar_step")
        s_sq = sem("squares_ready")
        s_norm = sem("norm_ready")
        s_soft_in = sem("softmax_in_ready")
        s_soft_exp = sem("softmax_exp_done")
        s_arg = sem("stick_argument_ready")
        s_mod = sem("modulation_turned")
        s_vo = sem("token_rows_copied")
        vo_full = sem("token_rows_turned")
        s_prob_v = sem("probs_ready_by_vector")
        s_prob_s = sem("probs_ready_by_scalar")
        s_mixed = sem("mixed_ready")
        s_shift = sem("peer_shifted_ready")
        s_pexp = sem("peer_exp_done")
        s_chosen = sem("chosen_ready")
        s_index = sem("indices_ready")
        s_split = sem("split_ready")
        s_xs = sem("split_landed")
        s_idx8 = sem("indices_staged")
        s_turn = sem("gather_may_start")
        u_landed = [sem(f"u_landed{j}") for j in range(4)]
        v_landed = [sem(f"v_landed{j}") for j in range(8)]
        v_free = [sem(f"v_free{j}") for j in range(8)]
        xb_full = [sem(f"x_broadcast_full{j}") for j in range(2)]
        xb_free = [sem(f"x_broadcast_free{j}") for j in range(2)]
        s_dots = sem("dots_ready")
        s_gelu = sem("gelus_ready")
        s_wts = sem("expert_weights_ready")
        vo_free = sem("peer_out_free")
        s_conv = sem("conv_ready")
        w_high = [sem(f"high_weights{s}") for s in range(SLOTS)]
        w_split = [sem(f"split_weights{s}") for s in range(SLOTS)]
        s_scaled = sem("norm_scaled")
        s_x_hi = sem("high_input_ready")
        s_x_lo = sem("split_input_ready")
        s_hid_hi = sem("high_hidden_ready")
        s_hid = sem("split_hidden_ready")
        s_cvec = sem("conditioning_ready")
        s_kpe = sem("kpe_ready")
        s_kn = sem("k_normed")
        s_qn = sem("q_normed")
        s_qr = sem("q_rotated")
        s_kcat = sem("kpe_spread")
        s_out = sem("out_stored")

        def steps(eng, first, count, size=4):
            runs = count // size
            if runs >= 2:
                with eng.Fori(0, runs) as i:
                    for s in range(size):
                        yield i * size + (first + s), first + s, i
            else:
                runs = 0
            for s in range(runs * size, count):
                yield first + s, first + s, 0

        def slot_of(stage, s):
            return (CHUNK[stage] + s) % SLOTS

        def bank_of(stage, s):
            return (GROUP[stage] + s) % BANKS

        def wait_weights(eng, stage, s, i=0):
            c = CHUNK[stage] + s
            eng.wait_ge(w_landed[c % SLOTS], i * 16 + 16 * (c // SLOTS + 1))

        def wait_slot(eng, stage, s, i=0):
            c = CHUNK[stage] + s
            eng.wait_ge(w_free[c % SLOTS], i + (c // SLOTS + 1))

        def wait_full(eng, stage, s, i=0):
            g = GROUP[stage] + s
            eng.wait_ge(full[g % BANKS], i + (g // BANKS + 1))

        def wait_free(eng, stage, s, i=0):
            g = GROUP[stage] + s
            eng.wait_ge(free[g % BANKS], i + (g // BANKS + 1))

        def wait_emptied(eng, stage, s, i=0):
            g = GROUP[stage] + s
            eng.wait_ge(free[g % BANKS], i + (g // BANKS + 2))

        def split_of(stage, s):
            run, off = RUN_OF[stage]
            n = off + s
            b = (CHUNK[run] + n) % SLOTS
            return run, n, b, SPLIT_BEFORE[run][b] + n // SLOTS + 1

        def wait_all_emptied(eng, stage, n):
            for s in range(max(0, n - BANKS), n):
                wait_emptied(eng, stage, s)

        def at(a, n, lo, size):
            if isinstance(n, int):
                return a[:, n, lo:lo + size]
            return a[:, bass.ds(n, 1), lo:lo + size].rearrange("p a n -> p (a n)")

        def some(a, n, size):
            return a[:, n:n + size] if isinstance(n, int) else a[:, bass.ds(n, size)]

        def some2(a, n, size):
            return a[:, :, n:n + size] if isinstance(n, int) else a[:, :, bass.ds(n, size)]

        def turns_of(eng):
            for start, count, kind, first in TURNS:
                if count > 1:
                    with eng.Fori(0, count) as i:
                        yield i + start, i, start // 8, kind, first
                else:
                    yield start, 0, start // 8, kind, first

        block = ctx.enter_context(nc.Block())

        @block.sync
        def _(sp):
            def load(stage, s, i, src, shape):
                wait_slot(sp, stage, s, i)
                b = slot_of(stage, s)
                n = shape[0] * shape[1]
                sp.dma_start(ring[b][:, 0:n].rearrange("p (k n) -> p k n", k=shape[0]), src)\
                    .then_inc(w_landed[b], 16)

            def load_wide(stage, m, n, kt=KD, cols=WIDE, first=0):
                mv = m.rearrange("(k p) n -> p k n", p=P)
                for j, s, i in steps(sp, 0, n):
                    load(stage, s, i, mv[:, :, bass.ds(j * cols + first, cols)], (kt, cols))

            def load_deep(stage, m, n):
                mv = m.rearrange("(k p) n -> p k n", p=P)
                load(stage, 0, 0, mv[:, 0:2, :], (2, D))
                for j, s, i in steps(sp, 1, n - 2):
                    load(stage, s, i, mv[:, bass.ds(j * 2, 2), :], (2, D))
                load(stage, n - 1, 0, mv[:, 2 * n - 2:2 * n, :], (2, D))

            def load_ffn(up, down, layer):
                gv = w["ffn_w_gate_2"][layer].rearrange("(k p) n -> p k n", p=P)
                uv = w["ffn_w_up_2"][layer].rearrange("(k p) n -> p k n", p=P)
                for j, s, i in steps(sp, 0, 11, 2):
                    load(up, 2 * s, i, gv[:, :, bass.ds(j * WIDE, WIDE)], (KD, WIDE))
                    load(up, 2 * s + 1, i, uv[:, :, bass.ds(j * WIDE, WIDE)], (KD, WIDE))
                load_deep(down, w["ffn_w_down_2"][layer], 11)

            def load_layer0(s, first):
                load_wide(first, w["conv_w_in_2"][0], 12)
                load_wide(f"conv_out_{s}", w["conv_w_out_2"][0], 4)
                load_ffn(f"up_{s}", f"down_{s}", 0)

            for b in range(SLOTS - 1):
                sp.sem_inc(w_free[b], 1)

            def start(dst, src):
                sp.dma_start(dst, src).then_inc(s_start, 16)

            start(consts[:, :], consts_dram[:, 0:CCOLS["end"]])
            start(masks, consts_dram[:, CCOLS["end"]:CCOLS["all"]])
            start(x_tok, w["x"][0].rearrange("(a p) d -> p a d", p=P))
            for name, key, rows in (("norm1", "norm1_g", 8), ("norm2", "norm2_g", 8), ("mix", "norm_mix_g_2", 16),
                                    ("ffn", "norm_ffn_g_2", 16), ("q_lat", "mla_q_norm_g_2", 6),
                                    ("kv_lat", "mla_kv_norm_g_2", 2), ("conv_b", "conv_b_2", 8),
                                    ("c", "c_2", 8)):
                a = VROWS[name]
                start(vrows[a:a + rows, :], w[key].rearrange("l (k p) -> (l k) p", p=P))
            for name, key in (("final", "final_norm_g"), ("c_ctx", "c_ctx_2")):
                start(vrows[VROWS[name]:VROWS[name] + 8, :], w[key].rearrange("(k p) -> k p", p=P))
            start(vrows[VROWS["conv_k"]:VROWS["conv_k"] + 24, :],
                  w["conv_k_2"][0].rearrange("j (k p) -> (j k) p", p=P))
            start(brows[0:96, :], w["mod_b_2"].rearrange("l (k p) -> (l k) p", p=P))
            for name, a, b in (("qn", "mla_qn_nope_g_2", "mla_qn_rope_g_2"), ("kn", "mla_kn_nope_g_2", "mla_kn_rope_g_2")):
                r = VROWS[name]
                start(vrows[r:r + 1, 0:NOPE], w[a])
                start(vrows[r:r + 1, NOPE:QH], w[b])
                start(vrows[r:r + 1, QH:P], w[b])
            start(ctx_tok, w["ctx_2"][0].rearrange("(a p) d -> p a d", p=P))

            wi = w["w_in"][0].rearrange("(k p) n -> p k n", p=P)
            for s in range(12):
                load("qkv", s, 0, wi[:, :, s * WIDE:(s + 1) * WIDE], (KD, WIDE))
            load_wide("gates", w["w_in"][0], 8, first=12 * WIDE)
            load_wide("attention", w["mod_w_2"][0], MODS)
            for stage, key in (("out_moba", "w_out_moba"), ("out_sb", "w_out_sb")):
                mv = w[key][0].rearrange("(k p) n -> p k n", p=P)
                for s in range(2):
                    load(stage, s, 0, mv[:, :, s * 512:(s + 1) * 512], (4, 512))
            load_wide("mix", w["w_mix_out"][0], 4)
            load_wide("peer_q", w["peer_w_q"][0], 8)
            sp.wait_ge(s_mixed, 1)
            sp.dma_start(keys, w["peer_sub_keys"][0].rearrange("h b n c -> n (h b) c")).then_inc(s_keys, 16)
            load_wide("mod1", w["mod_w_2"][1], MODS)
            load_layer0("ctx", "early_ctx")
            load_layer0("lat", "conv_in_lat")
            load_wide("mla_in", w["mla_w_in_2"][0], 4)
            mv = w["mla_w_in_2"][0].rearrange("(k p) n -> p k n", p=P)
            load("mla_in", 4, 0, mv[:, :, QLAT + KVLAT:QLAT + KVLAT + ROPE], (KD, ROPE))
            mv = w["mla_w_kv_up_2"][0].rearrange("(k p) n -> p k n", p=P)
            for s in range(2):
                load("heads", s, 0, mv[:, :, 1024 * s:1024 * s + 1024], (2, 1024))
            mv = w["mla_w_q_up_2"][0].rearrange("(k p) n -> p k n", p=P)
            for s in range(8):
                load("heads", 2 + s, 0, mv[:, :, 2 * QH * s:2 * QH * (s + 1)], (6, 2 * QH))
            load_wide("mla_out", w["mla_w_out_2"][0], 4)
            load_ffn("up_1", "down_1", 1)
            wait_all_emptied(sp, "turn_out", 4)
            sp.dma_start(out_dram[0].rearrange("(a p) d -> p a d", p=P), out_tok).then_inc(s_out, 16)
            sp.wait_ge(s_out, 16)

        N_START = 16 * 22

        @block.gpsimd
        def _(pool):
            pool.wait_ge(s_split, 3)
            for n in range(16):
                for j in range(3):
                    lo = 32 * j + 16 * (n // 8)
                    nc.gpsimd.dma_start(xs[lo:lo + 16, n % 8, :], split[j][16 * (n % 8):16 * (n % 8) + 16, n // 8, :])\
                        .then_inc(s_xs, 16)
            pool.wait_ge(s_index, 3)
            pool.wait_ge(s_xs, 16 * 48)
            def stage_indices(half, it, done):
                for j in range(8):
                    pool.wait_ge(v_free[j], done)
                pool.sem_inc(s_turn, 1)
                nc.gpsimd.tensor_copy(idx8[:, half, :], idx_t[:, bass.ds(it * 16 + 8 * half, 8)]).then_inc(s_idx8, 1)
                pool.wait_ge(s_idx8, it * 2 + half + 1)
                pool.sem_inc(s_turn, 1)

            def fetch(table, s, dst, landed):
                at = bass.IndirectOffsetOnAxis(ap=idx8[:, s // 8, s % 8:s % 8 + 1], axis=0)
                nc.gpsimd.indirect_dma_start(out=dst, out_offset=None, in_=w[table][0], in_offset=at)\
                    .then_inc(landed, 16)

            def fetch_u(s, it):
                pool.wait_ge(xb_free[1], it * 16 + s + 1)
                pool.sem_inc(s_turn, 1)
                fetch("peer_u", s, ubuf[s % 4], u_landed[s % 4])

            def fetch_v(s, it):
                pool.wait_ge(v_free[s % 8], it * 2 + s // 8 + 2)
                pool.sem_inc(s_turn, 1)
                fetch("peer_v", s, vbuf[s % 8], v_landed[s % 8])

            def turn_of(it, last):
                for s in range(16):
                    if s == 4:
                        stage_indices(1, it, it * 2 + 2)
                    if s == 12 and not last:
                        stage_indices(0, it + 1, it * 2 + 3)
                    fetch_v(s, it)
                    if s < 12:
                        fetch_u(s + 4, it)
                    elif not last:
                        fetch_u(s - 12, it + 1)

            stage_indices(0, 0, 1)
            for s in range(4):
                fetch_u(s, 0)
            with pool.Fori(0, 15) as it:
                turn_of(it, False)
            turn_of(15, True)
            pool.wait_ge(s_kpe, 1)
            nc.gpsimd.tensor_copy(kcat[NOPE:QH], kpe[NOPE:QH, :].unsqueeze(1).to_broadcast([ROPE, MH, 2 * T]))\
                .then_inc(s_kcat, 1)

        @block.tensor
        def _(pe):
            for j in range(8):
                pe.sem_inc(v_free[j], 2)

            def product(stage, rhs, kt, i, s, cols=WIDE, width=T, group=None, quarter=None):
                wt = ring[slot_of(stage, s)][:, 0:kt * cols].rearrange("p (k n) -> p k n", k=kt)
                g = s if group is None else group
                wait_weights(pe, stage, s, i)
                wait_free(pe, stage, g, i)
                b = bank[bank_of(stage, g)]
                for m in range(cols // P):
                    for k in range(kt):
                        mm = nc.tensor.matmul(b[:, m * width:(m + 1) * width], wt[:, k, m * P:(m + 1) * P],
                                              rhs(k), start=(k == 0), stop=(k == kt - 1))
                        if m == k == 0:
                            opens(stage, s, mm)
                        if quarter and k % 4 == 3 and m * kt + k + 1 < 16:
                            quarter((m * kt + k + 1) // 4)
                mm.then_inc(full[bank_of(stage, g)], 1)

            def opens(stage, s, mm):
                mm.then_inc(w_free[(CHUNK[stage] + s - 1) % SLOTS], 1)

            def products(stage, rhs, n, kt=KD):
                for j, s, i in steps(pe, 0, n):
                    product(stage, rhs, kt, i, s)

            def turns(stage, g, pieces):
                wait_free(pe, stage, g)
                b = bank[bank_of(stage, g)]
                for col, src in pieces:
                    n, m = src.shape[0], src.shape[1]
                    mm = nc.tensor.transpose(b[0:m, col:col + n], src, ident[0:n, 0:n])
                mm.then_inc(full[bank_of(stage, g)], 1)

            def norm(r, stage, kt=KD, width=T, src=None):
                pe.wait_ge(s_sq, r + 1)
                wait_free(pe, stage, 0)
                b = bank[bank_of(stage, 0)]
                for k in range(kt):
                    mm = nc.tensor.matmul(b[:, 0:width], ones[:, 0:P], sq[:, k, 0:T] if src is None else src(k),
                                          start=(k == 0), stop=(k == kt - 1))
                mm.then_inc(full[bank_of(stage, 0)], 1)

            def three(out, hi, lo, b, cut, start, stop, **more_args):
                first = nc.tensor.matmul(out, cut(w_hi[b]), hi, start=start, stop=False, **more_args)
                nc.tensor.matmul(out, cut(w_lo[b]),
                                 hi, start=False, stop=False, **more_args)
                return first, nc.tensor.matmul(out, cut(w_hi[b]), lo, start=False, stop=stop, **more_args)

            def product_split(stage, i, s, n=None):
                _, _, slot, count = split_of(stage, s)
                pe.wait_ge(w_split[slot], i + count)
                wait_free(pe, stage, s, i)
                b = bank[bank_of(stage, s)]
                for m in range(2):
                    for k in range(KD):
                        if n is not None and m == 0:
                            pe.wait_ge(s_x_lo, KD * n + k + 1)
                        first, mm = three(
                            b[:, m * T:(m + 1) * T], x_hi[:, k, :], x_lo[:, k, :], slot,
                            lambda a: a.rearrange("p (k n) -> p k n", k=KD)[:, k, m * P:(m + 1) * P],
                            k == 0, k == KD - 1)
                        if m == k == 0:
                            opens(stage, s, first)
                mm.then_inc(full[bank_of(stage, s)], 1)

            def down_chunk_split(stage, j, s, i, first, last):
                _, _, slot, count = split_of(stage, s)
                pe.wait_ge(w_split[slot], i + count)
                for k in range(2):
                    for m in range(KD):
                        b = bank_of(stage, m // 2)
                        begun, mm = three(
                            bank[b][:, (m % 2) * T:(m % 2) * T + T], at(hid_hi, j * 2 + k, 0, T),
                            at(hid_lo, j * 2 + k, 0, T), slot,
                            lambda a: a.rearrange("p (k n) -> p k n", k=2)[:, k, m * P:(m + 1) * P],
                            first and k == 0 and m % 2 == 0, last and k == 1, skip_group_check=True)
                        if m == k == 0:
                            opens(stage, s, begun)
                        if last and k == 1 and m % 2 == 1:
                            mm.then_inc(full[b], 1)

            def ffn_split(up, dn, n):
                for j, s, i in steps(pe, 0, 11, 2):
                    for half in range(2):
                        product_split(up, i, 2 * s + half, n + 2 if s == half == 0 else None)
                wait_all_emptied(pe, up, 22)
                pe.wait_ge(s_hid, 2 + 11 * (n + 1))
                down_opens(dn)
                down_chunk_split(dn, 0, 0, 0, True, False)
                for j, s, i in steps(pe, 1, 9):
                    down_chunk_split(dn, j, s, i, False, False)
                down_chunk_split(dn, 10, 10, 0, False, True)

            def down_opens(stage):
                for g in range(4):
                    wait_free(pe, stage, g)

            def down_chunk(stage, j, s, i, first, last, quarter=None):
                wait_weights(pe, stage, s, i)
                wt = ring[slot_of(stage, s)].rearrange("p (k n) -> p k n", k=2)
                for k in range(2):
                    for m in range(KD):
                        b = bank_of(stage, m // 2)
                        mm = nc.tensor.matmul(
                            bank[b][:, (m % 2) * T:(m % 2) * T + T], wt[:, k, m * P:(m + 1) * P],
                            at(hid, j * 2 + k, 0, T),
                            start=(first and k == 0 and m % 2 == 0), stop=(last and k == 1),
                            skip_group_check=True)
                        if m == k == 0:
                            opens(stage, s, mm)
                        if last and k == 1 and m % 2 == 1:
                            mm.then_inc(full[b], 1)
                        if quarter and m % 4 == 3 and k * KD + m + 1 < 16:
                            quarter((k * KD + m + 1) // 4)

            def mod_chunk(stage, s, i=0, group=None):
                g = s if group is None else group
                wait_weights(pe, stage, s, i)
                wait_free(pe, stage, g, i)
                wt = ring[slot_of(stage, s)].rearrange("p (k n) -> p k n", k=KD)
                for k in range(KD):
                    mm = nc.tensor.matmul(bank[bank_of(stage, g)][0:2, 0:WIDE], cvec[:, k, :], wt[:, k, :],
                                          start=(k == 0), stop=(k == KD - 1))
                    if k == 0:
                        opens(stage, s, mm)
                mm.then_inc(full[bank_of(stage, g)], 1)

            def mod_turn(stage, s, layer, j, i=0, group=None):
                wait_emptied(pe, stage, s if group is None else group, i)
                for m in range(2):
                    mm = nc.tensor.matmul(sbank[3][:, bass.ds(j * 4 + 96 * layer + 2 * m, 2)],
                                          mrow[:, s % 4, m * P:(m + 1) * P], ident[0:2, 0:2], start=True, stop=True)
                mm.then_inc(s_mod, 1)

            def lat(k):
                return nrm[:, k, T:2 * T]

            def con(k):
                return nrm[:, k, 0:T]

            pe.wait_ge(s_start, N_START)
            turns("vectors", 0, [(0, vrows[0:VROWS["end"], :])])
            turns("vectors", 1, [(0, brows[0:96, :])])
            for stage, src in (("turn_x", x_tok), ("turn_ctx", ctx_tok)):
                for g in range(4):
                    turns(stage, g, [(256 * a + 128 * t, src[:, t, (2 * g + a) * P:(2 * g + a + 1) * P])
                                     for a in range(2) for t in range(2)])

            norm(0, "norm1")
            for s in range(12):
                if s % 6 < 4:
                    product_split("qkv", 0, s, 0 if s == 0 else None)
                else:
                    _, _, slot, count = split_of("qkv", s)
                    pe.wait_ge(w_split[slot], count)
                    wait_free(pe, "qkv", s)
                    high, low = (a[slot].rearrange("p (k n) -> p k n", k=KD) for a in (w_hi, w_lo))
                    for t in range(2):
                        out = bank[bank_of("qkv", s)][:, t * WIDE:(t + 1) * WIDE]
                        here = slice(t * P, (t + 1) * P)
                        for k in range(KD):
                            mm = nc.tensor.matmul(out, x_hi[:, k, here], high[:, k, :], start=(k == 0), stop=False)
                            if t == k == 0:
                                opens("qkv", s, mm)
                            nc.tensor.matmul(out, x_lo[:, k, here], high[:, k, :], start=False, stop=False)
                            mm = nc.tensor.matmul(out, x_hi[:, k, here], low[:, k, :], start=False, stop=(k == KD - 1))
                    mm.then_inc(full[bank_of("qkv", s)], 1)
            for j, s, i in steps(pe, 0, 8):
                product_split("gates", i, s)

            wait_all_emptied(pe, "qkv", 12)
            pe.wait_ge(s_cvec, 2)
            for s in range(HALVES + 3):
                if s < HALVES:
                    b, kind, h = s % 3, s // HEADS, s % HEADS
                    pe.wait_ge(sc_free[b], s // 3 + 1)
                    lo = DH * (h % 2)
                    for t in range(2):
                        mm = nc.tensor.matmul(sbank[b][:, t * T:(t + 1) * T],
                                              qk[lo:lo + DH, 8 * kind + h // 2, t * P:(t + 1) * P],
                                              qk[lo:lo + DH, 8 * kind + 4 + h // 2, :], start=True, stop=True)
                    mm.then_inc(sc_full[b], 1)
                for j in MOD_STEP[s]:
                    mod_chunk("attention", j, group=ATT.index(("mod", j)))
                    if j:
                        mod_turn("attention", j - 1, 0, j - 1, group=ATT.index(("mod", j - 1)))
                if 2 <= s < HALVES + 2:
                    n = s - 2
                    if n < HEADS:
                        pe.wait_ge(s_prob_v, n + 1)
                    else:
                        pe.wait_ge(s_prob_s, n - HEADS + 1)
                    turns("attention", ATT.index(("turn", n)),
                          [(256 * a + 128 * t, prob[:, n % 3, t, a * P:(a + 1) * P])
                           for a in range(2) for t in range(2)])
                if s >= 3:
                    n = s - 3
                    kind, h = n // HEADS, n % HEADS
                    g = ATT.index(("value", n // 2))
                    b = bank[bank_of("attention", g)]
                    wait_emptied(pe, "attention", ATT.index(("turn", n)))
                    if n % 2 == 0:
                        wait_free(pe, "attention", g)
                    lo = DH * (n % 2)
                    for a in range(2):
                        mm = nc.tensor.matmul(b[lo:lo + DH, 0:T], vtok[:, a, 512 * kind + DH * h:512 * kind + DH * h + DH],
                                              prob_t[:, n % 2, a, :], start=(a == 0), stop=(a == 1))
                    if n % 2 == 1:
                        mm.then_inc(full[bank_of("attention", g)], 1)

            mod_turn("attention", MODS - 1, 0, MODS - 1, group=ATT.index(("mod", MODS - 1)))
            wait_all_emptied(pe, "attention", len(ATT))
            for n, stage in enumerate(("out_moba", "out_sb")):
                for s in range(2):
                    wt = ring[slot_of(stage, s)].rearrange("p (k n) -> p k n", k=4)
                    wait_weights(pe, stage, s)
                    for g in range(2 * s, 2 * s + 2):
                        wait_free(pe, stage, g)
                        for m in range(2):
                            col = (g % 2) * 256 + m * P
                            for k in range(4):
                                mm = nc.tensor.matmul(bank[bank_of(stage, g)][:, m * T:(m + 1) * T],
                                                      wt[:, k, col:col + P], o_t[:, 4 * n + k, :],
                                                      start=(k == 0), stop=(k == 3))
                                if g == 2 * s and m == k == 0:
                                    opens(stage, s, mm)
                        mm.then_inc(full[bank_of(stage, g)], 1)
            pe.wait_ge(s_mixed, 1)
            products("mix", lambda k: gate[:, k, :], 4)

            norm(1, "norm2")
            pe.wait_ge(s_norm, 2)
            products("peer_q", lat, 8)
            pe.wait_ge(s_keys, 16)
            norm(2, "mixnorm_ctx")
            for g in range(4):
                turns("turn_keys", g, [(P * a, keys[:, 4 * g + a, :]) for a in range(4)])
            wait_all_emptied(pe, "peer_q", 8)
            wait_all_emptied(pe, "turn_keys", 4)
            for g in range(8):
                t, n = g // 4, g % 4
                wait_free(pe, "peer_scores", g)
                for a in range(4):
                    mm = nc.tensor.matmul(bank[bank_of("peer_scores", g)][:, a * P:(a + 1) * P],
                                          pq[:, 4 * n + a, t * P:(t + 1) * P], keys_t[:, 4 * n + a, :],
                                          start=True, stop=True)
                mm.then_inc(full[bank_of("peer_scores", g)], 1)
            for g in range(4):
                turns("turn_x2", g, [(P * a, lat(4 * (g % 2) + a)[:, (g // 2) * P:(g // 2) * P + P]) for a in range(4)])

            for j, s, i in steps(pe, 0, MODS):
                mod_chunk("mod1", s, i)
                if s % 4:
                    mod_turn("mod1", s - 1, 1, j - 1, i)
                if s % 4 == 3:
                    mod_turn("mod1", s, 1, j, i)

            pe.wait_ge(s_norm, 3)
            for s in range(2):
                product("early_ctx", con, KD, 0, s)
            pe.wait_ge(s_chosen, 1)
            turns("turn_chosen", 0, [(P * t, chosen[:, t, :]) for t in range(2)]
                  + [(256 + P * t, shifted[:, t].rearrange("p h k -> p (h k)")) for t in range(2)])
            pe.wait_ge(s_xs, 16 * 48)
            for s in range(2):
                product("late_ctx", con, KD, 0, s)

            vo = wide[1]

            def gather(it, i, half, kind, first):
                def spread(s):
                    for c in range(2):
                        pe.wait_ge(xb_free[c], it * 16 + s + (1 if c == 0 else 4))
                        nc.tensor.matmul(sbank[c], sel[:, 16 * half + s, :],
                                         at(xs, it - 8 * half, 512 * c, 512), start=True, stop=True)\
                            .then_inc(xb_full[c], 1)

                def experts(s):
                    if s == 0:
                        pe.wait_ge(vo_free, it + 1)
                    if s % 4 == 0:
                        pe.wait_ge(s_wts, it * 4 + s // 4 + 1)
                    pe.wait_ge(v_landed[s % 8], (it * 2 + s // 8 + 1) * 16)
                    for c in range(2):
                        mm = nc.tensor.matmul(vo[0:16, 512 * c:512 * c + 512], wts[:, 16 * s:16 * s + 16],
                                              vbuf[s % 8][:, 512 * c:512 * c + 512],
                                              start=(s == 0), stop=(s == 15))
                    mm.then_inc(v_free[s % 8], 1)

                def both(quad):
                    for s in range(4 * quad, 4 * quad + 4):
                        spread(s)
                        experts(s - 4)

                def extra(k, quarter=None):
                    s = first + k
                    if kind == "conv_in":
                        product("conv_in_ctx", con, KD, i, s, quarter=quarter)
                        return True
                    if kind == "conv_out":
                        if k == 0:
                            pe.wait_ge(s_conv, 1)
                        product("conv_out_ctx", lambda n: cproj[:, n, :], KD, 0, s, quarter=quarter)
                        return True
                    if kind == "norm" and k == 0:
                        norm(3, "ffnnorm_ctx")
                    if kind == "up" and s < 22:
                        if s == 0:
                            pe.wait_ge(s_norm, 4)
                        product("up_ctx", con, KD, i, s, quarter=quarter)
                        return True
                    if kind == "down" and s < 11 and (s > 0 or k == 0) and (first > 0 or k == 0):
                        if s == 0:
                            wait_all_emptied(pe, "up_ctx", 22)
                            down_opens("down_ctx")
                        down_chunk("down_ctx", i * 4 + s, s, i, s == 0, s == 10, quarter=quarter)
                        return True
                    return False

                spread(0)
                if not extra(0, spread):
                    for s in range(1, 4):
                        spread(s)
                both(1)
                extra(1)
                both(2)
                both(3)
                extra(2)
                for s in range(12, 16):
                    experts(s)
                extra(3)
                pe.wait_ge(s_vo, it + 1)
                for m in range(KD):
                    mm = nc.tensor.matmul(vo[:, 16 * m:16 * m + 16], rows16[:, m * P:(m + 1) * P], ident[0:16, 0:16],
                                          start=True, stop=True)
                mm.then_inc(vo_full, 1)

            pe.wait_ge(s_index, 3)
            for it, i, half, kind, first in turns_of(pe):
                gather(it, i, half, kind, first)
            pe.wait_ge(vo_free, 17)

            norm(4, "norm_final")
            norm(5, "mixnorm_lat")
            for j, s, i in steps(pe, 0, 12):
                product_split("conv_in_lat", i, s, 1 if s == 0 else None)
            norm(6, "mixnorm1_ctx")
            pe.wait_ge(s_conv, 2)
            products("conv_out_lat", lambda k: cproj[:, k, :], 4)
            norm(7, "ffnnorm_lat")
            ffn_split("up_lat", "down_lat", 0)

            norm(8, "mixnorm1_lat")
            pe.wait_ge(s_norm, 9)
            for s in range(3):
                product("mla_in", lat, KD, 0, s)
            wait_weights(pe, "mla_in", 3)
            wt = ring[slot_of("mla_in", 3)].rearrange("p (k n) -> p k n", k=KD)
            for m in range(2):
                wait_free(pe, "mla_in", 3 + m)
                for k in range(KD):
                    mm = nc.tensor.matmul(bank[bank_of("mla_in", 3 + m)][:, :], wt[:, k, m * P:(m + 1) * P],
                                          nrm[:, k, :], start=(k == 0), stop=(k == KD - 1))
                    if m == k == 0:
                        opens("mla_in", 3, mm)
                mm.then_inc(full[bank_of("mla_in", 3 + m)], 1)
            wait_weights(pe, "mla_in", 4)
            wait_free(pe, "mla_in", 5)
            wt = ring[slot_of("mla_in", 4)][:, 0:KD * ROPE].rearrange("p (k n) -> p k n", k=KD)
            for k in range(KD):
                mm = nc.tensor.matmul(bank[bank_of("mla_in", 5)][NOPE:QH, :], wt[:, k, :], nrm[:, k, :],
                                      start=(k == 0), stop=(k == KD - 1))
                if k == 0:
                    opens("mla_in", 4, mm)
            mm.then_inc(full[bank_of("mla_in", 5)], 1)

            def square_wide(k):
                return sq[:, 2 * k:2 * k + 2, :].rearrange("p a t -> p (a t)")

            norm(9, "qlat_norm", 6)
            norm(10, "kvlat_norm", 2, 2 * T, square_wide)
            pe.wait_ge(s_sq, 12)
            wait_free(pe, "kpe_norm", 0)
            nc.tensor.matmul(bank[bank_of("kpe_norm", 0)][NOPE:QH, :], mean[NOPE:QH, NOPE:QH],
                             square_wide(0)[NOPE:QH, :], start=True, stop=True)\
                .then_inc(full[bank_of("kpe_norm", 0)], 1)
            pe.wait_ge(s_norm, 12)
            wait_free(pe, "kpe_turn", 0)
            nc.tensor.matmul(bank[bank_of("kpe_turn", 0)][NOPE:QH, 0:T], turn[NOPE:QH, NOPE:QH],
                             kpe[NOPE:QH, T:2 * T], start=True, stop=True)\
                .then_inc(full[bank_of("kpe_turn", 0)], 1)
            for g, (kind, n) in enumerate(HEAD):
                if kind in ("key_mean", "query_mean"):
                    wait_emptied(pe, "heads", HEAD.index((kind.split("_")[0], n)))
                if kind == "query_turn":
                    pe.wait_ge(s_qn, n + 1)
                wait_free(pe, "heads", g)
                b = bank[bank_of("heads", g)]
                if kind in ("key", "value"):
                    s = n // 8 if kind == "key" else n // 4
                    wait_weights(pe, "heads", s)
                    wt = ring[slot_of("heads", s)].rearrange("p (k n) -> p k n", k=2)
                if kind == "key":
                    at_n = P * (n % 8)
                    for k in range(2):
                        mm = nc.tensor.matmul(b[0:NOPE, :], wt[:, k, at_n:at_n + NOPE], kvlat[:, k, :],
                                              start=(k == 0), stop=(k == 1))
                        if n % 8 == k == 0:
                            opens("heads", s, mm)
                if kind == "value":
                    t = n % 4
                    for k in range(2):
                        mm = nc.tensor.matmul(b[:, :], kvlat[:, k, t * P:(t + 1) * P],
                                              wt[:, k, :].rearrange("p (h c) -> p h c", h=8)[:, :, NOPE:P],
                                              start=(k == 0), stop=(k == 1))
                if kind == "query":
                    wait_weights(pe, "heads", 2 + n)
                    wt = ring[slot_of("heads", 2 + n)][:, 0:12 * QH].rearrange("p (k n) -> p k n", k=6)
                    for m in range(2):
                        for k in range(6):
                            mm = nc.tensor.matmul(b[0:QH, m * T:(m + 1) * T], wt[:, k, m * QH:(m + 1) * QH],
                                                  qlat[:, k, :], start=(k == 0), stop=(k == 5))
                            if m == k == 0:
                                opens("heads", 2 + n, mm)
                if kind in ("key_mean", "query_mean"):
                    rows = NOPE if kind == "key_mean" else QH
                    mm = nc.tensor.matmul(b[0:rows, :], mean[0:rows, 0:rows],
                                          squares[0:rows, SQUARE[(kind.split("_")[0], n)] % 12, :],
                                          start=True, stop=True)
                if kind == "query_turn":
                    mm = nc.tensor.matmul(b[0:QH, :], turn[0:QH, 0:QH],
                                          q[0:QH, 2 * n:2 * n + 2, :].rearrange("p a t -> p (a t)"), start=True, stop=True)
                mm.then_inc(full[bank_of("heads", g)], 1)
            pe.wait_ge(s_qr, 8)
            pe.wait_ge(s_kn, MH)
            pe.wait_ge(s_kcat, 1)
            for s in range(MH + 2):
                if s < MH:
                    for t in range(2):
                        n = 2 * s + t
                        pe.wait_ge(sc_free[n % 4], SCORED[n % 4] + n // 4 + 1)
                        nc.tensor.matmul(sbank[n % 4], q[0:QH, s, t * P:(t + 1) * P], kcat[0:QH, s, :],
                                         start=True, stop=True).then_inc(sc_full[n % 4], 1)
                if s >= 2:
                    n = s - 2
                    g = MATT.index(("value", n // 2))
                    b = bank[bank_of("mla_attention", g)]
                    for half in range(2):
                        wait_emptied(pe, "mla_attention", MATT.index(("turn", 2 * n + half)))
                    if n % 2 == 0:
                        wait_free(pe, "mla_attention", g)
                    lo = MV * (n % 2)
                    for a in range(4):
                        mm = nc.tensor.matmul(b[lo:lo + MV, 0:T], vmla[:, a, MV * n:MV * n + MV], mprob_t[:, n % 2, a, :],
                                              start=(a == 0), stop=(a == 3))
                    if n % 2 == 1:
                        mm.then_inc(full[bank_of("mla_attention", g)], 1)
                if 1 <= s <= MH:
                    n = s - 1
                    pe.wait_ge(s_prob_v, HEADS + n + 1)
                    for half in range(2):
                        turns("mla_attention", MATT.index(("turn", 2 * n + half)),
                              [(256 * a + 128 * t, mprob[:, n % 2, t, (2 * half + a) * P:(2 * half + a + 1) * P])
                               for a in range(2) for t in range(2)])
            wait_all_emptied(pe, "mla_attention", len(MATT))
            products("mla_out", lambda k: o_mla[:, k, :], 4)
            norm(12, "ffnnorm1")
            ffn_split("up_1", "down_1", 1)
            wait_all_emptied(pe, "down_1", 4)
            for g in range(4):
                turns("turn_out", g, [(P * a, h_lat[:, 4 * (g % 2) + a, (g // 2) * P:(g // 2) * P + P]) for a in range(4)])

        @block.scalar
        def _(act):
            for b in range(BANKS):
                act.sem_inc(free[b], 1)
            act.sem_inc(vo_free, 1)

            def leave(stage, g, dst, i=0, cols=slice(0, 512), rows=slice(0, P), func=ACT.Copy, scale=1.0, bias=None):
                wait_full(act, stage, g, i)
                b = bank_of(stage, g)
                src = bank[b][rows, cols]
                if len(dst.shape) == 3:
                    src = src.rearrange("p (a n) -> p a n", a=dst.shape[1])
                more_args = {} if bias is None else {"bias": bias}
                nc.scalar.activation(dst, src, func, scale=scale, **more_args).then_inc(free[b], 1)

            def leaves(stage, n, dst, per=2, **kw):
                for j, s, i in steps(act, 0, n):
                    where = bass.ds(j * per, per) if not isinstance(j, int) else slice(j * per, j * per + per)
                    leave(stage, s, dst[:, where, :], i, **kw)

            def root(stage, d, width=T, rows=slice(0, P), slot=0):
                leave(stage, 0, std[rows, slot, 0:width], cols=slice(0, width), rows=rows,
                      func=ACT.Sqrt, scale=1.0 / d, bias=eps[rows, :])

            def high(stage, s, i=0):
                run, n, b, _ = split_of(stage, s)
                wait_weights(act, run, n, i)
                nc.scalar.activation(w_hi[b][:, :], ring[b][:, :], ACT.Copy).then_inc(w_high[b], 1)

            def high_input(n, shift):
                for k in range(KD):
                    act.wait_ge(s_scaled, KD * n + k + 1)
                    if shift is None:
                        nc.scalar.activation(x_hi[:, k, :], nrm[:, k, T:2 * T], ACT.Copy).then_inc(s_x_hi, 1)
                    else:
                        nc.scalar.activation(x_hi[:, k, :], nrm[:, k, T:2 * T], ACT.Identity, bias=shift(k))\
                            .then_inc(s_x_hi, 1)

            def gated(up, dn, n):
                for j, s, i in steps(act, 0, 11, 2):
                    high(up, 2 * s + 3, i)
                    high(up, 2 * s + 4, i)
                    act.wait_ge(s_hid, j + (11 * n + 1))
                    leave(up, 2 * s, hid_raw[:, s % 2], i, func=ACT.Silu)
                for j, s, i in steps(act, 3, 8):
                    high(dn, s, i)

            leave("vectors", 0, vec[:, :], cols=slice(0, VROWS["end"]))
            leave("vectors", 1, modb[:, :], cols=slice(0, 96))
            leaves("turn_x", 4, h_lat)
            leaves("turn_ctx", 4, h_ctx)
            wait_emptied(act, "vectors", 0)
            for s, name in enumerate(("c", "c_ctx")):
                nc.scalar.activation(cvec[:, :, s], vec[:, VROWS[name]:VROWS[name] + 8], ACT.Silu).then_inc(s_cvec, 1)
            for s in range(3):
                high("qkv", s)
            root("norm1", D)
            high_input(0, None)
            for s in range(12):
                kind, n = s // 6, s % 6
                high("qkv", s + 3)
                if n < 4:
                    leave("qkv", s, qk[:, 8 * kind + 2 * n:8 * kind + 2 * n + 2, :], scale=DH ** -0.5 if n < 2 else 1.0)
                else:
                    at = 512 * kind + 256 * (n - 4)
                    leave("qkv", s, vtok[:, :, at:at + 256])
            for s in range(8):
                if s + 3 < 8:
                    high("gates", s + 3)
                leave("gates", s, gate[:, 2 * s:2 * s + 2, :], func=ACT.Sigmoid)

            def mod_rows(stage, s, i=0, group=None, done=None):
                if done is not None:
                    act.wait_ge(s_mod, done)
                leave(stage, s if group is None else group, mrow[:, s % 4, :], i, cols=slice(0, WIDE), rows=slice(0, 2))

            for s in range(HALVES + 3):
                for j in MOD_STEP[s]:
                    mod_rows("attention", j, group=ATT.index(("mod", j)), done=j - 3 if j >= 4 else None)
                if s < HALVES:
                    act.wait_ge(s_soft_in, s + 1)
                    if s < HEADS:
                        for t in range(2):
                            last = nc.scalar.activation(prob[:, s % 3, t, :], logit[:, s % 3, t, :], ACT.Exp,
                                                        bias=small[:, s, t:t + 1], accum_out=small[:, s, 2 + t:3 + t])
                        last.then_inc(s_soft_exp, 1)
                    else:
                        nc.scalar.activation(expo[:, s % 3], expo[:, s % 3], ACT.Exp).then_inc(a_step, 1)
                        act.wait_ge(a_step, s - HEADS + 1)
                        nc.scalar.activation(soft[:, s % 3], expo[:, s % 3], ACT.Ln, bias=ones[:, 0:1])\
                            .then_inc(s_soft_exp, 1)
                if HEADS < s <= HALVES:
                    n = s - 1
                    act.wait_ge(s_arg, n - HEADS + 1)
                    nc.scalar.activation(prob[:, n % 3], logit[:, n % 3], ACT.Exp).then_inc(s_prob_s, 1)
                if 2 <= s < HALVES + 2:
                    leave("attention", ATT.index(("turn", s - 2)), prob_t[:, (s - 2) % 2])
                if s >= 3 and (s - 3) % 2 == 1:
                    leave("attention", ATT.index(("value", (s - 3) // 2)), o_t[:, (s - 3) // 2, :], cols=slice(0, T))

            root("norm2", D)
            leaves("peer_q", 8, pq)
            root("mixnorm_ctx", D)
            for g in range(4):
                leave("turn_keys", g, keys_t[:, 4 * g:4 * g + 4, :])
            for g in range(8):
                leave("peer_scores", g, score[:, g // 4, 4 * (g % 4):4 * (g % 4) + 4, :])
            for g in range(4):
                leave("turn_x2", g, x2_tok[:, g // 2, 512 * (g % 2):512 * (g % 2) + 512])
            for j, s, i in steps(act, 0, MODS):
                mod_rows("mod1", s, i, done=i * 4 + (MODS + s - 3))
            act.wait_ge(s_xs, 16 * 48)
            leave("early_ctx", 0, cproj[:, 0:2, :])
            act.wait_ge(s_shift, 1)
            nc.scalar.activation(shifted, shifted, ACT.Exp).then_inc(s_pexp, 1)
            leave("early_ctx", 1, cproj[:, 2:4, :])
            for s in range(2):
                leave("late_ctx", s, cproj[:, 2 * s + 4:2 * s + 6, :])

            def gather(it, i, half, kind, first):
                def gelu(quad):
                    act.wait_ge(s_dots, it * 4 + quad + 1)
                    nc.scalar.activation(gelus[:, 4 * quad:4 * quad + 4], dots[:, 4 * quad:4 * quad + 4], ACT.Gelu)\
                        .then_inc(s_gelu, 1)

                def extra(k):
                    s = first + k
                    if kind == "conv_in":
                        leave("conv_in_ctx", s, some(cproj, (i * 4 + s + 4) * 2, 2), i)
                    if kind == "norm" and k == 0:
                        root("ffnnorm_ctx", D)
                    if kind == "up" and s < 22 and k % 2 == 0:
                        leave("up_ctx", s, some(hid, i * 4 + s, 2), i, func=ACT.Silu)

                gelu(0)
                extra(0)
                gelu(1)
                extra(1)
                gelu(2)
                gelu(3)
                extra(2)
                act.wait_ge(v_free[7], it * 2 + 4)
                nc.scalar.activation(rows16[:, :], wide[1][0:16, :], ACT.Copy).then_inc(s_vo, 1)
                extra(3)
                act.wait_ge(vo_full, it + 1)
                nc.scalar.activation(some2(peer, it * 16, 16), wide[1][:, 0:P].rearrange("p (m t) -> p m t", m=KD),
                                     ACT.Copy).then_inc(vo_free, 1)

            for it, i, half, kind, first in turns_of(act):
                gather(it, i, half, kind, first)

            for s in range(3):
                high("conv_in_lat", s)
            root("norm_final", D)
            root("mixnorm_lat", D)
            high_input(1, lambda k: mod[:, 0, k, 0:1])
            for j, s, i in steps(act, 0, 8):
                high("conv_in_lat", s + 3, i)
                leave("conv_in_lat", s, some(cproj, j * 2, 2), i)
            high("conv_in_lat", 11)
            for s in range(8, 12):
                leave("conv_in_lat", s, cproj[:, 2 * s:2 * s + 2, :])
            root("mixnorm1_ctx", D)
            for s in range(3):
                high("up_lat", s)
            root("ffnnorm_lat", D)
            high_input(2, lambda k: mod[:, 0, 24 + k, 0:1])
            gated("up_lat", "down_lat", 0)

            root("mixnorm1_lat", D)
            for s in range(3):
                leave("mla_in", s, qlat[:, 2 * s:2 * s + 2, :])
            for m in range(2):
                leave("mla_in", 3 + m, kvlat[:, m, :])
            leave("mla_in", 5, kpe[NOPE:QH, :], rows=slice(NOPE, QH))
            root("qlat_norm", QLAT)
            root("kvlat_norm", KVLAT, 2 * T)
            root("kpe_norm", 1.0, 2 * T, slice(NOPE, QH))
            for g, (kind, n) in enumerate(HEAD):
                if kind == "value":
                    leave("heads", g, vmla[:, n % 4, 512 * (n // 4):512 * (n // 4) + 512])
                if kind in ("key", "query"):
                    wait_full(act, "heads", g)
                    b = bank_of("heads", g)
                    rows = slice(0, NOPE if kind == "key" else QH)
                    dst = kcat[rows, n, :] if kind == "key" else q[rows, 2 * n:2 * n + 2, :].rearrange("p a t -> p (a t)")
                    nc.scalar.activation(dst, bank[b][rows, :], ACT.Copy)
                    nc.scalar.activation(squares[rows, SQUARE[(kind, n)] % 12, :], bank[b][rows, :], ACT.Square)\
                        .then_inc(free[b], 1)
                if kind in ("key_mean", "query_mean"):
                    rows = slice(0, NOPE if kind == "key_mean" else QH)
                    m = n if kind == "key_mean" else MH + n
                    if m >= 2:
                        act.wait_ge(s_kn if m - 2 < MH else s_qn, m - 1 if m - 2 < MH else m - 1 - MH)
                    leave("heads", g, std[rows, m % 2, :], rows=rows, func=ACT.Sqrt, bias=eps[rows, :])
            for s in range(MH + 2):
                if s < MH:
                    act.wait_ge(s_soft_in, HALVES + s + 1)
                    for t in range(2):
                        n = 2 * s + t
                        nc.scalar.activation(mprob[:, s % 2, t, :], sbank[n % 4], ACT.Exp, scale=QH ** -0.5,
                                             bias=msmall[:, s, t:t + 1], accum_out=msmall[:, s, 2 + t:3 + t])\
                            .then_inc(sc_free[n % 4], 1)
                if s >= 2 and s % 2 == 1:
                    leave("mla_attention", MATT.index(("value", (s - 2) // 2)), o_mla[:, (s - 2) // 2, :],
                          cols=slice(0, T))
                if 1 <= s <= MH:
                    for half in range(2):
                        leave("mla_attention", MATT.index(("turn", 2 * (s - 1) + half)),
                              mprob_t[:, (s - 1) % 2, 2 * half:2 * half + 2, :])
            for s in range(3):
                high("up_1", s)
            root("ffnnorm1", D)
            high_input(3, lambda k: mod[:, 1, 24 + k, 0:1])
            gated("up_1", "down_1", 1)
            for g in range(4):
                leave("turn_out", g, out_tok[:, g // 2, 512 * (g % 2):512 * (g % 2) + 512])

        @block.vector
        def _(v):
            for b in range(4):
                v.sem_inc(sc_free[b], 1)
            v.sem_inc(s_hid, 2)
            v.sem_inc(xb_free[0], 1)
            v.sem_inc(xb_free[1], 4)

            counted = [0]

            def settle(instruction):
                counted[0] += 1
                instruction.then_inc(s_step, 1)
                v.wait_ge(s_step, counted[0])

            def tt(out, a, b, op):
                return nc.vector.tensor_tensor(out, a, b, op)

            def spread_last(a, n):
                return a.unsqueeze(len(a.shape)).to_broadcast([*a.shape, n])

            def apply_norm(r, root_stage, kt, src, gain, dst, shift=None, width=T, rows=slice(0, P)):
                wait_emptied(v, root_stage, 0)
                settle(nc.vector.reciprocal(rstd[rows, 0, 0:width], std[rows, 0, 0:width]))
                for k in range(kt):
                    last = nc.vector.scalar_tensor_tensor(dst(k), src(k), gain(k), rstd[rows, 0, 0:width],
                                                          ALU.mult, ALU.mult)
                if shift is not None:
                    settle(last)
                    for k in range(kt):
                        last = nc.vector.tensor_scalar(dst(k), dst(k), shift(k), None, ALU.add)
                last.then_inc(s_norm, 1)
                v.wait_ge(s_norm, r + 1)

            def low(stage, s, i=0):
                _, _, b, count = split_of(stage, s)
                v.wait_ge(w_high[b], i + count)
                tt(w_lo[b][:, :], ring[b][:, :], w_hi[b][:, :].bitcast(F32), ALU.subtract)\
                    .then_inc(w_split[b], 1)

            def norm_split(n, stage, gain, shift=None):
                tt(sq[:, :, :], h_lat[:, :, :], h_lat[:, :, :], ALU.mult).then_inc(s_sq, 1)
                for s in range(3):
                    low(RUNS[n][0], s)
                wait_emptied(v, stage, 0)
                settle(nc.vector.reciprocal(rstd[:, 0, 0:T], std[:, 0, 0:T]))
                for k in range(KD + 1):
                    if k < KD:
                        nc.vector.scalar_tensor_tensor(lat(k), h_lat[:, k, :], gain(k), rstd[:, 0, 0:T],
                                                       ALU.mult, ALU.mult).then_inc(s_scaled, 1)
                    if k >= 1:
                        m = k - 1
                        v.wait_ge(s_x_hi, KD * n + m + 1)
                        hi = x_hi[:, m, :].bitcast(F32)
                        if shift is None:
                            last = tt(x_lo[:, m, :], lat(m), hi, ALU.subtract)
                        else:
                            last = nc.vector.scalar_tensor_tensor(x_lo[:, m, :], lat(m), shift(m), hi,
                                                                  ALU.add, ALU.subtract)
                        last.then_inc(s_x_lo, 1)
                v.wait_ge(s_x_lo, KD * (n + 1))
                v.sem_inc(s_norm, 1)

            def mod_norm_split(n, stage, layer, i):
                norm_split(n, stage, lambda k: gmod[:, layer, i, k, 0:1], lambda k: mod[:, layer, 24 * i + k, 0:1])

            def hidden_split(up, dn, n):
                for j, s, i in steps(v, 0, 11, 2):
                    low(up, 2 * s + 3, i)
                    low(up, 2 * s + 4, i)
                    wait_full(v, up, 2 * s + 1, i)
                    wait_emptied(v, up, 2 * s, i)
                    b = bank_of(up, 2 * s + 1)
                    raw = hid_raw[:, s % 2]
                    tt(raw, raw, bank[b][:, :].rearrange("p (a t) -> p a t", a=2), ALU.mult).then_inc(free[b], 1)
                    wait_emptied(v, up, 2 * s + 1, i)
                    hi = some(hid_hi, j * 2, 2)
                    nc.vector.tensor_copy(hi, raw).then_inc(s_hid_hi, 1)
                    v.wait_ge(s_hid_hi, j + (11 * n + 1))
                    tt(some(hid_lo, j * 2, 2), raw, hi.bitcast(F32), ALU.subtract).then_inc(s_hid, 1)
                for j, s, i in steps(v, 3, 8):
                    low(dn, s, i)

            def norm(r, stage, x, gain, dst, shift=None):
                tt(sq[:, :, :], x[:, :, :], x[:, :, :], ALU.mult).then_inc(s_sq, 1)
                apply_norm(r, stage, KD, lambda k: x[:, k, :], gain, dst, shift)

            def lat(k):
                return nrm[:, k, T:2 * T]

            def con(k):
                return nrm[:, k, 0:T]

            def mod_norm(r, stage, layer, i, x, dst, who):
                norm(r, stage, x, lambda k: gmod[:, layer, i, k, who:who + 1], dst,
                     lambda k: mod[:, layer, 24 * i + k, who:who + 1])

            def residual_bank(stage, layer, i, h, who, g):
                wait_full(v, stage, g)
                b = bank_of(stage, g)
                for m in range(2):
                    k = 2 * g + m
                    last = nc.vector.scalar_tensor_tensor(
                        h[:, k, :], bank[b][:, m * T:(m + 1) * T], mod[:, layer, 24 * i + 16 + k, who:who + 1],
                        h[:, k, :], ALU.mult, ALU.add)
                last.then_inc(free[b], 1)

            def residual(stage, layer, i, h, who, n):
                for g in range(4):
                    residual_bank(stage, layer, i, h, who, g)
                wait_all_emptied(v, stage, 4)

            def hidden_pair(up, j, s, i):
                wait_full(v, up, 2 * s + 1, i)
                wait_emptied(v, up, 2 * s, i)
                b = bank_of(up, 2 * s + 1)
                here = some(hid, j * 2, 2)
                tt(here, here, bank[b][:, :].rearrange("p (a t) -> p a t", a=2), ALU.mult).then_inc(free[b], 1)

            def convolve(name, n):
                nc.vector.memset(z[:, :, 0:1], 0.0)
                settle(nc.vector.memset(z[:, :, T + 1:T + 2], 0.0))
                wait_all_emptied(v, f"conv_in_{name}", n)
                settle(tt(z[:, :, 1:T + 1], cproj[:, 8:16, :], cproj[:, 16:24, :], ALU.mult))
                for k in range(KD):
                    last = nc.vector.tensor_scalar(cproj[:, 8 + k, :], z[:, k, 0:T], vcol("conv_k", k),
                                                   vcol("conv_b", k), ALU.mult, ALU.add)
                settle(last)
                for tap in (1, 2):
                    for k in range(KD):
                        last = nc.vector.scalar_tensor_tensor(
                            cproj[:, 8 + k, :], z[:, k, tap:tap + T], vcol("conv_k", 8 * tap + k), cproj[:, 8 + k, :],
                            ALU.mult, ALU.add)
                    settle(last)
                tt(cproj[:, 0:8, :], cproj[:, 0:8, :], cproj[:, 8:16, :], ALU.mult).then_inc(s_conv, 1)

            wait_emptied(v, "vectors", 0)
            wait_all_emptied(v, "turn_x", 4)
            wait_all_emptied(v, "turn_ctx", 4)
            norm_split(0, "norm1", lambda k: vcol("norm1", k))
            for s in range(3, 20):
                low("qkv", s)
            settle(nc.vector.memset(wts[:, :], 0.0))
            nc.vector.tensor_copy(sel[:, :, :], spread_last(row32, P)).then_inc(s_index, 1)

            def modulation(layer):
                v.wait_ge(s_mod, MODS * (layer + 1))
                settle(tt(mod[:, layer], sbank[3][:, 96 * layer:96 * layer + 96].rearrange("p (m s) -> p m s", s=2),
                          spread_last(modb[:, 48 * layer:48 * layer + 48], 2), ALU.add))
                for i, name in enumerate(("mix", "ffn")):
                    a = VROWS[name] + 8 * layer
                    last = nc.vector.scalar_tensor_tensor(gmod[:, layer, i], mod[:, layer, 24 * i + 8:24 * i + 16, :],
                                                          1.0, spread_last(vec[:, a:a + 8], 2), ALU.add, ALU.mult)
                settle(last)

            def front(n):
                b = c = n % 3
                v.wait_ge(sc_full[b], n // 3 + 1)
                scores = sbank[b].rearrange("p (t k) -> p t k", t=2)
                if n < HEADS:
                    slope = 2.0 ** (-8.0 * (n + 1) / HEADS)
                    nc.vector.scalar_tensor_tensor(logit[:, c], dist, -slope, scores, ALU.mult, ALU.add)\
                        .then_inc(sc_free[b], 1)
                    v.wait_ge(sc_free[b], n // 3 + 2)
                    nc.vector.tensor_reduce(small[:, n, 0:2], logit[:, c], AX.X, ALU.max, negate=True)\
                        .then_inc(s_soft_in, 1)
                else:
                    if n - 3 >= HEADS:
                        v.wait_ge(s_prob_s, n - 3 - HEADS + 1)
                    tt(logit[:, c], scores, strict, ALU.add).then_inc(sc_free[b], 1)
                    v.wait_ge(sc_free[b], n // 3 + 2)
                    nc.vector.scalar_tensor_tensor(expo[:, c], logit[:, c], -1.0, logit[:, c], ALU.mult, ALU.min)\
                        .then_inc(s_soft_in, 1)

            def back(n):
                c = n % 3
                v.wait_ge(s_soft_exp, n + 1)
                if n < HEADS:
                    settle(nc.vector.reciprocal(small[:, n, 4:6], small[:, n, 2:4]))
                    tt(prob[:, c], prob[:, c], spread_last(small[:, n, 4:6], T), ALU.mult).then_inc(s_prob_v, 1)
                else:
                    settle(nc.vector.scalar_tensor_tensor(soft[:, c], logit[:, c], 0.0, soft[:, c], ALU.max, ALU.add))
                    for t in range(2):
                        last = nc.vector.tensor_tensor_scan(expo[:, c, t, ::-1], ones, soft[:, c, t, ::-1], 0.0,
                                                            ALU.mult, ALU.add)
                    settle(last)
                    tt(logit[:, c], logit[:, c], expo[:, c], ALU.subtract).then_inc(s_arg, 1)

            for s in range(HALVES + 1):
                if s < HALVES:
                    front(s)
                if s >= 1:
                    back(s - 1)

            wait_all_emptied(v, "gates", 8)
            for n, stage in enumerate(("out_moba", "out_sb")):
                for g in range(4):
                    wait_full(v, stage, g)
                    b = bank_of(stage, g)
                    here = gate[:, 8 * n + 2 * g:8 * n + 2 * g + 2, :]
                    tt(here, here, bank[b][:, :].rearrange("p (a t) -> p a t", a=2), ALU.mult).then_inc(free[b], 1)
                wait_all_emptied(v, stage, 4)
            tt(gate[:, 0:8, :], gate[:, 0:8, :], gate[:, 8:16, :], ALU.add).then_inc(s_mixed, 1)
            for g in range(4):
                wait_full(v, "mix", g)
                b = bank_of("mix", g)
                here = h_lat[:, 2 * g:2 * g + 2, :]
                tt(here, here, bank[b][:, :].rearrange("p (a t) -> p a t", a=2), ALU.add).then_inc(free[b], 1)
            wait_all_emptied(v, "mix", 4)
            norm(1, "norm2", h_lat, lambda k: vcol("norm2", k), lat)
            modulation(0)
            mod_norm(2, "mixnorm_ctx", 0, 0, h_ctx, con, 1)

            def sixteen(rows, best_of, index_of, count):
                for a in range(0, count, 4):
                    four = range(a, a + 4)
                    for n in four:
                        last = nc.vector.max(best_of(n)[:, 0:8], rows(n))
                    settle(last)
                    for n in four:
                        nc.vector.max_index(index_of(n)[:, 0:8], best_of(n)[:, 0:8], rows(n))
                        last = nc.vector.match_replace(rows(n), best_of(n)[:, 0:8], rows(n), -3.4e38)
                    settle(last)
                    for n in four:
                        last = nc.vector.max(best_of(n)[:, 8:16], rows(n))
                    settle(last)
                    for n in four:
                        last = nc.vector.max_index(index_of(n)[:, 8:16], best_of(n)[:, 8:16], rows(n))
                settle(last)

            wait_all_emptied(v, "turn_x2", 4)
            nc.vector.tensor_copy(split[0], x2_tok).then_inc(s_split, 1)
            v.wait_ge(s_split, 1)
            settle(tt(rest, x2_tok, split[0], ALU.subtract))
            nc.vector.tensor_copy(split[1], rest).then_inc(s_split, 1)
            v.wait_ge(s_split, 2)
            settle(tt(rest, rest, split[1], ALU.subtract))
            nc.vector.tensor_copy(split[2], rest).then_inc(s_split, 1)

            for t in range(2):
                sixteen(lambda n: score[:, t, n, :], lambda n: top[:, t, n, :], lambda n: top_i[:, t, n, :], 16)
                nc.vector.tensor_copy(top_f[:, t], top_i[:, t])
                pair = top[:, t].rearrange("p (h b) k -> p h b k", b=2)
                settle(tt(cand.rearrange("p h (i j) -> p h i j", i=TOPK),
                          pair[:, :, 0, :].unsqueeze(3).to_broadcast([P, PH, TOPK, TOPK]),
                          pair[:, :, 1, :].unsqueeze(2).to_broadcast([P, PH, TOPK, TOPK]), ALU.add))
                pos_h = pos.rearrange("p (h k) -> p h k", h=PH)
                sixteen(lambda n: cand[:, n, :], lambda n: best[:, t, n, :], lambda n: pos_h[:, n, :], PH)
                nc.vector.tensor_scalar(part[:, 0], pos, 4, None, ALU.logical_shift_right)
                settle(nc.vector.tensor_scalar(part[:, 1], pos, 15, None, ALU.bitwise_and))
                settle(nc.vector.tensor_copy(part_f, part))
                index = top_f[:, t].rearrange("p (h b) k -> p h b k", b=2)
                for b in range(2):
                    settle(tt(eq, spread_last(part_f[:, b], TOPK),
                              iota.unsqueeze(1).to_broadcast([P, P, TOPK]), ALU.is_equal))
                    eq_h = eq.rearrange("p (h k) m -> p h k m", h=PH)
                    settle(tt(eq_h, eq_h, index[:, :, b, :].unsqueeze(2).to_broadcast([P, PH, TOPK, TOPK]), ALU.mult))
                    settle(nc.vector.tensor_reduce(pick[:, b], eq, AX.X, ALU.add))
                nc.vector.scalar_tensor_tensor(chosen[:, t], pick[:, 0], float(KEYS), pick[:, 1], ALU.mult, ALU.add)
                last = tt(shifted[:, t], best[:, t], best[:, t, :, 0:1].to_broadcast([P, PH, TOPK]), ALU.subtract)
                settle(last)
            v.sem_inc(s_shift, 1)
            v.wait_ge(s_pexp, 1)
            settle(nc.vector.tensor_reduce(sums[:, 0], shifted, AX.X, ALU.add))
            settle(nc.vector.reciprocal(sums[:, 1], sums[:, 0]))
            last = None
            for t in range(2):
                last = tt(shifted[:, t], shifted[:, t], spread_last(sums[:, 1, t], TOPK), ALU.mult)
            last.then_inc(s_chosen, 1)

            wait_full(v, "turn_chosen", 0)
            b = bank_of("turn_chosen", 0)
            nc.vector.tensor_copy(idx_t[:, :], bank[b][:, 0:T]).then_inc(s_index, 1)
            v.wait_ge(s_index, 2)
            nc.vector.tensor_copy(gate_t[:, :], bank[b][:, T:2 * T]).then_inc(s_index, 1)
            v.wait_ge(s_index, 3)
            v.sem_inc(free[b], 1)
            modulation(1)

            def gather(it, i, half, kind, first):
                def products(quad):
                    for s in range(4 * quad, 4 * quad + 4):
                        v.wait_ge(u_landed[s % 4], (it * 4 + quad + 1) * 16)
                        for c in range(2):
                            v.wait_ge(xb_full[c], it * 16 + s + 1)
                            u = ubuf[s % 4][:, 512 * c:512 * c + 512]
                            nc.vector.tensor_tensor_reduce(u, u, sbank[c], 1.0, 0.0, ALU.mult, ALU.add,
                                                           halves[:, c, s:s + 1]).then_inc(xb_free[c], 1)
                    v.wait_ge(xb_free[1], it * 16 + 4 * quad + 8)
                    four = slice(4 * quad, 4 * quad + 4)
                    tt(dots[:, four], halves[:, 0, four], halves[:, 1, four], ALU.add).then_inc(s_dots, 1)

                def weigh(quad):
                    v.wait_ge(s_gelu, it * 4 + quad + 1)
                    tt(wts[:, 68 * quad:68 * quad + 52:17], gelus[:, 4 * quad:4 * quad + 4],
                       some(gate_t, it * 16 + 4 * quad, 4), ALU.mult).then_inc(s_wts, 1)

                def extra(k):
                    s = first + k
                    if kind == "conv" and k == 3:
                        convolve("ctx", 8)
                    if kind == "conv_out":
                        residual_bank("conv_out_ctx", 0, 0, h_ctx, 1, k)
                    if kind == "norm":
                        if k == 0:
                            apply_norm(3, "ffnnorm_ctx", KD, lambda n: h_ctx[:, n, :],
                                       lambda n: gmod[:, 0, 1, n, 1:2], con, lambda n: mod[:, 0, 24 + n, 1:2])
                    if kind == "up" and s < 22 and k % 2 == 1:
                        hidden_pair("up_ctx", i * 2 + s // 2, s // 2, i)

                if kind == "norm":
                    wait_all_emptied(v, "conv_out_ctx", 4)
                    tt(sq[:, :, :], h_ctx[:, :, :], h_ctx[:, :, :], ALU.mult).then_inc(s_sq, 1)
                products(0)
                weigh(0)
                extra(0)
                products(1)
                weigh(1)
                extra(1)
                products(2)
                weigh(2)
                products(3)
                weigh(3)
                extra(2)
                extra(3)

            for it, i, half, kind, first in turns_of(v):
                gather(it, i, half, kind, first)
            residual("down_ctx", 0, 1, h_ctx, 1, 1)
            v.wait_ge(vo_free, 17)
            settle(tt(h_lat[:, :, :], h_lat[:, :, :], peer, ALU.add))
            norm(4, "norm_final", h_lat, lambda k: vcol("final", k), lambda k: h_lat[:, k, :])

            mod_norm_split(1, "mixnorm_lat", 0, 0)
            for j, s, i in steps(v, 0, 8):
                low("conv_in_lat", s + 3, i)
            low("conv_in_lat", 11)
            tt(sq[:, :, :], h_ctx[:, :, :], h_ctx[:, :, :], ALU.mult).then_inc(s_sq, 1)
            convolve("lat", 12)
            apply_norm(6, "mixnorm1_ctx", KD, lambda k: h_ctx[:, k, :], lambda k: gmod[:, 1, 0, k, 1:2], con,
                       lambda k: mod[:, 1, k, 1:2])
            residual("conv_out_lat", 0, 0, h_lat, 0, 2)
            mod_norm_split(2, "ffnnorm_lat", 0, 1)
            hidden_split("up_lat", "down_lat", 0)
            residual("down_lat", 0, 1, h_lat, 0, 3)

            mod_norm(8, "mixnorm1_lat", 1, 0, h_lat, lat, 0)
            wait_all_emptied(v, "mla_in", 6)
            tt(sq[:, 0:6, :], qlat, qlat, ALU.mult).then_inc(s_sq, 1)
            apply_norm(9, "qlat_norm", 6, lambda k: qlat[:, k, :], lambda k: vcol("q_lat", k), lambda k: qlat[:, k, :])

            def square_wide(n, rows):
                return sq[rows, 2 * n:2 * n + 2, :].rearrange("p a t -> p (a t)")

            every = slice(0, P)
            for k in range(2):
                last = tt(square_wide(k, every), kvlat[:, k, :], kvlat[:, k, :], ALU.mult)
            last.then_inc(s_sq, 1)
            apply_norm(10, "kvlat_norm", 2, lambda k: kvlat[:, k, :], lambda k: vcol("kv_lat", k),
                       lambda k: kvlat[:, k, :], width=2 * T)
            rope = slice(NOPE, QH)
            tt(square_wide(0, rope), kpe[rope, :], kpe[rope, :], ALU.mult).then_inc(s_sq, 1)
            apply_norm(11, "kpe_norm", 1, lambda k: kpe[rope, :], lambda k: vcol("kn", 0)[rope, :],
                       lambda k: kpe[rope, :], width=2 * T, rows=rope)
            wait_full(v, "kpe_turn", 0)
            b = bank_of("kpe_turn", 0)
            nc.vector.tensor_tensor(std[rope, 0, 0:T], bank[b][rope, 0:T], sin[rope, :], ALU.mult).then_inc(free[b], 1)
            settle(tt(kpe[rope, T:2 * T], kpe[rope, T:2 * T], cos[rope, :], ALU.mult))
            tt(kpe[rope, T:2 * T], kpe[rope, T:2 * T], std[rope, 0, 0:T], ALU.add).then_inc(s_kpe, 1)
            v.wait_ge(s_kpe, 1)

            def head_norm(m, mean_at, x, rows, gain, done):
                wait_emptied(v, "heads", HEAD.index(mean_at))
                settle(nc.vector.reciprocal(rstd[rows, m % 2, :], std[rows, m % 2, :]))
                nc.vector.scalar_tensor_tensor(x, x, gain[rows], rstd[rows, m % 2, :], ALU.mult, ALU.mult)\
                    .then_inc(done, 1)

            for n in range(MH):
                head_norm(n, ("key_mean", n), kcat[0:NOPE, n, :], slice(0, NOPE), vcol("kn", 0), s_kn)
            for s in range(9):
                if s < 8:
                    head_norm(MH + s, ("query_mean", s), q[0:QH, 2 * s:2 * s + 2, :].rearrange("p a t -> p (a t)"),
                              slice(0, QH), vcol("qn", 0), s_qn)
                if s >= 1:
                    n = s - 1
                    g = HEAD.index(("query_turn", n))
                    wait_full(v, "heads", g)
                    b = bank_of("heads", g)
                    pair = q[0:QH, 2 * n:2 * n + 2, :]
                    turned = sq[0:QH, 2 * (n % 4):2 * (n % 4) + 2, :]
                    tt(turned, bank[b][0:QH, :].rearrange("p (a t) -> p a t", a=2),
                       sin[0:QH, :].unsqueeze(1).to_broadcast([QH, 2, T]), ALU.mult).then_inc(free[b], 1)
                    settle(tt(pair, pair, cos[0:QH, :].unsqueeze(1).to_broadcast([QH, 2, T]), ALU.mult))
                    tt(pair, pair, turned, ALU.add).then_inc(s_qr, 1)
            for s in range(MH + 1):
                if s < MH:
                    for t in range(2):
                        n = 2 * s + t
                        v.wait_ge(sc_full[n % 4], SCORED[n % 4] + n // 4 + 1)
                        last = nc.vector.tensor_reduce(msmall[:, s, 4 + t:5 + t], sbank[n % 4], AX.X, ALU.max, negate=True)
                    settle(last)
                    nc.vector.tensor_scalar(msmall[:, s, 0:2], msmall[:, s, 4:6], QH ** -0.5, None, ALU.mult)\
                        .then_inc(s_soft_in, 1)
                if s >= 1:
                    m = s - 1
                    for t in range(2):
                        n = 2 * m + t
                        v.wait_ge(sc_free[n % 4], SCORED[n % 4] + n // 4 + 2)
                    settle(nc.vector.reciprocal(msmall[:, m, 6:8], msmall[:, m, 2:4]))
                    for t in range(2):
                        last = nc.vector.tensor_scalar(mprob[:, m % 2, t, :], mprob[:, m % 2, t, :],
                                                       msmall[:, m, 6 + t:7 + t], None, ALU.mult)
                    last.then_inc(s_prob_v, 1)
            residual("mla_out", 1, 0, h_lat, 0, 4)
            mod_norm_split(3, "ffnnorm1", 1, 1)
            hidden_split("up_1", "down_1", 1)
            residual("down_1", 1, 1, h_lat, 0, 5)


_INS = ["x", "norm1_g", "w_in", "w_out_moba", "w_out_sb", "w_mix_out", "norm2_g", "peer_w_q", "peer_sub_keys",
        "peer_u", "peer_v", "final_norm_g", "c_2", "ctx_2", "c_ctx_2", "norm_mix_g_2", "norm_ffn_g_2", "mod_w_2",
        "mod_b_2", "ffn_w_gate_2", "ffn_w_up_2", "ffn_w_down_2", "conv_w_in_2", "conv_k_2", "conv_b_2",
        "conv_w_out_2", "mla_w_in_2", "mla_q_norm_g_2", "mla_w_q_up_2", "mla_kv_norm_g_2", "mla_w_kv_up_2",
        "mla_qn_nope_g_2", "mla_qn_rope_g_2", "mla_kn_nope_g_2", "mla_kn_rope_g_2", "mla_w_out_2"]


def kernel(**inputs):
    import concourse.bacc as bacc
    from concourse.bass_utils import run_bass_kernel_spmd

    nc = bacc.Bacc("TRN2", target_bir_lowering=False, num_devices=1)
    arrays, w = {}, {}
    for name in _INS:
        a = np.ascontiguousarray(inputs[name])
        arrays[f"in_{name}_dram"] = a
        w[name] = nc.dram_tensor(f"in_{name}_dram", a.shape, mybir.dt.from_np(a.dtype), kind="ExternalInput").ap()
    arrays["in_consts_dram"] = constants()
    consts = nc.dram_tensor("in_consts_dram", arrays["in_consts_dram"].shape, F32, kind="ExternalInput").ap()
    out = nc.dram_tensor("out_0_dram", (1, T, D), F32, kind="ExternalOutput").ap()
    program(nc, w, consts, out)
    r = run_bass_kernel_spmd(nc, [arrays], core_ids=[0])
    return r.results[0]["out_0_dram"]
```
